# Optimizing a Trainium2 kernel written in Bass

```python
import jax
import jax.numpy as jnp
from jax import lax
import numpy as np
import jax, jax.numpy as jnp

D_MODEL = 1024
BATCH = 1
SEQ = 256
DEPTH = 1

N_BRANCH = 4
BRANCH_WIDTH = 512
RWKV_HEADS = 8
RWKV_HEAD_DIM = BRANCH_WIDTH // RWKV_HEADS
RWKV_DECAY_RANK = 64
RWKV_ICL_RANK = 64
RWKV_VALUE_RANK = 32
RWKV_GATE_RANK = 128
RWKV_LNX_EPS = 64e-5
HGRN_HEADS = 4
HGRN_HEAD_DIM = BRANCH_WIDTH // HGRN_HEADS
MLSTM_HEADS = 4
MLSTM_HEAD_DIM = BRANCH_WIDTH // MLSTM_HEADS
CHUNK = 64
LRU_BLOCKS = 8
LRU_BLOCK_DIM = BRANCH_WIDTH // LRU_BLOCKS
LRU_C = 8.0
CONV_WIDTH = 4
N_EXPERTS = 32
TOP_K = 4
D_EXPERT = 1024
SWIGLU_LIMIT = 7.0
SWIGLU_ALPHA = 1.702
EXPERT_BLOCK = 128
D_PLE = 256
LN_EPS = 1e-5
NORM_EPS = 1e-6
DEEPNORM_ALPHA = (2 * DEPTH) ** 0.25
DEEPNORM_BETA = (8 * DEPTH) ** -0.25

RWKV_SPLITS = (BRANCH_WIDTH, BRANCH_WIDTH, BRANCH_WIDTH, RWKV_DECAY_RANK, RWKV_ICL_RANK, RWKV_GATE_RANK)
RWKV_COLS = 3 * BRANCH_WIDTH + RWKV_DECAY_RANK + RWKV_ICL_RANK + RWKV_GATE_RANK
HGRN_COLS = 4 * BRANCH_WIDTH
MLSTM_SPLITS = (BRANCH_WIDTH, BRANCH_WIDTH, BRANCH_WIDTH, BRANCH_WIDTH, MLSTM_HEADS, MLSTM_HEADS)
MLSTM_COLS = 4 * BRANCH_WIDTH + 2 * MLSTM_HEADS
LRU_COLS = 2 * BRANCH_WIDTH
GATE_COLS = N_BRANCH * D_MODEL
N_COLS_BASE = RWKV_COLS + HGRN_COLS + MLSTM_COLS + LRU_COLS + GATE_COLS
N_COLS_REST = N_COLS_BASE + RWKV_VALUE_RANK

F32 = jnp.float32


def _split(z, sizes):
    return jnp.split(z, np.cumsum(sizes)[:-1].tolist(), axis=-1)

def _layernorm(x, g, b, dtype):
    xf = x.astype(F32)
    xc = xf - jnp.mean(xf, -1, keepdims=True)
    var = jnp.mean(xc * xc, -1, keepdims=True)
    return (xc * lax.rsqrt(var + LN_EPS) * g + b).astype(dtype)

def _head_layernorm(y, eps):
    yc = y - jnp.mean(y, -1, keepdims=True)
    out = yc * lax.rsqrt(jnp.mean(yc * yc, -1, keepdims=True) + eps)
    return out.reshape(out.shape[:-2] + (-1,))

def _head_rmsnorm(y, eps):
    out = y * lax.rsqrt(jnp.mean(y * y, -1, keepdims=True) + eps)
    return out.reshape(out.shape[:-2] + (-1,))

def _token_shift(z):
    return jnp.pad(z, ((0, 0), (1, 0), (0, 0)))[:, :-1]

def _causal_conv(z, w, b):
    seq = z.shape[1]
    zp = jnp.pad(z, ((0, 0), (CONV_WIDTH - 1, 0), (0, 0)))
    out = b
    for j in range(CONV_WIDTH):
        out = out + zp[:, j:j + seq] * w[j]
    return out

def _to_heads(t, n_heads):
    bsz, seq, width = t.shape
    return t.reshape(bsz, seq, n_heads, width // n_heads).transpose(0, 2, 1, 3)

def _from_heads(t):
    return t.transpose(0, 2, 1, 3)

def _to_chunks(t):
    bsz, nh, seq = t.shape[:3]
    t = t.reshape((bsz, nh, seq // CHUNK, CHUNK) + t.shape[3:])
    return jnp.moveaxis(t, 2, 0)

def _from_chunks(t):
    nc, bsz, nh, c, dv = t.shape
    return jnp.moveaxis(t, 0, 2).reshape(bsz, nh, nc * c, dv)

def rwkv7_mix(zA, v_first, v_mix, mu, w0, w2, a0, a2, g2, k_k, k_a, r_k, lnx_g, lnx_b):
    bsz, seq = zA.shape[:2]
    zA = zA + (_token_shift(zA) - zA) * mu
    r, k, v, xw, xa, xg = _split(zA, RWKV_SPLITS)
    w_log = -jax.nn.softplus(-(w0 + jnp.tanh(xw) @ w2)) - 0.5
    decay = jnp.exp(-jnp.exp(w_log))
    a = jax.nn.sigmoid(a0 + xa @ a2)
    g = jax.nn.sigmoid(xg) @ g2
    if v_mix is not None:
        v = v + (v_first - v) * jax.nn.sigmoid(v_mix)

    def hs(t):
        return t.reshape(bsz, seq, RWKV_HEADS, RWKV_HEAD_DIM)

    kk = hs(k * k_k)
    kk = kk / jnp.maximum(jnp.sqrt(jnp.sum(kk * kk, -1, keepdims=True)), 1e-12)
    k = k * (1.0 + (a - 1.0) * k_a)
    rh, kh, vh, dh, ah = hs(r), hs(k), hs(v), hs(decay), hs(a)
    neg_kk = -kk
    kk_a = kk * ah

    def step(state, inp):
        r_t, w_t, k_t, v_t, a_t, b_t = inp
        sa = jnp.einsum('bhvk,bhk->bhv', state, a_t)
        state = state * w_t[:, :, None, :] + sa[..., None] * b_t[:, :, None, :] + v_t[..., None] * k_t[:, :, None, :]
        return state, jnp.einsum('bhvk,bhk->bhv', state, r_t)

    xs = tuple(jnp.moveaxis(t, 1, 0) for t in (rh, dh, kh, vh, neg_kk, kk_a))
    state0 = jnp.zeros((bsz, RWKV_HEADS, RWKV_HEAD_DIM, RWKV_HEAD_DIM), F32)
    _, y = lax.scan(step, state0, xs)
    y = jnp.moveaxis(y, 0, 1)
    y = _head_layernorm(y, RWKV_LNX_EPS) * lnx_g + lnx_b
    bonus = (jnp.sum(rh * kh * r_k, -1, keepdims=True) * vh).reshape(bsz, seq, BRANCH_WIDTH)
    return (y + bonus) * g, v

def _gla_chunked(q, k, v, log_f):
    bsz, nh, _, dk = q.shape
    dv = v.shape[-1]
    causal = jnp.tril(jnp.ones((CHUNK, CHUNK), bool))

    def chunk(state, inp):
        qc, kc, vc, lf = inp
        bcum = jnp.cumsum(lf, axis=-2)
        o_inter = jnp.einsum('bhtd,bhde->bhte', qc * jnp.exp(bcum), state)
        diff = bcum[:, :, :, None, :] - bcum[:, :, None, :, :]
        pair_decay = jnp.exp(jnp.where(causal[:, :, None], diff, -jnp.inf))
        attn = jnp.einsum('bhtd,bhsd,bhtsd->bhts', qc, kc, pair_decay)
        o = o_inter + jnp.einsum('bhts,bhse->bhte', attn, vc)
        b_last = bcum[:, :, -1]
        state = jnp.exp(b_last)[..., None] * state + jnp.einsum('bhsd,bhse->bhde', kc * jnp.exp(b_last[:, :, None] - bcum), vc)
        return state, o

    state0 = jnp.zeros((bsz, nh, dk, dv), F32)
    _, o = lax.scan(chunk, state0, tuple(_to_chunks(t) for t in (q, k, v, log_f)))
    return _from_chunks(o)

def hgrn2_mix(zB, lb, norm_w):
    q, f, i, g = _split(zB, (BRANCH_WIDTH,) * 4)
    q = jax.nn.silu(q)
    log_f = jnp.logaddexp(jnp.log(lb), jnp.log1p(-lb) + jax.nn.log_sigmoid(f))
    k = (1.0 - lb) * jax.nn.sigmoid(-f)
    o = _gla_chunked(*(_to_heads(t, HGRN_HEADS) for t in (q, k, i, log_f)))
    o = _head_rmsnorm(_from_heads(o), NORM_EPS) * norm_w
    return o * jax.nn.silu(g)

def _mlstm_chunked(q, k, v, i_pre, log_f):
    bsz, nh, _, dk = q.shape
    dv = v.shape[-1]
    causal = jnp.tril(jnp.ones((CHUNK, CHUNK), bool))

    def chunk(carry, inp):
        c_mat, n_vec, m_prev = carry
        qc, kc, vc, ic, lf = inp
        fcum = jnp.cumsum(lf, axis=-1)
        log_w = jnp.where(causal, fcum[..., :, None] - fcum[..., None, :] + ic[..., None, :], -jnp.inf)
        log_inter = fcum + m_prev[..., None]
        m_t = jnp.maximum(log_inter, jnp.max(log_w, -1))
        w_intra = jnp.exp(log_w - m_t[..., None])
        w_inter = jnp.exp(log_inter - m_t)
        s_qk = jnp.einsum('bhtd,bhsd->bhts', qc, kc) * w_intra
        num = w_inter[..., None] * jnp.einsum('bhtd,bhde->bhte', qc, c_mat) + jnp.einsum('bhts,bhse->bhte', s_qk, vc)
        den = w_inter * jnp.einsum('bhtd,bhd->bht', qc, n_vec) + jnp.sum(s_qk, -1)
        h = num / jnp.maximum(jnp.abs(den), jnp.exp(-m_t))[..., None]
        f_last = fcum[..., -1]
        log_s = f_last[..., None] - fcum + ic
        m_new = jnp.maximum(f_last + m_prev, jnp.max(log_s, -1))
        ws = jnp.exp(log_s - m_new[..., None])
        carry_decay = jnp.exp(f_last + m_prev - m_new)
        c_mat = carry_decay[..., None, None] * c_mat + jnp.einsum('bhs,bhsd,bhse->bhde', ws, kc, vc)
        n_vec = carry_decay[..., None] * n_vec + jnp.einsum('bhs,bhsd->bhd', ws, kc)
        return (c_mat, n_vec, m_new), h

    carry0 = (jnp.zeros((bsz, nh, dk, dv), F32), jnp.zeros((bsz, nh, dk), F32), jnp.full((bsz, nh), -1e30, F32))
    _, h = lax.scan(chunk, carry0, tuple(_to_chunks(t) for t in (q, k, v, i_pre, log_f)))
    return _from_chunks(h)

def mlstm_mix(zC, conv_w, conv_b, i_bias, f_bias, norm_w):
    q, k, v, o, ig, fg = _split(zC, MLSTM_SPLITS)
    qk = jax.nn.silu(_causal_conv(jnp.concatenate([q, k], -1), conv_w, conv_b))
    q, k = _split(qk, (BRANCH_WIDTH, BRANCH_WIDTH))
    qh = _to_heads(q, MLSTM_HEADS)
    kh = _to_heads(k, MLSTM_HEADS) * MLSTM_HEAD_DIM ** -0.5
    vh = _to_heads(v, MLSTM_HEADS)
    i_pre = (ig + i_bias).transpose(0, 2, 1)
    log_f = jax.nn.log_sigmoid(fg + f_bias).transpose(0, 2, 1)
    h = _mlstm_chunked(qh, kh, vh, i_pre, log_f)
    h = _head_layernorm(_from_heads(h), NORM_EPS) * norm_w
    return jax.nn.sigmoid(o) * h

def _linear_combine(left, right):
    a_l, b_l = left
    a_r, b_r = right
    return a_l * a_r, a_r * b_l + b_r

def rglru_mix(zD, conv_w, conv_b, wx, bx, wa, ba, lam):
    xr, gate = _split(zD, (BRANCH_WIDTH, BRANCH_WIDTH))
    xc = _causal_conv(xr, conv_w, conv_b)
    bsz, seq = xc.shape[:2]
    xb = xc.reshape(bsz, seq, LRU_BLOCKS, LRU_BLOCK_DIM)
    gate_x = jax.nn.sigmoid(jnp.einsum('bsgi,gij->bsgj', xb, wx) + bx).reshape(bsz, seq, BRANCH_WIDTH)
    gate_a = jax.nn.sigmoid(jnp.einsum('bsgi,gij->bsgj', xb, wa) + ba).reshape(bsz, seq, BRANCH_WIDTH)
    log_a = LRU_C * gate_a * jax.nn.log_sigmoid(lam)
    mult = jnp.sqrt(-jnp.expm1(2.0 * log_a)).at[:, 0].set(1.0)
    _, h = lax.associative_scan(_linear_combine, (jnp.exp(log_a), mult * gate_x * xc), axis=1)
    return h * jax.nn.gelu(gate)

def _expert_ffn(xb, w_gu, b_gu, w_down, b_down):
    gu = xb @ w_gu + b_gu
    gate, up = gu[:, :D_EXPERT], gu[:, D_EXPERT:]
    gate = jnp.minimum(gate, SWIGLU_LIMIT)
    up = jnp.clip(up, -SWIGLU_LIMIT, SWIGLU_LIMIT)
    glu = gate * jax.nn.sigmoid(SWIGLU_ALPHA * gate)
    return ((up + 1.0) * glu) @ w_down + b_down

def moe(xf, router_w, router_b, w_gu, b_gu, w_down, b_down):
    n_tok = xf.shape[0]
    logits = (xf @ router_w + router_b).astype(F32)
    top_val, top_idx = lax.top_k(logits, TOP_K)
    gate = jax.nn.softmax(top_val, axis=-1)
    n_assign = n_tok * TOP_K
    n_blocks = -(-n_assign // EXPERT_BLOCK) + N_EXPERTS
    n_slots = n_blocks * EXPERT_BLOCK
    e_flat = top_idx.reshape(-1)
    order = jnp.argsort(e_flat)
    e_sorted = e_flat[order]
    counts = jnp.bincount(e_flat, length=N_EXPERTS)
    padded = (counts + EXPERT_BLOCK - 1) // EXPERT_BLOCK * EXPERT_BLOCK
    start = jnp.cumsum(counts) - counts
    pad_end = jnp.cumsum(padded)
    pad_start = pad_end - padded
    dest = pad_start[e_sorted] + jnp.arange(n_assign) - start[e_sorted]
    slot_tok = jnp.zeros((n_slots,), jnp.int32).at[dest].set((order // TOP_K).astype(jnp.int32))
    slot_w = jnp.zeros((n_slots,), F32).at[dest].set(gate.reshape(-1)[order])
    block_e = jnp.minimum(jnp.searchsorted(pad_end, jnp.arange(n_blocks) * EXPERT_BLOCK, side='right'), N_EXPERTS - 1)
    xs = xf[slot_tok].reshape(n_blocks, EXPERT_BLOCK, -1)

    def run_block(args):
        xb, e = args
        return _expert_ffn(xb, w_gu[e], b_gu[e], w_down[e], b_down[e])

    ys = lax.map(run_block, (xs, block_e)).reshape(n_slots, -1)
    return jnp.zeros(xf.shape, F32).at[slot_tok].add(ys.astype(F32) * slot_w[:, None])

def first_inputs(seed: int = 0) -> dict:
    key = jax.random.key(seed)
    ks = iter(jax.random.split(key, 64))
    L, W, D = DEPTH, BRANCH_WIDTH, D_MODEL

    def nrm(shape, scale):
        return scale * jax.random.normal(next(ks), shape, F32)

    def uni(shape, lo, hi):
        return jax.random.uniform(next(ks), shape, F32, lo, hi)

    return {
        'x': nrm((BATCH, SEQ, D), 1.0),
        'p': nrm((L, BATCH, SEQ, D_PLE), 1.0),
        'w_in_first': nrm((D, N_COLS_BASE), D ** -0.5),
        'w_in_rest': nrm((L - 1, D, N_COLS_REST), D ** -0.5),
        'rwkv_mu': uni((L, RWKV_COLS), 0.0, 1.0),
        'rwkv_w0': uni((L, W), -6.0, 0.0),
        'rwkv_w2': nrm((L, RWKV_DECAY_RANK, W), 0.5 * RWKV_DECAY_RANK ** -0.5),
        'rwkv_a0': nrm((L, W), 0.1),
        'rwkv_a2': nrm((L, RWKV_ICL_RANK, W), 0.5 * RWKV_ICL_RANK ** -0.5),
        'rwkv_v0': nrm((L - 1, W), 0.1),
        'rwkv_v2': nrm((L - 1, RWKV_VALUE_RANK, W), 0.5 * RWKV_VALUE_RANK ** -0.5),
        'rwkv_g2': nrm((L, RWKV_GATE_RANK, W), RWKV_GATE_RANK ** -0.5),
        'rwkv_k_k': 0.85 + nrm((L, W), 0.05),
        'rwkv_k_a': 1.0 + nrm((L, W), 0.05),
        'rwkv_r_k': nrm((L, RWKV_HEADS, RWKV_HEAD_DIM), 0.1),
        'rwkv_lnx_g': 1.0 + nrm((L, W), 0.05),
        'rwkv_lnx_b': nrm((L, W), 0.02),
        'hgrn_lower_bounds': nrm((L, W), 1.0),
        'hgrn_norm_w': 1.0 + nrm((L, W), 0.05),
        'mlstm_conv_w': nrm((L, CONV_WIDTH, 2 * W), CONV_WIDTH ** -0.5),
        'mlstm_conv_b': nrm((L, 2 * W), 0.02),
        'mlstm_i_bias': nrm((L, MLSTM_HEADS), 0.1),
        'mlstm_f_bias': jnp.linspace(3.0, 6.0, MLSTM_HEADS, dtype=F32) + nrm((L, MLSTM_HEADS), 0.1),
        'mlstm_norm_w': 1.0 + nrm((L, W), 0.05),
        'lru_conv_w': nrm((L, CONV_WIDTH, W), CONV_WIDTH ** -0.5),
        'lru_conv_b': nrm((L, W), 0.02),
        'lru_wx': nrm((L, LRU_BLOCKS, LRU_BLOCK_DIM, LRU_BLOCK_DIM), LRU_BLOCK_DIM ** -0.5),
        'lru_bx': nrm((L, LRU_BLOCKS, LRU_BLOCK_DIM), 0.02),
        'lru_wa': nrm((L, LRU_BLOCKS, LRU_BLOCK_DIM, LRU_BLOCK_DIM), LRU_BLOCK_DIM ** -0.5),
        'lru_ba': nrm((L, LRU_BLOCKS, LRU_BLOCK_DIM), 0.02),
        'lru_lambda': uni((L, W), 3.5, 9.0),
        'w_branch': nrm((L, N_BRANCH, W, D), W ** -0.5),
        'w_out': nrm((L, D, D), DEEPNORM_BETA * D ** -0.5),
        'ln1_g': 1.0 + nrm((L, D), 0.05),
        'ln1_b': nrm((L, D), 0.02),
        'router_w': nrm((L, D, N_EXPERTS), D ** -0.5),
        'router_b': nrm((L, N_EXPERTS), 0.01),
        'expert_w_gu': nrm((L, N_EXPERTS, D, 2 * D_EXPERT), D ** -0.5),
        'expert_b_gu': nrm((L, N_EXPERTS, 2 * D_EXPERT), 0.02),
        'expert_w_down': nrm((L, N_EXPERTS, D_EXPERT, D), DEEPNORM_BETA * D_EXPERT ** -0.5),
        'expert_b_down': nrm((L, N_EXPERTS, D), 0.02),
        'ple_gate_w': nrm((L, D, D), D ** -0.5),
        'ple_proj_w': nrm((L, D_PLE, D), DEEPNORM_BETA * D_PLE ** -0.5),
        'ln2_g': 1.0 + nrm((L, D), 0.05),
        'ln2_b': nrm((L, D), 0.02),
    }

def first_block(x, p, w_in_first, w_in_rest, rwkv_mu, rwkv_w0, rwkv_w2, rwkv_a0, rwkv_a2, rwkv_v0, rwkv_v2,
              rwkv_g2, rwkv_k_k, rwkv_k_a, rwkv_r_k, rwkv_lnx_g, rwkv_lnx_b, hgrn_lower_bounds, hgrn_norm_w,
              mlstm_conv_w, mlstm_conv_b, mlstm_i_bias, mlstm_f_bias, mlstm_norm_w, lru_conv_w, lru_conv_b,
              lru_wx, lru_bx, lru_wa, lru_ba, lru_lambda, w_branch, w_out, ln1_g, ln1_b, router_w, router_b,
              expert_w_gu, expert_b_gu, expert_w_down, expert_b_down, ple_gate_w, ple_proj_w, ln2_g, ln2_b):
    dt = x.dtype
    bsz, seq, _ = x.shape
    lb_all = jnp.cumsum(jax.nn.softmax(hgrn_lower_bounds.astype(F32), axis=0), axis=0)
    lb_all = lb_all - lb_all[0]
    v_first = None
    for layer in range(DEPTH):
        w_in = w_in_first if layer == 0 else w_in_rest[layer - 1]
        z = (x @ w_in).astype(F32)
        zA, zB, zC, zD, zG = _split(z[..., :N_COLS_BASE], (RWKV_COLS, HGRN_COLS, MLSTM_COLS, LRU_COLS, GATE_COLS))
        v_mix = None if layer == 0 else rwkv_v0[layer - 1] + z[..., N_COLS_BASE:] @ rwkv_v2[layer - 1]
        yA, v_cur = rwkv7_mix(zA, v_first, v_mix, rwkv_mu[layer], rwkv_w0[layer], rwkv_w2[layer], rwkv_a0[layer],
                              rwkv_a2[layer], rwkv_g2[layer], rwkv_k_k[layer], rwkv_k_a[layer], rwkv_r_k[layer],
                              rwkv_lnx_g[layer], rwkv_lnx_b[layer])
        if layer == 0:
            v_first = v_cur
        yB = hgrn2_mix(zB, lb_all[layer], hgrn_norm_w[layer])
        yC = mlstm_mix(zC, mlstm_conv_w[layer], mlstm_conv_b[layer], mlstm_i_bias[layer], mlstm_f_bias[layer],
                       mlstm_norm_w[layer])
        yD = rglru_mix(zD, lru_conv_w[layer], lru_conv_b[layer], lru_wx[layer], lru_bx[layer], lru_wa[layer],
                       lru_ba[layer], lru_lambda[layer])
        gates = jax.nn.sigmoid(zG).reshape(bsz, seq, N_BRANCH, D_MODEL)
        merged = jnp.zeros((bsz, seq, D_MODEL), F32)
        for n, yb in enumerate((yA, yB, yC, yD)):
            merged = merged + gates[:, :, n] * (yb @ w_branch[layer, n])
        mix = merged @ w_out[layer]
        x = _layernorm(DEEPNORM_ALPHA * x + mix, ln1_g[layer], ln1_b[layer], dt)
        moe_out = moe(x.reshape(bsz * seq, D_MODEL), router_w[layer], router_b[layer], expert_w_gu[layer],
                      expert_b_gu[layer], expert_w_down[layer], expert_b_down[layer]).reshape(bsz, seq, D_MODEL)
        ple = jax.nn.sigmoid(x @ ple_gate_w[layer]) * (p[layer] @ ple_proj_w[layer])
        x = _layernorm(DEEPNORM_ALPHA * x + moe_out + ple, ln2_g[layer], ln2_b[layer], dt)
    return x


DEPTH_2 = 2

N_META = 16
META_PAD = CHUNK - N_META
HEAD_DIM = 64
A_HEADS = 8
IDX_HEADS = 8
IDX_DIM = 64
DSA_MAX_K = 256
A_QBLK = 64
B_HEADS = 8
B_VDIM = 2 * HEAD_DIM
C_HEADS = 8
C_KV_HEADS = 2
C_WINDOW = 128
C_WIN_CHUNKS = C_WINDOW // CHUNK
D_WIDTH = 512
POOL_WINDOWS = (2, 4, 8, 16)
D_GROUP = D_WIDTH // len(POOL_WINDOWS)
D_FF = 2816
EPS = 1e-6
NEG = -1e30

EVEN_SIZES = ([A_HEADS * HEAD_DIM] * 3 + [IDX_HEADS * IDX_DIM, IDX_DIM, IDX_HEADS]
              + [B_HEADS * HEAD_DIM] * 2 + [B_HEADS * B_VDIM] * 2)
EVEN_IN = sum(EVEN_SIZES)
EVEN_OUT = A_HEADS * HEAD_DIM + B_HEADS * B_VDIM
ODD_SIZES = [C_HEADS * HEAD_DIM, C_KV_HEADS * HEAD_DIM, C_KV_HEADS * HEAD_DIM, D_WIDTH]
ODD_IN = sum(ODD_SIZES)
ODD_OUT = C_HEADS * HEAD_DIM + D_WIDTH
N_EVEN = (DEPTH_2 + 1) // 2
N_ODD = DEPTH_2 // 2


def rms_norm(x, gain=None):
    xf = x.astype(jnp.float32)
    y = xf * lax.rsqrt(jnp.mean(xf * xf, axis=-1, keepdims=True) + EPS)
    if gain is not None:
        y = y * gain.astype(jnp.float32)
    return y.astype(x.dtype)

def swiglu(x, w_in, w_out):
    g, u = jnp.split(x @ w_in, 2, axis=-1)
    return (jax.nn.silu(g) * u) @ w_out

def split_cols(a, sizes):
    out, off = [], 0
    for s in sizes:
        out.append(a[..., off:off + s])
        off += s
    return out

def chunk_ids(n):
    return (jnp.arange(n) + META_PAD) // CHUNK

def pad_left(a):
    return jnp.pad(a, [(0, 0), (META_PAD, 0)] + [(0, 0)] * (a.ndim - 2))

def dsa_attention(q, k, v, iq, ik, iw, top_k):
    B, L, H, dh = q.shape
    cid = chunk_ids(L)
    nb = -(-L // A_QBLK)
    padn = nb * A_QBLK - L

    def blocks(a):
        a = jnp.pad(a, [(0, 0), (0, padn)] + [(0, 0)] * (a.ndim - 2))
        return jnp.moveaxis(a.reshape((B, nb, A_QBLK) + a.shape[2:]), 1, 0)

    q_cid = chunk_ids(nb * A_QBLK).reshape(nb, A_QBLK)
    iw = iw * (IDX_HEADS ** -0.5 * IDX_DIM ** -0.5)
    gather = jax.vmap(lambda t, i: t[i])

    def one_block(args):
        qb, iqb, iwb, qc = args
        logits = jnp.einsum('bqhd,bsd->bqhs', iqb, ik)
        score = jnp.einsum('bqh,bqhs->bqs', iwb, jax.nn.relu(logits)).astype(jnp.float32)
        adm = cid[None, :] <= qc[:, None]
        score = jnp.where(adm[None], score, NEG)
        _, idx = lax.top_k(score, top_k)
        valid = cid[idx] <= qc[None, :, None]
        kg = gather(k, idx)
        vg = gather(v, idx)
        s = jnp.einsum('bqhd,bqkhd->bhqk', qb, kg).astype(jnp.float32) * dh ** -0.5
        s = jnp.where(valid[:, None], s, NEG)
        p = jax.nn.softmax(s, axis=-1).astype(v.dtype)
        return jnp.einsum('bhqk,bqkhd->bqhd', p, vg)

    out = lax.map(one_block, (blocks(q), blocks(iq), blocks(iw), q_cid))
    return jnp.moveaxis(out, 0, 1).reshape(B, nb * A_QBLK, H, dh)[:, :L]

def rotary(x, pos):
    d = x.shape[-1]
    inv = 1.0 / (10000.0 ** (jnp.arange(0, d, 2, dtype=jnp.float32) / d))
    ang = pos.astype(jnp.float32)[:, None] * inv[None]
    cos = jnp.cos(ang)[None, :, None, :]
    sin = jnp.sin(ang)[None, :, None, :]
    x1, x2 = jnp.split(x.astype(jnp.float32), 2, axis=-1)
    return jnp.concatenate([x1 * cos - x2 * sin, x1 * sin + x2 * cos], axis=-1).astype(x.dtype)

def retention(q, k, v):
    B, Lp, H, dk = q.shape
    dv = v.shape[-1]
    N = Lp // CHUNK
    pos = jnp.arange(Lp) - META_PAD
    q = rotary(q, pos)
    k = rotary(k, pos) * dk ** -0.5
    log_g = jnp.log(1.0 - 2.0 ** (-5.0 - jnp.arange(H, dtype=jnp.float32)))
    i = jnp.arange(CHUNK, dtype=jnp.float32)
    rel = i[:, None] - i[None, :]
    dmat = jnp.where(rel >= 0, jnp.exp(jnp.maximum(rel, 0.0)[None] * log_g[:, None, None]), 0.0)
    q_dec = jnp.exp((i + 1.0)[:, None] * log_g[None])
    k_dec = jnp.exp((CHUNK - 1.0 - i)[:, None] * log_g[None])
    c_dec = jnp.exp(CHUNK * log_g)
    qc = q.reshape(B, N, CHUNK, H, dk)
    kc = k.reshape(B, N, CHUNK, H, dk)
    vc = v.reshape(B, N, CHUNK, H, dv)
    inner = jnp.einsum('bnihd,bnjhd->bnhij', qc, kc) * dmat.astype(q.dtype)
    inner = jnp.einsum('bnhij,bnjhe->bnihe', inner, vc)

    def step(S, xs):
        qn, kn, vn = xs
        cross = jnp.einsum('bihd,bhde->bihe', qn, S) * q_dec[None, :, :, None]
        S = S * c_dec[None, :, None, None] + jnp.einsum(
            'bjhd,bjhe->bhde', kn * k_dec[None, :, :, None], vn)
        return S, cross

    S0 = jnp.zeros((B, H, dk, dv), jnp.float32)
    _, cross = lax.scan(step, S0, (jnp.moveaxis(qc, 1, 0), jnp.moveaxis(kc, 1, 0),
                                   jnp.moveaxis(vc, 1, 0)))
    out = inner + jnp.moveaxis(cross, 0, 1).astype(inner.dtype)
    return out.reshape(B, Lp, H, dv)

def swa_sinks(q, k, v, sinks):
    B, Lp, H, dh = q.shape
    G = k.shape[2]
    R = H // G
    N = Lp // CHUNK
    W = C_WIN_CHUNKS

    def band(t):
        tc = t.reshape(B, N, CHUNK, G, dh)
        tp = jnp.pad(tc, ((0, 0), (W, 0), (0, 0), (0, 0), (0, 0)))
        bnd = jnp.concatenate([tp[:, j:j + N] for j in range(W + 1)], axis=2)
        meta = jnp.broadcast_to(t[:, META_PAD:CHUNK][:, None], (B, N, N_META, G, dh))
        return jnp.concatenate([meta, bnd], axis=2)

    kb, vb = band(k), band(v)
    key_chunk = jnp.arange(N)[:, None] - W + (jnp.arange((W + 1) * CHUNK) // CHUNK)[None]
    valid = jnp.concatenate([jnp.ones((N, N_META), bool), key_chunk >= 1], axis=1)
    qg = q.reshape(B, N, CHUNK, G, R, dh)
    s = jnp.einsum('bncgrd,bnkgd->bngrck', qg, kb).astype(jnp.float32) * dh ** -0.5
    s = jnp.where(valid[None, :, None, None, None, :], s, NEG)
    sink = jnp.broadcast_to(sinks.reshape(G, R).astype(jnp.float32)[None, None, :, :, None, None],
                            s.shape[:-1] + (1,))
    p = jax.nn.softmax(jnp.concatenate([s, sink], axis=-1), axis=-1)[..., :-1].astype(v.dtype)
    out = jnp.einsum('bngrck,bnkgd->bncgrd', p, vb)
    return out.reshape(B, Lp, H, dh)

def pool_mixer(x, d_mix, d_scale):
    B, L, _ = x.shape
    xg = x.astype(jnp.float32).reshape(B, L, len(POOL_WINDOWS), D_GROUP)
    cs = jnp.pad(jnp.cumsum(xg, axis=1), ((0, 0), (1, 0), (0, 0), (0, 0)))
    t = jnp.arange(L)
    pooled = []
    for gi, w in enumerate(POOL_WINDOWS):
        c = cs[:, :, gi]
        lag = jnp.pad(c, ((0, 0), (w, 0), (0, 0)))[:, 1:L + 1]
        cnt = jnp.minimum(t + 1, w).astype(jnp.float32)[None, :, None]
        pooled.append((c[:, 1:] - lag) / cnt)
    pooled = jnp.stack(pooled, axis=2)
    y = (pooled - xg).astype(x.dtype)
    y = jnp.einsum('blgc,gce->blge', y, d_mix).reshape(B, L, D_WIDTH)
    return y * d_scale

def even_mixer(h, w_in, a_qn, a_kn, w_out, top_k):
    B, L, _ = h.shape
    aq, ak, av, iq, ik, iw, bq, bk, bv, bg = split_cols(h @ w_in, EVEN_SIZES)
    hd = lambda t, n: t.reshape(B, L, n, -1)
    aq = rms_norm(hd(aq, A_HEADS), a_qn)
    ak = rms_norm(hd(ak, A_HEADS), a_kn)
    ya = dsa_attention(aq, ak, hd(av, A_HEADS), hd(iq, IDX_HEADS), ik, iw, top_k)
    ya = ya.reshape(B, L, -1)
    yb = retention(pad_left(hd(bq, B_HEADS)), pad_left(hd(bk, B_HEADS)),
                   pad_left(hd(bv, B_HEADS)))[:, META_PAD:]
    yb = rms_norm(yb).astype(h.dtype).reshape(B, L, -1) * jax.nn.silu(bg)
    return jnp.concatenate([ya, yb], axis=-1) @ w_out

def odd_mixer(h, w_in, c_qn, c_kn, c_sinks, d_mix, d_scale, w_out):
    B, L, _ = h.shape
    cq, ck, cv, dx = split_cols(h @ w_in, ODD_SIZES)
    hd = lambda t, n: t.reshape(B, L, n, -1)
    cq = rms_norm(hd(cq, C_HEADS), c_qn)
    ck = rms_norm(hd(ck, C_KV_HEADS), c_kn)
    yc = swa_sinks(pad_left(cq), pad_left(ck), pad_left(hd(cv, C_KV_HEADS)), c_sinks)
    yc = yc[:, META_PAD:].reshape(B, L, -1)
    yd = pool_mixer(dx, d_mix, d_scale)
    return jnp.concatenate([yc, yd], axis=-1) @ w_out

def second_inputs(seed: int = 0) -> dict:
    key = jax.random.key(seed)
    ks = jax.random.split(key, 21)
    f32 = jnp.float32
    nrm = lambda k, shape, fan: jax.random.normal(k, shape, f32) * fan ** -0.5
    gain = lambda k, shape: 1.0 + 0.05 * jax.random.normal(k, shape, f32)
    return {
        "x": jax.random.normal(ks[0], (BATCH, SEQ, D_MODEL), f32),
        "meta_tokens": jax.random.normal(ks[1], (N_META, D_MODEL), f32),
        "ffn1_norm": gain(ks[2], (DEPTH_2, D_MODEL)),
        "ffn1_w_in": nrm(ks[3], (DEPTH_2, D_MODEL, 2 * D_FF), D_MODEL),
        "ffn1_w_out": nrm(ks[4], (DEPTH_2, D_FF, D_MODEL), D_FF),
        "mix_norm": gain(ks[5], (DEPTH_2, D_MODEL)),
        "ffn2_norm": gain(ks[6], (DEPTH_2, D_MODEL)),
        "ffn2_w_in": nrm(ks[7], (DEPTH_2, D_MODEL, 2 * D_FF), D_MODEL),
        "ffn2_w_out": nrm(ks[8], (DEPTH_2, D_FF, D_MODEL), D_FF),
        "ev_w_in": nrm(ks[9], (N_EVEN, D_MODEL, EVEN_IN), D_MODEL),
        "ev_a_q_norm": gain(ks[10], (N_EVEN, HEAD_DIM)),
        "ev_a_k_norm": gain(ks[11], (N_EVEN, HEAD_DIM)),
        "ev_w_out": nrm(ks[12], (N_EVEN, EVEN_OUT, D_MODEL), EVEN_OUT),
        "od_w_in": nrm(ks[13], (N_ODD, D_MODEL, ODD_IN), D_MODEL),
        "od_c_q_norm": gain(ks[14], (N_ODD, HEAD_DIM)),
        "od_c_k_norm": gain(ks[15], (N_ODD, HEAD_DIM)),
        "od_c_sinks": 0.5 * jax.random.normal(ks[16], (N_ODD, C_HEADS), f32),
        "od_d_mix": nrm(ks[17], (N_ODD, len(POOL_WINDOWS), D_GROUP, D_GROUP), D_GROUP),
        "od_d_scale": gain(ks[18], (N_ODD, D_WIDTH)),
        "od_w_out": nrm(ks[19], (N_ODD, ODD_OUT, D_MODEL), ODD_OUT),
    }

def second_block(x, meta_tokens, ffn1_norm, ffn1_w_in, ffn1_w_out, mix_norm, ffn2_norm,
              ffn2_w_in, ffn2_w_out, ev_w_in, ev_a_q_norm, ev_a_k_norm, ev_w_out,
              od_w_in, od_c_q_norm, od_c_k_norm, od_c_sinks, od_d_mix, od_d_scale,
              od_w_out):
    B, S, D = x.shape
    top_k = min(DSA_MAX_K, S // 4)
    h = jnp.concatenate([jnp.broadcast_to(meta_tokens.astype(x.dtype)[None], (B, N_META, D)), x],
                        axis=1)
    for layer in range(DEPTH_2):
        h = h + (0.5 * swiglu(rms_norm(h, ffn1_norm[layer]), ffn1_w_in[layer],
                              ffn1_w_out[layer])).astype(h.dtype)
        hn = rms_norm(h, mix_norm[layer])
        if layer % 2 == 0:
            e = layer // 2
            y = even_mixer(hn, ev_w_in[e], ev_a_q_norm[e], ev_a_k_norm[e], ev_w_out[e], top_k)
        else:
            o = layer // 2
            y = odd_mixer(hn, od_w_in[o], od_c_q_norm[o], od_c_k_norm[o], od_c_sinks[o],
                          od_d_mix[o], od_d_scale[o], od_w_out[o])
        h = h + y.astype(h.dtype)
        h = h + (0.5 * swiglu(rms_norm(h, ffn2_norm[layer]), ffn2_w_in[layer],
                              ffn2_w_out[layer])).astype(h.dtype)
    return h[:, N_META:]


def setup_inputs(seed=0):
    out = dict(first_inputs(seed))
    for name, value in second_inputs(seed + 1).items():
        if name != "x":
            out[name + "_2"] = value
    return out


def reference(
    x, p, w_in_first, w_in_rest, rwkv_mu, rwkv_w0, rwkv_w2, rwkv_a0, rwkv_a2, rwkv_v0, rwkv_v2,
    rwkv_g2, rwkv_k_k, rwkv_k_a, rwkv_r_k, rwkv_lnx_g, rwkv_lnx_b, hgrn_lower_bounds,
    hgrn_norm_w, mlstm_conv_w, mlstm_conv_b, mlstm_i_bias, mlstm_f_bias, mlstm_norm_w,
    lru_conv_w, lru_conv_b, lru_wx, lru_bx, lru_wa, lru_ba, lru_lambda, w_branch, w_out, ln1_g,
    ln1_b, router_w, router_b, expert_w_gu, expert_b_gu, expert_w_down, expert_b_down,
    ple_gate_w, ple_proj_w, ln2_g, ln2_b, meta_tokens_2, ffn1_norm_2, ffn1_w_in_2, ffn1_w_out_2,
    mix_norm_2, ffn2_norm_2, ffn2_w_in_2, ffn2_w_out_2, ev_w_in_2, ev_a_q_norm_2, ev_a_k_norm_2,
    ev_w_out_2, od_w_in_2, od_c_q_norm_2, od_c_k_norm_2, od_c_sinks_2, od_d_mix_2, od_d_scale_2,
    od_w_out_2,
):
    x = first_block(
        x, p, w_in_first, w_in_rest, rwkv_mu, rwkv_w0, rwkv_w2, rwkv_a0, rwkv_a2, rwkv_v0,
        rwkv_v2, rwkv_g2, rwkv_k_k, rwkv_k_a, rwkv_r_k, rwkv_lnx_g, rwkv_lnx_b,
        hgrn_lower_bounds, hgrn_norm_w, mlstm_conv_w, mlstm_conv_b, mlstm_i_bias, mlstm_f_bias,
        mlstm_norm_w, lru_conv_w, lru_conv_b, lru_wx, lru_bx, lru_wa, lru_ba, lru_lambda,
        w_branch, w_out, ln1_g, ln1_b, router_w, router_b, expert_w_gu, expert_b_gu,
        expert_w_down, expert_b_down, ple_gate_w, ple_proj_w, ln2_g, ln2_b,
    )
    return second_block(
        x, meta_tokens_2, ffn1_norm_2, ffn1_w_in_2, ffn1_w_out_2, mix_norm_2, ffn2_norm_2,
        ffn2_w_in_2, ffn2_w_out_2, ev_w_in_2, ev_a_q_norm_2, ev_a_k_norm_2, ev_w_out_2,
        od_w_in_2, od_c_q_norm_2, od_c_k_norm_2, od_c_sinks_2, od_d_mix_2, od_d_scale_2,
        od_w_out_2,
    )


_drawn_inputs = setup_inputs


def setup_inputs(seed=0):
    import zlib

    import numpy as np

    out = dict(_drawn_inputs(seed))
    spreads = {}
    factors = {'rwkv_w2': 2.7,
     'rwkv_lnx_b': 3.67,
     'mlstm_conv_b': 3.399,
     'mlstm_i_bias': 200.0,
     'lru_bx': 7.214,
     'lru_ba': 8.0,
     'expert_b_gu': 4.614,
     'expert_b_down': 3.439,
     'ev_a_q_norm_2': 8.0,
     'ev_a_k_norm_2': 8.0,
     'od_c_q_norm_2': 8.0,
     'od_c_k_norm_2': 8.0,
     'od_c_sinks_2': 8.0,
     'od_d_scale_2': 3.005}
    for name, (base, spread) in spreads.items():
        noise = np.random.default_rng([zlib.crc32(name.encode()), seed]).standard_normal(out[name].shape)
        drawn = base * np.exp(spread * noise) if base else spread * noise
        out[name] = jnp.asarray(drawn.astype(out[name].dtype))
    for name, factor in factors.items():
        out[name] = (out[name] * factor).astype(out[name].dtype)
    return out
```

```python
from contextlib import ExitStack

import numpy as np

import concourse.bass as bass
from concourse import mybir

F32 = mybir.dt.float32
ALU = mybir.AluOpType
ACT = mybir.ActivationFunctionType
AX = mybir.AxisListType

P = 128
T1 = 256
META = 16
T2 = T1 + META
D = 1024
DT = D // P
W = 512
WT = W // P
NE = 32
CHUNK_TILES = 32
SLOTS = 6
EXPERT_TILES = 3 * DT * DT
FF = 2816
FFT = FF // P
RC = 16
TOPK2 = 64
FEW = 64
SLOTS_SMALL = FEW
NEG = -1e30
ALPHA = 2.0 ** 0.25
Q3 = [(0, 128), (128, 128), (256, T2 - 256)]


def tile_groups():
    r_cols = 1792
    b0, c0 = r_cols, r_cols + 2048
    d0 = c0 + 2048 + 8
    g0 = d0 + 1024
    out = []

    def per_out(name, idx, k, cols):
        out.append((name, idx, k, list(cols), "nk"))

    def per_in(name, idx, k, cols):
        out.append((name, idx, k, list(cols), "kn"))

    kx = range(DT)
    per_out("w_in_first", None, kx, range(0, r_cols, P))
    per_out("w_in_first", None, kx, [*range(b0, b0 + 1024, P), *range(b0 + 1536, b0 + 2048, P)])
    per_in("w_in_first", None, kx, range(b0 + 1024, b0 + 1536, P))
    per_out("w_in_first", None, kx, [*range(c0, c0 + 1024, P), *range(c0 + 1536, c0 + 2048, P)])
    per_in("w_in_first", None, kx, range(c0 + 1024, c0 + 1536, P))
    per_out("w_in_first", None, kx, range(d0, d0 + 1024, P))
    for d in range(DT):
        for n in range(4):
            per_out("w_in_first", None, kx, [g0 + n * D + d * P])
            per_out("w_branch", (0, n), range(WT), [d * P])
    per_out("w_out", (0,), kx, range(0, D, P))
    per_out("ple_gate_w", (0,), kx, range(0, D, P))
    per_out("ple_proj_w", (0,), range(2), range(0, D, P))
    for e in range(NE):
        per_in("expert_w_gu", (0, e), kx, range(0, D, P))
        per_in("expert_w_gu", (0, e), kx, range(D, 2 * D, P))
        per_in("expert_w_down", (0, e), kx, range(0, D, P))

    def ffn(name, layer):
        per_out(name + "_w_in_2", (layer,), kx, [c for j in range(FFT) for c in (j * P, FF + j * P)])
        per_out(name + "_w_out_2", (layer,), range(FFT), range(0, D, P))

    ffn("ffn1", 0)
    per_out("ev_w_in_2", (0,), kx, range(0, 1024, P))
    per_out("ev_w_in_2", (0,), kx, range(1536, 2048, P))
    per_out("ev_ik", None, kx, [0])
    per_out("ev_w_in_2", (0,), kx, range(2120, 3144, P))
    per_out("ev_w_in_2", (0,), kx, range(4168, 5192, P))
    per_in("ev_w_in_2", (0,), kx, range(1024, 1536, P))
    per_in("ev_w_in_2", (0,), kx, range(3144, 3656, P))
    per_in("ev_w_in_2", (0,), kx, range(3656, 4168, P))
    per_out("ev_w_out_2", (0,), range(12), range(0, D, P))
    ffn("ffn2", 0)
    ffn("ffn1", 1)
    per_out("od_w_in_2", (0,), kx, range(0, 512, P))
    per_out("od_ck", None, kx, [0, P])
    per_out("od_w_in_2", (0,), kx, range(768, 1280, P))
    per_out("od_w_in_2", (0,), kx, [640])
    per_out("od_w_out_2", (0,), kx, range(0, D, P))
    ffn("ffn2", 1)
    return out


N_TILES = sum(len(g[2]) * len(g[3]) for g in tile_groups())
N_CHUNKS = N_TILES // CHUNK_TILES
assert N_TILES % (CHUNK_TILES * SLOTS) == 0

COLUMNS = [("rwkv_mu", 14), ("rwkv_w0", 4), ("rwkv_a0", 4), ("rwkv_k_k", 4), ("rwkv_k_a", 4), ("rwkv_r_k", 4),
           ("rwkv_lnx_g", 4), ("rwkv_lnx_b", 4), ("hgrn_norm_w", 4), ("mlstm_conv_w", 32), ("mlstm_conv_b", 8),
           ("mlstm_norm_w", 4), ("lru_conv_w", 16), ("lru_conv_b", 4), ("lru_bx", 4), ("lru_ba", 4),
           ("lru_lambda", 4), ("ln1_g", 8), ("ln1_b", 8), ("ln2_g", 8), ("ln2_b", 8), 
           ("ffn1_norm_2", 16), ("mix_norm_2", 16), ("ffn2_norm_2", 16), ("od_d_scale_2", 4)]
COL_AT = {}
_n = 0
for _name, _tiles in COLUMNS:
    COL_AT[_name] = _n
    _n += _tiles
N_COLS = _n


def constants():
    i = np.arange(P)
    c = {}
    c["eye"] = np.eye(P)
    c["ones"] = np.ones((P, P))
    c["before"] = (i[:, None] < i[None]) * 1.0
    c["slots"] = np.ones((P, 1)) * np.arange(SLOTS_SMALL)
    c["ones_pair"] = (i[:, None] // 64 == i[None] // 64) * 1.0
    c["stacked_eye"] = np.vstack([np.eye(64), np.eye(64)])
    rot = np.zeros((P, P))
    for h in (0, 64):
        for d in range(32):
            rot[h + 32 + d, h + d] = -1.0
            rot[h + d, h + 32 + d] = 1.0
    c["rot"] = rot
    t = np.arange(T1)
    every = np.ones((P, 1))
    c["restart_rwkv"] = every * (t % RC != 0)
    c["restart_row"] = every * (t != 0)
    head, tm = i // RC, i % RC
    same = head[:, None] == head[None]
    c["rwkv_strict"] = same * (tm[:, None] < tm[None]) * 1.0
    c["rwkv_upto"] = same * (tm[:, None] <= tm[None]) * 1.0
    c["rwkv_below"] = same * (tm[:, None] > tm[None]) * 1.0
    levels = [np.eye(P)]
    for l in range(1, 8):
        b, half = 2 ** l, 2 ** (l - 1)
        levels.append((i[:, None] // b == i[None] // b) * (i[:, None] % b < half) * (i[None] % b >= half) * 1.0)
    c["hgrn_levels"] = np.concatenate(levels, 1)
    c["mlstm_mask"] = np.concatenate([np.where((i[:, None] + s) <= t[None], 0.0, NEG) for s in (0, P)], 1)
    c["row_select"] = np.concatenate([(i == h)[:, None] * np.ones((1, P)) for h in range(4)], 1)
    tok = np.arange(T2)
    ck = (tok + 48) // 64
    qi = [np.minimum(q0 + i, T2 - 1) for q0, _ in Q3]
    c["dsa_mask"] = np.concatenate([np.where(ck[None] <= ck[q][:, None], 0.0, NEG) for q in qi], 1)
    c["swa_mask"] = np.concatenate([
        np.where((tok[None] < META) | ((ck[None] >= 1) & (ck[None] <= ck[q][:, None]) & (ck[None] >= ck[q][:, None] - 2)),
                 0.0, NEG) for q in qi], 1)
    c["ret_mask"] = np.concatenate([(q[:, None] <= tok[None]) * 1.0 for q in qi], 1)
    inv = 1.0 / (10000.0 ** (np.arange(0, 64, 2, dtype=np.float32) / np.float32(64)))
    ang = tok.astype(np.float32)[None] * inv.astype(np.float32)[i % 32][:, None]
    c["cos"], c["sin"] = np.cos(ang), np.sin(ang)
    lg = np.log(1.0 - 2.0 ** (-5.0 - np.arange(8)))
    hd = 2 * np.arange(4)[None] + (i // 64)[:, None]
    c["ret_q"] = np.exp(tok[None, None] * lg[hd][:, :, None]).reshape(P, -1)
    c["ret_k"] = (np.exp(-tok[None, None] * lg[hd][:, :, None]) * 64 ** -0.5).reshape(P, -1)
    c["pool_inv"] = np.concatenate([every / np.minimum(tok + 1, w) for w in (2, 4, 8, 16)], 1)
    return {k: np.ascontiguousarray(v, dtype=np.float32) for k, v in c.items()}


CONST_SETS = {"all": ["eye", "ones", "ones_pair"],
              "router": ["before"], "experts": ["slots"],
              "rwkv": ["restart_rwkv", "stacked_eye", "rwkv_strict", "rwkv_upto", "rwkv_below"],
              "hgrn": ["restart_row", "hgrn_levels"],
              "mlstm": ["mlstm_mask", "row_select"],
              "even": ["dsa_mask"], "ret": ["ret_mask", "rot", "cos", "sin", "ret_q", "ret_k"],
              "odd": ["swa_mask", "pool_inv"]}


class Signal:

    def __init__(self, sem, count=0):
        self.sem, self.posts, self.takes, self.turn, self.turn_post = sem, count, count, None, None
        self.start = count

    def reader(self):
        return Signal(self.sem, self.start)

    def post(self):
        self.posts += 1
        return self.sem, 1

    def take(self, n=1):
        self.takes += n
        return self.sem, self._value(self.takes, self.turn)

    def posted(self):
        return self.sem, self._value(self.posts, self.turn_post)

    @staticmethod
    def _value(n, turn):
        return n if turn is None else turn[0] * turn[1] + n

    def begin(self, i, per, posts=False):
        if posts:
            self.turn_post, self._p0 = (i, per), self.posts
        else:
            self.turn, self._t0 = (i, per), self.takes

    def end(self, times, posts=False):
        if posts:
            per, self.turn_post = self.turn_post[1], None
            assert self.posts - self._p0 == per, (self.sem, "posts", self.posts - self._p0, per)
            self.posts = self._p0 + per * times
        else:
            per, self.turn = self.turn[1], None
            assert self.takes - self._t0 == per, (self.sem, "takes", self.takes - self._t0, per)
            self.takes = self._t0 + per * times


def counters(signals):
    return [(q.posts, q.takes) for q in signals]


def set_counters(signals, saved):
    for q, (posts, takes) in zip(signals, saved):
        q.posts, q.takes = posts, takes


class Weights:

    def __init__(self, ring, loaded, used):
        self.ring, self.loaded, self.used, self.at, self.pending, self.turn = ring, loaded, used, 0, None, None

    def take(self, pe, n=1):
        chunk, place = divmod(self.at, CHUNK_TILES)
        slot = chunk % SLOTS
        assert place + n <= CHUNK_TILES
        if place == 0:
            uses = chunk // SLOTS + 1
            if self.turn is not None:
                uses = self.turn[0] * self.turn[1] + uses
            pe.wait_ge(self.loaded[slot], uses * 16)
            assert self.pending is None
            if chunk:
                self.pending = (chunk - 1) % SLOTS
        self.at += n
        return self.ring[:, slot, place * P:(place + n) * P]


class Kernel:
    pass


def new_signal(K, name):
    sem, count = K.spare.pop() if K.spare else (K.new_semaphore(name), 0)
    K.counts.append(Signal(sem, count))
    return K.counts[-1]


def recycle(K):
    K.spare += [(s.sem, s.posts) for s in K.counts if s.takes in (s.start, s.posts)]
    K.counts = []


def matmul(K, out, lhsT, rhs, start, stop, signal=None):
    ins = K.nc.tensor.matmul(out, lhsT, rhs, start=start, stop=stop)
    if signal is not None:
        ins.then_inc(*signal.post())
    elif K.weights.pending is not None:
        ins.then_inc(K.weights.used[K.weights.pending], 1)
        K.weights.pending = None
    return ins


def stream_linear(K, pe, n_out, x, k_tiles, tokens, ready, free, banks=(0, 1, 2, 3)):
    for j in range(n_out):
        if j >= len(banks):
            pe.wait_ge(*free.take())
        for k in range(k_tiles):
            matmul(K, K.bank[banks[j % len(banks)]][:, 0:tokens], K.weights.take(pe), x(k), k == 0, k == k_tiles - 1,
                   ready if k == k_tiles - 1 else None)
    pe.wait_ge(*free.take(min(n_out, len(banks))))


def stream_tokens(K, pe, x, tiles, n, ready, free, banks):
    for k in range(DT):
        w = K.weights.take(pe, n)
        for b, (t0, tn) in enumerate(tiles):
            matmul(K, K.bank[banks[b]][0:tn, 0:n * P], x(k)[:, t0:t0 + tn], w, k == 0, k == DT - 1,
                   ready if k == DT - 1 else None)
    pe.wait_ge(*free.take(len(tiles)))


def flat(ap):
    return ap.rearrange("p a t -> p (a t)")


def linker(eng, chain):
    def then(ins):
        ins.then_inc(*chain.post())
        eng.wait_ge(*chain.posted())
    return then


class Norm:

    def __init__(self, K, st, name, x, out, lhsT, count, eps, mean=True, whole=False, banks=(4, 5)):
        self.K, self.x, self.out, self.lhsT, self.count, self.eps, self.mean, self.whole = \
            K, x, out, lhsT, count, eps, mean, whole
        self.banks = banks
        self.n, self.t = x.shape[1], x.shape[2]
        cols = self.t if whole else self.n * self.t
        self.cols = cols
        self.sq = st.enter_context(K.nc.sbuf_tensor(name + "_squares", [P, self.n, self.t], F32))
        self.rstd = st.enter_context(K.nc.sbuf_tensor(name + "_rstd", [P, cols], F32))
        self.given = new_signal(K, name + "_norm_given")
        self.summed = new_signal(K, name + "_norm_summed")
        self.var = new_signal(K, name + "_norm_var")
        self.root = new_signal(K, name + "_norm_root")

    def _parts(self):
        if self.whole:
            return [(self.banks[0], 0, self.t)]
        per = 512 // self.t
        return [(self.banks[i // per], i, min(per, self.n - i)) for i in range(0, self.n, per)]

    def _sums(self, src):
        if self.whole:
            for k in range(self.n):
                matmul(self.K, self.K.bank[self.banks[0]][:, 0:self.t], self.lhsT, src[:, k, :], k == 0, k == self.n - 1,
                       self.summed if k == self.n - 1 else None)
        else:
            parts = self._parts()
            for q, (b, i, m) in enumerate(parts):
                matmul(self.K, self.K.bank[b][:, 0:m * self.t], self.lhsT, flat(src[:, i:i + m, :]), True, True,
                       self.summed)

    def pe(self, pe):
        pe.wait_ge(*self.given.take())
        if self.mean:
            self._sums(self.x)
            pe.wait_ge(*self.given.take())
        self._sums(self.sq)

    def act(self, act):
        act.wait_ge(*self.var.take())
        act.activation(self.rstd[:, :], self.rstd[:, :], ACT.Sqrt).then_inc(*self.root.post())

    def dve(self, dve, chain, last):
        K, c = self.K, 1.0 / self.count
        if self.mean:
            dve.drain().then_inc(*self.given.post())
            if self.whole:
                dve.wait_ge(*self.summed.take())
                dve.tensor_scalar(self.rstd[:, :], K.bank[self.banks[0]][:, 0:self.t], c, None, ALU.mult).then_inc(*chain.post())
                dve.wait_ge(*chain.posted())
                mean = self.rstd[:, :].rearrange("p (a t) -> p a t", a=1).to_broadcast([P, self.n, self.t])
                dve.tensor_tensor(out=self.out, in0=self.x, in1=mean, op=ALU.subtract).then_inc(*chain.post())
            else:
                parts = self._parts()
                dve.wait_ge(*self.summed.take(len(parts)))
                for b, i, m in parts:
                    dve.scalar_tensor_tensor(out=flat(self.out[:, i:i + m, :]), in0=K.bank[b][:, 0:m * self.t], scalar=-c,
                                             in1=flat(self.x[:, i:i + m, :]), op0=ALU.mult, op1=ALU.add).then_inc(*chain.post())
            dve.wait_ge(*chain.posted())
            src = self.out
        else:
            src = self.x
        dve.tensor_tensor(out=self.sq[:, :, :], in0=src, in1=src, op=ALU.mult).then_inc(*self.given.post())
        parts = self._parts()
        dve.wait_ge(*self.summed.take(len(parts)))
        for b, i, m in parts:
            o = self.rstd[:, 0:self.t] if self.whole else self.rstd[:, i * self.t:(i + m) * self.t]
            s = self.t if self.whole else m * self.t
            ins = dve.tensor_scalar(o, K.bank[b][:, 0:s], c, self.eps, ALU.mult, ALU.add)
            ins.then_inc(*(self.var if (b, i, m) == parts[-1] else chain).post())
        dve.wait_ge(*self.root.take())
        dve.reciprocal(self.rstd[:, :], self.rstd[:, :]).then_inc(*chain.post())
        dve.wait_ge(*chain.posted())
        r = self.rstd[:, :].rearrange("p (a t) -> p a t", t=self.t)
        if self.whole:
            r = r.to_broadcast([P, self.n, self.t])
        dve.tensor_tensor(out=self.out, in0=src, in1=r, op=ALU.mult).then_inc(*last.post())


def end_stage(K):
    K.stages += 1
    n = K.stages
    recycle(K)

    @K.block.tensor
    def _(pe):
        pe.drain().then_inc(K.stage_done, 1)
        pe.wait_ge(K.stage_done, 3 * n)

    @K.block.scalar
    def _(act):
        act.drain().then_inc(K.stage_done, 1)
        act.wait_ge(K.stage_done, 3 * n)

    @K.block.vector
    def _(dve):
        dve.drain().then_inc(K.stage_done, 1)
        dve.wait_ge(K.stage_done, 3 * n)

    @K.block.gpsimd
    def _(pool):
        pool.wait_ge(K.stage_done, 3 * n)


def load_constants(K, st, name):
    out = {}
    for c in CONST_SETS[name]:
        out[c] = st.enter_context(K.nc.sbuf_tensor("c_" + c, [P, K.const_dram[c].shape[1]], F32))
    load(K, [(out[c][:, :], K.const_dram[c]) for c in CONST_SETS[name]])
    return out


def load(K, pairs):
    @K.block.gpsimd
    def _(pool):
        for dst, src in pairs:
            pool.dma_start(dst, src).then_inc(K.small_loaded, 16)
    K.small_loads += len(pairs)


def log_sigmoid(K, st, name, x, out):
    a = st.enter_context(K.nc.sbuf_tensor(name + "_abs", list(x.shape), F32))
    abs_ready, soft_ready = new_signal(K, name + "_abs_ready"), new_signal(K, name + "_soft_ready")

    def dve_abs(dve):
        dve.scalar_tensor_tensor(out=a[:, :], in0=x, scalar=-1.0, in1=x, op0=ALU.mult, op1=ALU.max)\
           .then_inc(*abs_ready.post())

    def act_log(act, chain):
        act.wait_ge(*abs_ready.take())
        act.activation(a[:, :], a[:, :], ACT.Exp, scale=-1.0).then_inc(*chain.post())
        act.wait_ge(*chain.posted())
        act.activation(a[:, :], a[:, :], ACT.Ln, bias=1.0).then_inc(*soft_ready.post())

    def dve_log(dve, last):
        dve.wait_ge(*soft_ready.take())
        dve.scalar_tensor_tensor(out=out, in0=x, scalar=0.0, in1=a[:, :], op0=ALU.min, op1=ALU.subtract)\
           .then_inc(*last.post())

    return dve_abs, act_log, dve_log


def rwkv_branch(K):
    nc, block, bank, col = K.nc, K.block, K.bank, K.col
    T = T1
    y = K.y_branch[:, 0]
    with ExitStack() as st:
        def sb(name, shape):
            return st.enter_context(nc.sbuf_tensor("rwkv_" + name, shape, F32))

        con = load_constants(K, st, "rwkv")
        w2a2, g2 = sb("w2a2", [P, W]), sb("g2", [P, W])
        load(K, [(w2a2[:, :], K.dram["rwkv_w2a2"]), (g2[:, :], K.dram["rwkv_g2"])])
        loads = 16 * K.small_loads

        zs = sb("shifted", [P, 14, T])
        g, lsum, lprev, sq = (sb(n, [P, 4, T]) for n in ("g", "log_sum", "log_prev", "kk_sq"))
        bt, kt, rt = (sb(n, [P, 4, T]) for n in ("b_t", "k_t", "r_t"))
        at, ew = lprev, lsum
        with ExitStack() as early:
            z = early.enter_context(nc.sbuf_tensor("rwkv_z", [P, 14, T + 1], F32))
            diff = early.enter_context(nc.sbuf_tensor("rwkv_diff", [P, T], F32))
        with ExitStack() as middle:
            tw, sg, av, lw, kk, nrm, en = (middle.enter_context(nc.sbuf_tensor("rwkv_" + n, shape, F32)) for n, shape in (
                ("tanh_w", [64, T]), ("sig_g", [P, T]), ("a", [P, 4, T]), ("log_w", [P, 4, T]), ("kk", [P, 4, T]),
                ("kk_norm", [P, 4, T]), ("exp_neg", [P, 4, T])))
        bonus = sq
        r, k, v = zs[:, 0:4, :], zs[:, 4:8, :], zs[:, 8:12, :]

        z_ready, z_free, _ = new_signal(K, "rw_z_ready"), new_signal(K, "rw_z_free"), None
        z_sb = z_free.reader()
        shifted, gates_in = new_signal(K, "rw_shifted"), new_signal(K, "rw_gates_in")
        lora_ready, lora_free, lora_out = new_signal(K, "rw_lora_ready"), new_signal(K, "rw_lora_free"), new_signal(K, "rw_lora_out")
        sums_ready, exps_ready = new_signal(K, "rw_log_sums"), new_signal(K, "rw_exps")
        sq_ready, ss_ready, nrm_ready = new_signal(K, "rw_sq"), new_signal(K, "rw_ss"), new_signal(K, "rw_nrm")
        rk_ready, bonus_ready = new_signal(K, "rw_rk"), new_signal(K, "rw_bonus")
        link, alink, gates_in_dve = new_signal(K, "rw_dve_chain"), new_signal(K, "rw_act_chain"), new_signal(K, "rw_low_rank_shifted")

        @block.tensor
        def _(pe):
            pe.wait_ge(K.x_loaded, 16)
            stream_linear(K, pe, 14, lambda k: K.x[:, k, 0:T], DT, T, z_ready, z_free)
            pe.wait_ge(*gates_in.take())
            pe.wait_ge(*shifted.take())
            pe.wait_ge(K.small_loaded, loads)
            for j in range(12):
                if j >= 4:
                    pe.wait_ge(*lora_free.take())
                f, q = divmod(j, 4)
                a, x = [(w2a2[0:64, q * P:(q + 1) * P], tw[:, :]), (w2a2[64:P, q * P:(q + 1) * P], zs[64:P, 12, :]),
                        (g2[:, q * P:(q + 1) * P], sg[:, :])][f]
                matmul(K, bank[j % 4][:, 0:T], a, x, True, True, lora_ready)
            pe.wait_ge(*lora_free.take(4))
            pe.wait_ge(*sq_ready.take())
            for q in range(2):
                matmul(K, bank[q][:, :], K.con["ones_pair"][:, :], flat(sq[:, 2 * q:2 * q + 2, :]), True, True, ss_ready)
            pe.wait_ge(*rk_ready.take())
            for q in range(2):
                matmul(K, bank[q][:, :], K.con["ones_pair"][:, :], flat(kk[:, 2 * q:2 * q + 2, :]), True, True, bonus_ready)

        @block.scalar
        def _(act):
            for j in range(14):
                act.wait_ge(*z_ready.take())
                act.activation(z[:, j, 1:T + 1], bank[j % 4][:, 0:T], ACT.Copy).then_inc(*z_free.post())
            act.wait_ge(*gates_in_dve.take())
            act.activation(tw[:, :], zs[0:64, 12, :], ACT.Tanh).then_inc(*alink.post())
            act.activation(sg[:, :], zs[:, 13, :], ACT.Sigmoid).then_inc(*gates_in.post())
            for j in range(12):
                f, q = divmod(j, 4)
                act.wait_ge(*lora_ready.take())
                if f == 0:
                    act.activation(lw[:, q, :], bank[j % 4][:, 0:T], ACT.Sigmoid, bias=col("rwkv_w0", q)).then_inc(*lora_free.post())
                elif f == 1:
                    act.activation(av[:, q, :], bank[j % 4][:, 0:T], ACT.Sigmoid, bias=col("rwkv_a0", q)).then_inc(*lora_free.post())
                else:
                    act.activation(g[:, q, :], bank[j % 4][:, 0:T], ACT.Copy).then_inc(*lora_free.post())
            act.drain().then_inc(*lora_out.post())
            act.wait_ge(*sums_ready.take())
            act.activation(flat(en[:, :, :]), flat(lsum[:, :, :]), ACT.Exp, scale=-1.0).then_inc(*alink.post())
            act.wait_ge(*alink.posted())
            act.activation(flat(ew[:, :, :]), flat(lsum[:, :, :]), ACT.Exp).then_inc(*alink.post())
            act.activation(flat(lprev[:, :, :]), flat(lprev[:, :, :]), ACT.Exp).then_inc(*exps_ready.post())
            act.wait_ge(*ss_ready.take(2))
            for q in range(2):
                act.activation(flat(nrm[:, 2 * q:2 * q + 2, :]), bank[q][:, :], ACT.Sqrt).then_inc(*(nrm_ready if q else alink).post())

        @block.vector
        def _(dve):
            then = linker(dve, link)

            then(dve.memset(z[:, :, 0:1], 0.0))
            dve.wait_ge(K.small_loaded, loads)
            dve.wait_ge(K.cols_loaded, 16)
            for j in range(14):
                dve.wait_ge(*z_sb.take())
                then(dve.tensor_tensor(out=diff[:, :], in0=z[:, j, 0:T], in1=z[:, j, 1:T + 1], op=ALU.subtract))
                ins = dve.scalar_tensor_tensor(out=zs[:, j, :], in0=diff[:, :], scalar=col("rwkv_mu", j), in1=z[:, j, 1:T + 1],
                                               op0=ALU.mult, op1=ALU.add)
                if j < 12:
                    ins.then_inc(*link.post())
                elif j == 12:
                    ins.then_inc(*shifted.post())
                else:
                    ins.then_inc(*gates_in_dve.post())
                dve.wait_ge(*(link if j < 12 else shifted if j == 12 else gates_in_dve).posted())
            dve.wait_ge(*lora_out.take())
            then(dve.tensor_scalar(flat(lw[:, :, :]), flat(lw[:, :, :]), -float(np.exp(-0.5)), None, ALU.mult))
            for q in range(4):
                ins = dve.tensor_tensor_scan(out=lsum[:, q, :], data0=con["restart_rwkv"][:, :], data1=lw[:, q, :],
                                             initial=0.0, op0=ALU.mult, op1=ALU.add)
                then(ins)
            dve.tensor_tensor(out=lprev[:, :, :], in0=lsum[:, :, :], in1=lw[:, :, :], op=ALU.subtract).then_inc(*sums_ready.post())
            for q in range(4):
                then(dve.tensor_scalar(kk[:, q, :], k[:, q, :], col("rwkv_k_k", q), None, ALU.mult))
            dve.tensor_tensor(out=sq[:, :, :], in0=kk[:, :, :], in1=kk[:, :, :], op=ALU.mult).then_inc(*sq_ready.post())
            for q in range(4):
                then(dve.tensor_scalar(kt[:, q, :], av[:, q, :], -1.0, col("rwkv_k_a", q), ALU.add, ALU.mult))
            then(dve.scalar_tensor_tensor(out=kt[:, :, :], in0=kt[:, :, :], scalar=1.0, in1=k, op0=ALU.add, op1=ALU.mult))
            dve.wait_ge(*nrm_ready.take())
            then(dve.tensor_scalar(nrm[:, :, :], nrm[:, :, :], 1e-12, None, ALU.max))
            then(dve.reciprocal(nrm[:, :, :], nrm[:, :, :]))
            then(dve.tensor_tensor(out=nrm[:, :, :], in0=kk[:, :, :], in1=nrm[:, :, :], op=ALU.mult))
            dve.wait_ge(*exps_ready.take())
            then(dve.scalar_tensor_tensor(out=at[:, :, :], in0=nrm[:, :, :], scalar=-1.0, in1=lprev[:, :, :], op0=ALU.mult, op1=ALU.mult))
            then(dve.tensor_tensor(out=bt[:, :, :], in0=nrm[:, :, :], in1=av[:, :, :], op=ALU.mult))
            then(dve.tensor_tensor(out=bt[:, :, :], in0=bt[:, :, :], in1=en[:, :, :], op=ALU.mult))
            then(dve.tensor_tensor(out=rt[:, :, :], in0=r, in1=ew[:, :, :], op=ALU.mult))
            then(dve.tensor_tensor(out=kk[:, :, :], in0=r, in1=kt[:, :, :], op=ALU.mult))
            for q in range(4):
                ins = dve.tensor_scalar(kk[:, q, :], kk[:, q, :], col("rwkv_r_k", q), None, ALU.mult)
                if q < 3:
                    then(ins)
                else:
                    ins.then_inc(*rk_ready.post())
            then(dve.tensor_tensor(out=kt[:, :, :], in0=kt[:, :, :], in1=en[:, :, :], op=ALU.mult))
            dve.wait_ge(*bonus_ready.take(2))
            for q in range(2):
                then(dve.tensor_tensor(out=flat(bonus[:, 2 * q:2 * q + 2, :]), in0=bank[q][:, :], in1=flat(v[:, 2 * q:2 * q + 2, :]), op=ALU.mult))

        rwkv_chunks(K, st, con, at, bt, kt, rt, v, ew, y, link)

        ln = Norm(K, st, "rw", y, y, K.con["ones_pair"][:, :], 64, 64e-5)
        normed = new_signal(K, "rw_normed")

        @block.tensor
        def _(pe):
            ln.pe(pe)

        @block.scalar
        def _(act):
            ln.act(act)

        @block.vector
        def _(dve):
            then = linker(dve, link)

            ln.dve(dve, link, normed)
            dve.wait_ge(*normed.posted())
            for q in range(4):
                then(dve.tensor_scalar(y[:, q, :], y[:, q, :], col("rwkv_lnx_g", q), col("rwkv_lnx_b", q), ALU.mult, ALU.add))
            then(dve.tensor_tensor(out=y, in0=y, in1=bonus[:, :, :], op=ALU.add))
            then(dve.tensor_tensor(out=y, in0=y, in1=g[:, :, :], op=ALU.mult))
    end_stage(K)


def rwkv_chunks(K, st, con, at, bt, kt, rt, v, ew, y, link):
    nc, block, bank = K.nc, K.block, K.bank
    NCH = T1 // RC
    H = 4 * 160

    def sb(name, shape):
        return st.enter_context(nc.sbuf_tensor("rwkv_" + name, shape, F32))

    xar, xb, xk, xv = sb("ar_x", [P, 2, H]), sb("b_x", [P, H]), sb("k_x", [P, H]), sb("v_x", [P, H])
    state = sb("state", [P, 4, 64])
    mt_b, mt_k, m_b = sb("mt_b", [P, 2, P]), sb("mt_k", [P, 2, P]), sb("m_b", [P, P])
    v_rows, b_rows, k_rows = sb("v_rows", [P, 64]), sb("b_rows", [P, 4, P]), sb("k_rows", [P, 4, P])
    m2, m2t, m4, m4t, m8t = (sb(n, [P, P]) for n in ("m2", "m2t", "m4", "m4t", "m8t"))
    u = sb("u", [P, 64])
    ydup = sb("y_twice", [P, 2, 64])
    to_pe, to_dve, to_act, act_out = (new_signal(K, "rwc_" + n) for n in ("for_tensor", "for_vector", "for_scalar", "rows_copied"))
    chain, y_twice, y_turned = new_signal(K, "rwc_dve_chain"), new_signal(K, "rwc_y_twice"), new_signal(K, "rwc_y_turned")

    def tile(x, p):
        return x[:, p * P:(p + 1) * P]

    @block.tensor
    def _(pe):
        with pe.Fori(0, NCH) as i:
            to_pe.begin(i, 7)
            act_out.begin(i, 1)
            y_twice.begin(i, 1)
            pe.wait_ge(*to_pe.take())
            for p in range(4):
                ax = xar[:, :, p * P:(p + 1) * P]
                nc.tensor.matmul(bank[0][:, 0:256].rearrange("p (a n) -> p a n", a=2), tile(xb, p), ax, start=p == 0, stop=p == 3)
            for p in range(4):
                ax = xar[:, :, p * P:(p + 1) * P]
                nc.tensor.matmul(bank[1][:, 0:256].rearrange("p (a n) -> p a n", a=2), tile(xk, p), ax, start=p == 0, stop=p == 3)
            for p in range(4):
                ins = nc.tensor.matmul(bank[2][:, 0:P], xar[:, 0, p * P:(p + 1) * P], tile(xb, p), start=p == 0, stop=p == 3)
            ins.then_inc(*to_dve.post())
            for p in range(4):
                nc.tensor.matmul(bank[3][:, 0:64], tile(xv, p), con["stacked_eye"][:, :], start=p == 0, stop=p == 3)
            for p in range(4):
                nc.tensor.transpose(bank[4][:, p * P:(p + 1) * P], tile(xb, p), K.con["eye"][:, :])
            for p in range(4):
                ins = nc.tensor.transpose(bank[5][:, p * P:(p + 1) * P], tile(xk, p), K.con["eye"][:, :])
            ins.then_inc(*to_act.post())
            for p in range(4):
                nc.tensor.matmul(bank[6][:, 0:64], xar[:, 0, p * P:(p + 1) * P], state[:, p, :], start=p == 0, stop=False)
            pe.wait_ge(*to_pe.take())
            pe.wait_ge(*act_out.take())
            nc.tensor.matmul(bank[6][:, 0:64], mt_k[:, 0, :], v_rows[:, :], start=False, stop=True)
            nc.tensor.matmul(bank[0][:, 0:P], mt_b[:, 0, :], m_b[:, :], start=True, stop=True)
            nc.tensor.matmul(bank[1][:, 0:P], m_b[:, :], mt_b[:, 0, :], start=True, stop=True).then_inc(*to_dve.post())
            pe.wait_ge(*to_pe.take())
            nc.tensor.matmul(bank[6][:, 64:128], mt_b[:, 0, :], u[:, :], start=True, stop=True)
            nc.tensor.matmul(bank[2][:, 0:P], m2t[:, :], m2[:, :], start=True, stop=True)
            nc.tensor.matmul(bank[3][:, 0:P], m2[:, :], m2t[:, :], start=True, stop=True).then_inc(*to_dve.post())
            pe.wait_ge(*to_pe.take())
            nc.tensor.matmul(bank[6][:, 128:192], m2t[:, :], u[:, :], start=True, stop=True)
            nc.tensor.matmul(bank[0][:, 0:P], m4[:, :], m4t[:, :], start=True, stop=True).then_inc(*to_dve.post())
            pe.wait_ge(*to_pe.take())
            nc.tensor.matmul(bank[6][:, 192:256], m4t[:, :], u[:, :], start=True, stop=True).then_inc(*to_dve.post())
            pe.wait_ge(*to_pe.take())
            nc.tensor.matmul(bank[6][:, 256:320], m8t[:, :], u[:, :], start=True, stop=True).then_inc(*to_dve.post())
            pe.wait_ge(*to_pe.take())
            for p in range(4):
                nc.tensor.matmul(bank[7][:, 0:64], xar[:, 1, p * P:(p + 1) * P], state[:, p, :], start=p == 0, stop=False)
            nc.tensor.matmul(bank[7][:, 0:64], mt_b[:, 1, :], u[:, :], start=False, stop=False)
            nc.tensor.matmul(bank[7][:, 0:64], mt_k[:, 1, :], v_rows[:, :], start=False, stop=True)
            for p in range(4):
                nc.tensor.matmul(bank[1][:, p * 64:(p + 1) * 64], b_rows[:, p, :], u[:, :], start=True, stop=False)
                ins = nc.tensor.matmul(bank[1][:, p * 64:(p + 1) * 64], k_rows[:, p, :], v_rows[:, :], start=False, stop=True)
            ins.then_inc(*to_dve.post())
            pe.wait_ge(*y_twice.take())
            nc.tensor.matmul(bank[2][:, 0:P], ydup[:, :, :].rearrange("p a v -> p (a v)"), K.con["eye"][:, :], start=True, stop=True)\
                .then_inc(*y_turned.post())
            to_pe.end(NCH)
            act_out.end(NCH)
            y_twice.end(NCH)

    @block.scalar
    def _(act):
        with act.Fori(0, NCH) as i:
            to_act.begin(i, 1)
            act.wait_ge(*to_act.take())
            nc.scalar.activation(v_rows[:, :], bank[3][:, 0:64], ACT.Copy)
            nc.scalar.activation(flat(b_rows[:, :, :]), bank[4][:, :], ACT.Copy)
            nc.scalar.activation(flat(k_rows[:, :, :]), bank[5][:, :], ACT.Copy).then_inc(*act_out.post())
            to_act.end(NCH)

    @block.vector
    def _(dve):
        then = linker(dve, chain)

        for t in (xar, xb, xk, xv, state):
            then(dve.memset(t[...], 0.0))
        per = 3
        with dve.Fori(0, NCH) as i:
            to_dve.begin(i, 7)
            y_turned.begin(i, 1)
            chain.begin(i, per, posts=True)
            now = bass.ds(i * RC, RC)
            for half in (0, 1):
                rows = slice(64 * half, 64 * half + 64)
                for dst, src in ((xar[rows, 0, :], at), (xar[rows, 1, :], rt), (xb[rows, :], bt), (xk[rows, :], kt), (xv[rows, :], v)):
                    own = dst.rearrange("q (p s) -> q p s", s=160)[:, :, half * RC:half * RC + RC]
                    ins = dve.tensor_copy(own, src[rows, :, now])
            ins.then_inc(*to_pe.post())
            dve.wait_ge(*to_dve.take())
            dve.tensor_tensor(out=mt_b[:, 0, :], in0=bank[0][:, 0:P], in1=con["rwkv_strict"][:, :], op=ALU.mult)
            dve.tensor_tensor(out=mt_b[:, 1, :], in0=bank[0][:, P:2 * P], in1=con["rwkv_upto"][:, :], op=ALU.mult)
            dve.tensor_tensor(out=mt_k[:, 0, :], in0=bank[1][:, 0:P], in1=con["rwkv_strict"][:, :], op=ALU.mult)
            dve.tensor_tensor(out=mt_k[:, 1, :], in0=bank[1][:, P:2 * P], in1=con["rwkv_upto"][:, :], op=ALU.mult)
            dve.tensor_tensor(out=m_b[:, :], in0=bank[2][:, 0:P], in1=con["rwkv_below"][:, :], op=ALU.mult).then_inc(*to_pe.post())
            dve.wait_ge(*to_dve.take())
            dve.tensor_copy(u[:, :], bank[6][:, 0:64])
            dve.tensor_copy(m2[:, :], bank[0][:, 0:P])
            dve.tensor_copy(m2t[:, :], bank[1][:, 0:P]).then_inc(*to_pe.post())
            dve.wait_ge(*to_dve.take())
            dve.tensor_tensor(out=u[:, :], in0=u[:, :], in1=bank[6][:, 64:128], op=ALU.add)
            dve.tensor_copy(m4[:, :], bank[2][:, 0:P])
            dve.tensor_copy(m4t[:, :], bank[3][:, 0:P]).then_inc(*to_pe.post())
            dve.wait_ge(*to_dve.take())
            dve.tensor_tensor(out=u[:, :], in0=u[:, :], in1=bank[6][:, 128:192], op=ALU.add)
            dve.tensor_copy(m8t[:, :], bank[0][:, 0:P]).then_inc(*to_pe.post())
            dve.wait_ge(*to_dve.take())
            dve.tensor_tensor(out=u[:, :], in0=u[:, :], in1=bank[6][:, 192:256], op=ALU.add).then_inc(*to_pe.post())
            dve.wait_ge(*to_dve.take())
            dve.tensor_tensor(out=u[:, :], in0=u[:, :], in1=bank[6][:, 256:320], op=ALU.add).then_inc(*to_pe.post())
            dve.wait_ge(*to_dve.take())
            dve.tensor_copy(ydup[:, 0, :], bank[7][:, 0:64])
            dve.tensor_copy(ydup[:, 1, :], bank[7][:, 0:64]).then_inc(*y_twice.post())
            then(dve.tensor_tensor(out=flat(state[:, :, :]), in0=flat(state[:, :, :]), in1=bank[1][:, 0:256], op=ALU.add))
            decay = ew[:, :, bass.ds(i * RC + RC - 1, 1)].to_broadcast([P, 4, 64])
            then(dve.tensor_tensor(out=state[:, :, :], in0=state[:, :, :], in1=decay, op=ALU.mult))
            dve.wait_ge(*y_turned.take())
            turned = bank[2][:, 0:P].rearrange("q (p a t) -> q p a t", a=2, t=RC)
            for half in (0, 1):
                rows = slice(64 * half, 64 * half + 64)
                ins = dve.tensor_copy(y[rows, :, now], turned[rows, :, half, :])
            then(ins)
            to_dve.end(NCH)
            y_turned.end(NCH)
            chain.end(NCH, posts=True)


def hgrn_branch(K):
    nc, block, bank, col = K.nc, K.block, K.bank, K.col
    T = T1
    y = K.y_branch[:, 1]
    with ExitStack() as st:
        def sb(name, shape):
            return st.enter_context(nc.sbuf_tensor("hgrn_" + name, shape, F32))

        con = load_constants(K, st, "hgrn")
        loads = 16 * K.small_loads
        q, f, k, g = sb("q", [P, 4, T]), sb("f", [P, 4, T]), sb("k", [P, 4, T]), sb("g", [P, 4, T])
        v = sb("v", [P, 2, W])
        lf, c = sb("log_f", [P, 4, T]), sb("cum_log", [P, 4, T])
        eq, ek = sb("decay_q", [P, 4 * T]), sb("decay_k", [P, 4 * T])
        ql, kl = sb("q_level", [P, 4 * T]), sb("k_level", [P, 4 * T])
        attn, cross = sb("attn", [P, 8, P]), sb("attn_cross", [P, 4, P])
        part = sb("attn_part", [P, 4, P])
        z_ready, z_free = new_signal(K, "hg_z_ready"), new_signal(K, "hg_z_free")
        v_ready, v_free, inputs = new_signal(K, "hg_v_ready"), new_signal(K, "hg_v_free"), new_signal(K, "hg_inputs")
        diffs, exps, level_ready, level_done = (new_signal(K, "hg_" + n) for n in ("diffs", "exps", "level_ready", "level_done"))
        attn_ready, o_ready, normed = new_signal(K, "hg_attn_ready"), new_signal(K, "hg_o_ready"), new_signal(K, "hg_normed")
        cum = new_signal(K, "hg_cum")
        link, alink = new_signal(K, "hg_dve_chain"), new_signal(K, "hg_act_chain")
        dve_abs, act_log, dve_log = log_sigmoid(K, st, "hg", flat(f[:, :, :]), flat(lf[:, :, :]))
        rms = Norm(K, st, "hg", y, y, K.con["ones"][:, :], P, 1e-6, mean=False)

        @block.tensor
        def _(pe):
            stream_linear(K, pe, 12, lambda kt: K.x[:, kt, 0:T], DT, T, z_ready, z_free)
            stream_tokens(K, pe, lambda kt: K.x[:, kt, :], [(0, P), (P, P)], 4, v_ready, v_free, (4, 5))
            for level in range(9):
                pe.wait_ge(*level_ready.take())
                if level < 8:
                    for h in range(4):
                        for b in range(2):
                            at = h * T + b * P
                            ins = nc.tensor.matmul(bank[(2 * h + b) // 4 + 2 * (level % 2)][:, (2 * h + b) % 4 * P:(2 * h + b) % 4 * P + P],
                                                   kl[:, at:at + P], ql[:, at:at + P], start=True, stop=True)
                else:
                    for h in range(4):
                        ins = nc.tensor.matmul(bank[h // 4 + 2 * (level % 2)][:, h % 4 * P:h % 4 * P + P],
                                               kl[:, h * T:h * T + P], ql[:, h * T + P:h * T + 2 * P], start=True, stop=True)
                ins.then_inc(*level_done.post())
            pe.wait_ge(*attn_ready.take())
            for h in range(4):
                o = bank[4 + h // 2][:, h % 2 * T:(h % 2 + 1) * T]
                cols = slice(h * P, (h + 1) * P)
                nc.tensor.matmul(o[:, 0:P], v[:, 0, cols], attn[:, 2 * h, :], start=True, stop=True)
                nc.tensor.matmul(o[:, P:2 * P], v[:, 0, cols], cross[:, h, :], start=True, stop=False)
                ins = nc.tensor.matmul(o[:, P:2 * P], v[:, 1, cols], attn[:, 2 * h + 1, :], start=False, stop=True)
            ins.then_inc(*o_ready.post())
            rms.pe(pe)

        @block.scalar
        def _(act):
            for j in range(12):
                act.wait_ge(*z_ready.take())
                dst, fn = [(q, ACT.Silu), (f, ACT.Copy), (g, ACT.Silu)][j // 4]
                act.activation(dst[:, j % 4, :], bank[j % 4][:, 0:T], fn).then_inc(*z_free.post())
            for b in range(2):
                act.wait_ge(*v_ready.take())
                act.activation(v[:, b, :], bank[4 + b][:, :], ACT.Copy).then_inc(*v_free.post())
            act.wait_ge(*z_free.posted())
            act.activation(flat(k[:, :, :]), flat(f[:, :, :]), ACT.Sigmoid, scale=-1.0).then_inc(*inputs.post())
            act_log(act, alink)
            for level in range(1, 9):
                act.wait_ge(*diffs.take())
                half, size = 2 ** level // 2, 2 ** level
                right = eq[:, :].rearrange("p (b s) -> p b s", s=size)[:, :, half:size]
                left = ek[:, :].rearrange("p (b s) -> p b s", s=size)[:, :, 0:half]
                act.activation(right, right, ACT.Exp).then_inc(*alink.post())
                act.activation(left, left, ACT.Exp).then_inc(*exps.post())
            rms.act(act)

        def add_level(dve, then, level):
            dve.wait_ge(*level_done.take())
            mask = con["hgrn_levels"][:, level * P:(level + 1) * P].rearrange("p (a t) -> p a t", a=1).to_broadcast([P, 4, P]) if level < 8 else None
            for b in range(2):
                src = bank[b + 2 * (level % 2)][:, :].rearrange("p (a t) -> p a t", t=P)
                if level == 0:
                    then(dve.tensor_tensor(out=attn[:, 4 * b:4 * b + 4, :], in0=src, in1=mask, op=ALU.mult))
                elif level < 8:
                    then(dve.tensor_tensor(out=part[:, :, :], in0=src, in1=mask, op=ALU.mult))
                    then(dve.tensor_tensor(out=attn[:, 4 * b:4 * b + 4, :], in0=attn[:, 4 * b:4 * b + 4, :], in1=part[:, :, :], op=ALU.add))
                elif b == 0:
                    then(dve.tensor_copy(cross[:, :, :], src))

        @block.vector
        def _(dve):
            then = linker(dve, link)
            dve.wait_ge(K.small_loaded, loads)
            for t in (eq, ek, ql, kl):
                then(dve.memset(t[:, :], 0.0))
            dve.wait_ge(*inputs.take())
            dve_abs(dve)
            dve_log(dve, cum)
            dve.wait_ge(*cum.posted())
            for h in range(4):
                then(dve.tensor_tensor_scan(out=c[:, h, :], data0=con["restart_row"][:, :], data1=lf[:, h, :],
                                            initial=0.0, op0=ALU.mult, op1=ALU.add))
            qf, kf, cf = flat(q[:, :, :]), flat(k[:, :, :]), flat(c[:, :, :])
            for level in range(9):
                half, size = 2 ** level // 2, 2 ** level
                if level == 0:
                    then(dve.tensor_copy(ql[:, :], qf))
                    dve.tensor_copy(kl[:, :], kf).then_inc(*level_ready.post())
                else:
                    def halves(x):
                        b = x.rearrange("p (b s) -> p b s", s=size)
                        return b[:, :, 0:half], b[:, :, half:size], b[:, :, half - 1:half].to_broadcast([P, 4 * T // size, half])
                    left, right, middle = halves(cf)
                    then(dve.tensor_tensor(out=halves(eq[:, :])[1], in0=right, in1=middle, op=ALU.subtract))
                    dve.tensor_tensor(out=halves(ek[:, :])[0], in0=middle, in1=left, op=ALU.subtract).then_inc(*diffs.post())
                    add_level(dve, then, level - 1)
                    dve.wait_ge(*exps.take())
                    then(dve.tensor_tensor(out=halves(ql[:, :])[1], in0=halves(qf)[1], in1=halves(eq[:, :])[1], op=ALU.mult))
                    dve.tensor_tensor(out=halves(kl[:, :])[0], in0=halves(kf)[0], in1=halves(ek[:, :])[0], op=ALU.mult)\
                        .then_inc(*level_ready.post())
            add_level(dve, then, 8)
            dve.drain().then_inc(*attn_ready.post())
            dve.wait_ge(*o_ready.take())
            for b in range(2):
                then(dve.tensor_copy(flat(y[:, 2 * b:2 * b + 2, :]), bank[4 + b][:, :]))
            rms.dve(dve, link, normed)
            dve.wait_ge(*normed.posted())
            for h in range(4):
                then(dve.scalar_tensor_tensor(out=y[:, h, :], in0=y[:, h, :], scalar=col("hgrn_norm_w", h), in1=g[:, h, :],
                                              op0=ALU.mult, op1=ALU.mult))
    end_stage(K)


def conv(K, dve, then, x, out, n, w, b, T):
    for j in range(n):
        then(dve.tensor_scalar(out[:, j, :], x[:, j, 0:T], K.col(w, j), K.col(b, j), ALU.mult, ALU.add))
        for s in range(1, 4):
            then(dve.scalar_tensor_tensor(out=out[:, j, :], in0=x[:, j, s:s + T], scalar=K.col(w, s * n + j), in1=out[:, j, :],
                                          op0=ALU.mult, op1=ALU.add))


def mlstm_branch(K):
    nc, block, bank, col = K.nc, K.block, K.bank, K.col
    T = T1
    y = K.y_branch[:, 2]
    with ExitStack() as st:
        def sb(name, shape):
            return st.enter_context(nc.sbuf_tensor("mlstm_" + name, shape, F32))

        con = load_constants(K, st, "mlstm")
        wg, gb = sb("w_gates", [P, DT, 8]), sb("gate_bias", [4, 2])
        load(K, [(wg[:, :, :], K.dram["mlstm_w_gates"]), (gb[:, :], K.dram["mlstm_gate_bias"])])
        loads = 16 * K.small_loads
        z = sb("z", [P, 8, T + 3])
        qk = sb("qk", [P, 8, T])
        o = sb("o", [P, 4, T])
        v = sb("v", [P, 2, W])
        ig, fg, lf, fc, gs, mx = (sb(n, [4, T]) for n in ("i", "f", "log_f", "cum_f", "g", "max_g"))
        rows = sb("rows", [4, 2, T])
        g_cols = sb("g_cols", [P, 2, 4])
        mneg, emt = sb("neg_max", [P, 4, T]), sb("exp_neg_m", [P, 4, T])
        arg, wgt, s = sb("arg", [P, 8, T]), sb("weights", [P, 8, T]), sb("scores", [P, 8, T])
        den = sb("den", [P, 4, T])
        z_ready, z_free = new_signal(K, "ml_z_ready"), new_signal(K, "ml_z_free")
        v_ready, v_free = new_signal(K, "ml_v_ready"), new_signal(K, "ml_v_free")
        z_sb, convolved, qk_ready = new_signal(K, "ml_z_sb"), new_signal(K, "ml_convolved"), new_signal(K, "ml_qk_ready")
        gate_ready, gate_free = new_signal(K, "ml_gate_ready"), new_signal(K, "ml_gate_free")
        rows_ready, minus_m, em, bc_ready, bc_done = (new_signal(K, "ml_" + n) for n in ("rows_ready", "m", "exp_m", "rows_everywhere", "rows_copied"))
        arg_ready, w_ready, s_ready, s_done, h_ready, h_done, normed = \
            (new_signal(K, "ml_" + n) for n in ("arg", "weights", "products", "scores", "sums", "sums_read", "normed"))
        link, alink, fdone = new_signal(K, "ml_dve_chain"), new_signal(K, "ml_act_chain"), new_signal(K, "ml_log_f")
        dve_abs, act_log, dve_log = log_sigmoid(K, st, "ml", fg[:, :], lf[:, :])
        ln = Norm(K, st, "ml", y, y, K.con["ones"][:, :], P, 1e-6)

        @block.tensor
        def _(pe):
            stream_linear(K, pe, 12, lambda kt: K.x[:, kt, 0:T], DT, T, z_ready, z_free)
            stream_tokens(K, pe, lambda kt: K.x[:, kt, :], [(0, P), (P, P)], 4, v_ready, v_free, (4, 5))
            pe.wait_ge(K.small_loaded, loads)
            for f in range(2):
                for kt in range(DT):
                    ins = nc.tensor.matmul(bank[f][0:4, 0:T], wg[:, kt, 4 * f:4 * f + 4], K.x[:, kt, 0:T], start=kt == 0, stop=kt == DT - 1)
                ins.then_inc(*gate_ready.post())
            pe.wait_ge(*rows_ready.take())
            for b in range(2):
                nc.tensor.transpose(bank[0][:, 4 * b:4 * b + 4], gs[:, b * P:(b + 1) * P], K.con["eye"][0:4, 0:4])
            for h in range(4):
                ins = nc.tensor.matmul(bank[1 + h][:, :], con["row_select"][0:4, h * P:(h + 1) * P], rows[:, :, :].rearrange("p a t -> p (a t)"),
                                       start=True, stop=True)
            ins.then_inc(*bc_ready.post())
            pe.wait_ge(*qk_ready.take())
            pe.wait_ge(*bc_done.take())
            for h in range(4):
                for b in range(2):
                    ins = nc.tensor.matmul(bank[h][:, b * T:(b + 1) * T], qk[:, 4 + h, b * P:(b + 1) * P], qk[:, h, :], start=True, stop=True)
            ins.then_inc(*s_ready.post())
            pe.wait_ge(*s_done.take())
            for h in range(4):
                for b in range(2):
                    nc.tensor.matmul(bank[4 + h][:, 0:T], v[:, b, h * P:(h + 1) * P], s[:, 2 * h + b, :], start=b == 0, stop=b == 1)
                for b in range(2):
                    ins = nc.tensor.matmul(bank[4 + h][:, T:2 * T], K.con["ones"][:, :], s[:, 2 * h + b, :], start=b == 0, stop=b == 1)
            ins.then_inc(*h_ready.post())
            pe.wait_ge(*h_done.take())
            ln.pe(pe)

        @block.scalar
        def _(act):
            for j in range(12):
                act.wait_ge(*z_ready.take())
                if j < 8:
                    act.activation(z[:, j, 3:T + 3], bank[j % 4][:, 0:T], ACT.Copy).then_inc(*z_free.post())
                else:
                    act.activation(o[:, j - 8, :], bank[j % 4][:, 0:T], ACT.Sigmoid).then_inc(*z_free.post())
            for b in range(2):
                act.wait_ge(*v_ready.take())
                act.activation(v[:, b, :], bank[4 + b][:, :], ACT.Copy).then_inc(*v_free.post())
            act.drain().then_inc(*z_sb.post())
            act.wait_ge(K.small_loaded, loads)
            act.wait_ge(*gate_ready.take(2))
            act.activation(ig[:, :], bank[0][0:4, 0:T], ACT.Identity, bias=gb[:, 0:1]).then_inc(*alink.post())
            act.activation(fg[:, :], bank[1][0:4, 0:T], ACT.Identity, bias=gb[:, 1:2]).then_inc(*gate_free.post())
            act_log(act, alink)
            act.wait_ge(*minus_m.take())
            act.activation(rows[:, 1, :], rows[:, 1, :], ACT.Exp).then_inc(*em.post())
            act.wait_ge(*convolved.take())
            act.activation(flat(qk[:, :, :]), flat(qk[:, :, :]), ACT.Silu).then_inc(*alink.post())
            act.wait_ge(*alink.posted())
            act.activation(flat(qk[:, 4:8, :]), flat(qk[:, 4:8, :]), ACT.Copy, scale=P ** -0.5).then_inc(*qk_ready.post())
            act.wait_ge(*arg_ready.take())
            for h in range(4):
                for b in range(2):
                    ins = act.activation(wgt[:, 2 * h + b, :], arg[:, 2 * h + b, :], ACT.Exp, bias=g_cols[:, b, h:h + 1])
            ins.then_inc(*w_ready.post())
            ln.act(act)

        @block.vector
        def _(dve):
            then = linker(dve, link)
            then(dve.memset(z[:, :, 0:3], 0.0))
            dve.wait_ge(*z_sb.take())
            dve.wait_ge(*gate_free.take())
            dve.wait_ge(K.small_loaded, loads)
            dve_abs(dve)
            dve_log(dve, fdone)
            dve.wait_ge(*fdone.posted())
            ones = K.con["ones"][0:4, 0:1].to_broadcast([4, T])
            then(dve.tensor_tensor_scan(out=fc[:, :], data0=ones, data1=lf[:, :], initial=0.0, op0=ALU.mult, op1=ALU.add))
            then(dve.tensor_tensor(out=gs[:, :], in0=ig[:, :], in1=fc[:, :], op=ALU.subtract))
            then(dve.tensor_tensor_scan(out=mx[:, :], data0=ones, data1=gs[:, :], initial=-3e38, op0=ALU.mult, op1=ALU.max))
            then(dve.tensor_scalar(rows[:, 0, :], mx[:, :], -1.0, None, ALU.mult))
            dve.tensor_tensor(out=rows[:, 1, :], in0=rows[:, 0, :], in1=fc[:, :], op=ALU.subtract).then_inc(*minus_m.post())
            dve.wait_ge(*em.take())
            dve.drain().then_inc(*rows_ready.post())
            conv(K, dve, then, z, qk, 8, "mlstm_conv_w", "mlstm_conv_b", T)
            dve.drain().then_inc(*convolved.post())
            dve.wait_ge(*bc_ready.take())
            then(dve.tensor_copy(g_cols[:, :, :].rearrange("p a h -> p (a h)"), bank[0][:, 0:8]))
            for h in range(4):
                for b in range(2):
                    then(dve.tensor_tensor(out=arg[:, 2 * h + b, :], in0=bank[1 + h][:, 0:T], in1=con["mlstm_mask"][:, b * T:(b + 1) * T], op=ALU.add))
                then(dve.tensor_copy(emt[:, h, :], bank[1 + h][:, T:2 * T]))
            dve.drain().then_inc(*arg_ready.post())
            dve.drain().then_inc(*bc_done.post())
            dve.wait_ge(*s_ready.take())
            dve.wait_ge(*w_ready.take())
            for h in range(4):
                ins = dve.tensor_tensor(out=flat(s[:, 2 * h:2 * h + 2, :]), in0=bank[h][:, :], in1=flat(wgt[:, 2 * h:2 * h + 2, :]), op=ALU.mult)
            ins.then_inc(*s_done.post())
            dve.wait_ge(*h_ready.take())
            for h in range(4):
                then(dve.tensor_copy(den[:, h, :], bank[4 + h][:, T:2 * T]))
                then(dve.scalar_tensor_tensor(out=den[:, h, :], in0=den[:, h, :], scalar=-1.0, in1=den[:, h, :], op0=ALU.mult, op1=ALU.max))
            then(dve.tensor_tensor(out=den[:, :, :], in0=den[:, :, :], in1=emt[:, :, :], op=ALU.max))
            then(dve.reciprocal(den[:, :, :], den[:, :, :]))
            for h in range(4):
                then(dve.tensor_tensor(out=y[:, h, :], in0=bank[4 + h][:, 0:T], in1=den[:, h, :], op=ALU.mult))
            dve.drain().then_inc(*h_done.post())
            ln.dve(dve, link, normed)
            dve.wait_ge(*normed.posted())
            for h in range(4):
                then(dve.scalar_tensor_tensor(out=y[:, h, :], in0=y[:, h, :], scalar=col("mlstm_norm_w", h), in1=o[:, h, :],
                                              op0=ALU.mult, op1=ALU.mult))
    end_stage(K)


def lru_branch(K):
    nc, block, bank, col = K.nc, K.block, K.bank, K.col
    T = T1
    y = K.y_branch[:, 3]
    with ExitStack() as st:
        def sb(name, shape):
            return st.enter_context(nc.sbuf_tensor("lru_" + name, shape, F32))

        wx = sb("wx_wa", [P, 8, P])
        load(K, [(wx[:, :, :], K.dram["lru_w"])])
        loads = 16 * K.small_loads
        z, xc = sb("z", [P, 4, T + 3]), sb("convolved", [P, 4, T])
        gelu, gx, ga = sb("gelu", [P, 4, T]), sb("gate_x", [P, 4, T]), sb("gate_a", [P, 4, T])
        a, m, r = sb("a", [P, 4, T]), sb("mult", [P, 4, T]), sb("r", [P, 4, T])
        ls = sb("log_sig_lambda", [P, 4])
        z_ready, z_free, z_sb, convolved = (new_signal(K, "lr_" + n) for n in ("z_ready", "z_free", "z_sb", "convolved"))
        g_ready, g_free, g_sb = new_signal(K, "lr_gates_ready"), new_signal(K, "lr_gates_free"), new_signal(K, "lr_gates_sb")
        la, exps, var, root = (new_signal(K, "lr_" + n) for n in ("log_a", "exps", "one_minus", "root"))
        link, alink, ldone = new_signal(K, "lr_dve_chain"), new_signal(K, "lr_act_chain"), new_signal(K, "lr_lambda")
        lam = K.cols[:, COL_AT["lru_lambda"]:COL_AT["lru_lambda"] + 4]
        dve_abs, act_log, dve_log = log_sigmoid(K, st, "lr", lam, ls[:, :])

        @block.tensor
        def _(pe):
            stream_linear(K, pe, 8, lambda kt: K.x[:, kt, 0:T], DT, T, z_ready, z_free)
            pe.wait_ge(K.small_loaded, loads)
            pe.wait_ge(*convolved.take())
            for j in range(8):
                if j >= 4:
                    pe.wait_ge(*g_free.take())
                nc.tensor.matmul(bank[j % 4][:, 0:T], wx[:, j, :], xc[:, j % 4, :], start=True, stop=True).then_inc(*g_ready.post())
            pe.wait_ge(*g_free.take(4))

        @block.scalar
        def _(act):
            act_log(act, alink)
            for j in range(8):
                act.wait_ge(*z_ready.take())
                if j < 4:
                    act.activation(z[:, j, 3:T + 3], bank[j % 4][:, 0:T], ACT.Copy).then_inc(*z_free.post())
                else:
                    act.activation(gelu[:, j - 4, :], bank[j % 4][:, 0:T], ACT.Gelu_apprx_tanh).then_inc(*z_free.post())
            act.drain().then_inc(*z_sb.post())
            for j in range(8):
                act.wait_ge(*g_ready.take())
                act.activation((gx if j < 4 else ga)[:, j % 4, :], bank[j % 4][:, 0:T], ACT.Sigmoid,
                               bias=col("lru_bx" if j < 4 else "lru_ba", j % 4)).then_inc(*g_free.post())
            act.drain().then_inc(*g_sb.post())
            act.wait_ge(*la.take())
            act.activation(flat(m[:, :, :]), flat(a[:, :, :]), ACT.Tanh).then_inc(*alink.post())
            act.wait_ge(*alink.posted())
            act.activation(flat(a[:, :, :]), flat(a[:, :, :]), ACT.Exp).then_inc(*exps.post())
            act.wait_ge(*var.take())
            act.activation(flat(m[:, :, :]), flat(m[:, :, :]), ACT.Sqrt).then_inc(*root.post())

        @block.vector
        def _(dve):
            then = linker(dve, link)
            dve_abs(dve)
            dve_log(dve, ldone)
            dve.wait_ge(*ldone.posted())
            then(dve.memset(z[:, :, 0:3], 0.0))
            dve.wait_ge(*z_sb.take())
            conv(K, dve, then, z, xc, 4, "lru_conv_w", "lru_conv_b", T)
            dve.drain().then_inc(*convolved.post())
            dve.wait_ge(*g_sb.take())
            for j in range(4):
                then(dve.tensor_scalar(a[:, j, :], ga[:, j, :], ls[:, j:j + 1], 8.0, ALU.mult, ALU.mult))
            dve.drain().then_inc(*la.post())
            then(dve.tensor_tensor(out=gx[:, :, :], in0=gx[:, :, :], in1=xc[:, :, :], op=ALU.mult))
            dve.wait_ge(*exps.take())
            then(dve.tensor_scalar(r[:, :, :], m[:, :, :], -1.0, 1.0, ALU.mult, ALU.add))
            then(dve.reciprocal(r[:, :, :], r[:, :, :]))
            dve.scalar_tensor_tensor(out=m[:, :, :], in0=m[:, :, :], scalar=-2.0, in1=r[:, :, :], op0=ALU.mult, op1=ALU.mult).then_inc(*var.post())
            dve.wait_ge(*root.take())
            then(dve.memset(m[:, :, 0:1], 1.0))
            then(dve.tensor_tensor(out=m[:, :, :], in0=m[:, :, :], in1=gx[:, :, :], op=ALU.mult))
            for j in range(4):
                then(dve.tensor_tensor_scan(out=r[:, j, :], data0=a[:, j, :], data1=m[:, j, :], initial=0.0, op0=ALU.mult, op1=ALU.add))
            then(dve.tensor_tensor(out=y, in0=r[:, :, :], in1=gelu[:, :, :], op=ALU.mult))
    end_stage(K)


def merge(K):
    nc, block, bank, col = K.nc, K.block, K.bank, K.col
    T = T1
    with ExitStack() as st:
        def sb(name, shape):
            return st.enter_context(nc.sbuf_tensor("merge_" + name, shape, F32))

        gate, prod = sb("gate", [P, 2, T]), sb("product", [P, 2, T])
        merged = sb("merged", [P, DT, T])
        g_ready, b_ready, g_sb, b_free = (new_signal(K, "mg_" + n) for n in ("gate_ready", "branch_ready", "gate_sb", "branch_free"))
        p_free, merged_ready, o_ready, o_free, normed = (new_signal(K, "mg_" + n) for n in ("gate_free", "merged", "out_ready", "out_free", "normed"))
        link = new_signal(K, "mg_dve_chain")
        g_free = g_sb.reader()
        x = K.x[:, :, 0:T]
        ln = Norm(K, st, "l1", x, x, K.con["ones"][:, :], D, 1e-5, whole=True)

        @block.tensor
        def _(pe):
            for i in range(4 * DT):
                if i >= 2:
                    pe.wait_ge(*g_free.take())
                for k in range(DT):
                    matmul(K, bank[i % 2][:, 0:T], K.weights.take(pe), K.x[:, k, 0:T], k == 0, k == DT - 1, g_ready if k == DT - 1 else None)
                if i >= 2:
                    pe.wait_ge(*b_free.take())
                for k in range(WT):
                    matmul(K, bank[2 + i % 2][:, 0:T], K.weights.take(pe), K.y_branch[:, i % 4, k, :], k == 0, k == WT - 1,
                           b_ready if k == WT - 1 else None)
            pe.wait_ge(*g_free.take(2))
            pe.wait_ge(*b_free.take(2))
            pe.wait_ge(*merged_ready.take())
            stream_linear(K, pe, DT, lambda k: merged[:, k, :], DT, T, o_ready, o_free)
            ln.pe(pe)

        @block.scalar
        def _(act):
            for i in range(4 * DT):
                act.wait_ge(*g_ready.take())
                if i >= 2:
                    act.wait_ge(*p_free.take())
                act.activation(gate[:, i % 2, :], bank[i % 2][:, 0:T], ACT.Sigmoid).then_inc(*g_sb.post())
            act.wait_ge(*p_free.take(2))
            ln.act(act)

        @block.vector
        def _(dve):
            then = linker(dve, link)
            for i in range(4 * DT):
                d, n = divmod(i, 4)
                dve.wait_ge(*g_sb.take())
                dve.wait_ge(*b_ready.take())
                dst = merged[:, d, :] if n == 0 else prod[:, i % 2, :]
                dve.tensor_tensor(out=dst, in0=bank[2 + i % 2][:, 0:T], in1=gate[:, i % 2, :], op=ALU.mult).then_inc(*b_free.post())
                dve.wait_ge(*b_free.posted())
                if n:
                    ins = dve.tensor_tensor(out=merged[:, d, :], in0=merged[:, d, :], in1=prod[:, i % 2, :], op=ALU.add)
                else:
                    ins = dve.engine_nop()
                ins.then_inc(*p_free.post())
                dve.wait_ge(*p_free.posted())
            dve.drain().then_inc(*merged_ready.post())
            for j in range(DT):
                dve.wait_ge(*o_ready.take())
                dve.scalar_tensor_tensor(out=x[:, j, :], in0=x[:, j, :], scalar=ALPHA, in1=bank[j % 4][:, 0:T], op0=ALU.mult, op1=ALU.add)\
                    .then_inc(*o_free.post())
            dve.wait_ge(*o_free.posted())
            ln.dve(dve, link, normed)
            dve.wait_ge(*normed.posted())
            for j in range(DT):
                then(dve.tensor_scalar(x[:, j, :], x[:, j, :], col("ln1_g", j), col("ln1_b", j), ALU.mult, ALU.add))
    end_stage(K)


def router_and_ple(K):
    nc, block, bank = K.nc, K.block, K.bank
    T = T1
    with ExitStack() as st:
        def sb(name, shape):
            return st.enter_context(nc.sbuf_tensor("router_" + name, shape, F32))

        rw, rb = sb("w", [P, DT, NE]), sb("bias", [P, NE])
        p_in, bd = sb("p", [P, 2, T]), sb("b_down", [NE, D])
        load(K, [(rw[:, :, :], K.dram["router_w"]), (rb[:, :], K.dram["router_b"]), (p_in[:, :, :], K.dram["p"]),
                 (bd[:, :], K.dram["expert_b_down"])])
        logits, rest, e = sb("logits", [P, 2, NE]), sb("rest", [P, 2, NE]), sb("exp", [P, 2, NE])
        top, first, total = sb("top", [P, 2, 8]), sb("neg_first", [P, 2]), sb("total", [P, 2])
        sig = sb("ple_gate", [P, DT, T])
        lg_ready, shifted, exps, gates_rows, turned, gates_ready = \
            (new_signal(K, "rt_" + n) for n in ("logits", "top", "exps", "gates", "turned", "gates_in_place"))
        chosen, placed, rows_ready, rows_done = (new_signal(K, "rt_" + n) for n in ("chosen", "places", "token_rows", "rows_copied"))
        con = load_constants(K, st, "router")
        loads = 16 * K.small_loads
        g_ready, g_free, p_ready, p_free, b_ready, b_free = \
            (new_signal(K, "rt_" + n) for n in ("ple_gate_ready", "ple_gate_free", "ple_ready", "ple_free", "bias_ready", "bias_free"))
        link = new_signal(K, "rt_dve_chain")
        sig_sb = g_free.reader()

        @block.tensor
        def _(pe):
            pe.wait_ge(K.small_loaded, loads)
            for b in range(2):
                for k in range(DT):
                    ins = nc.tensor.matmul(bank[4 + b][:, 0:NE], K.x[:, k, b * P:(b + 1) * P], rw[:, k, :], start=k == 0, stop=k == DT - 1)
                ins.then_inc(*lg_ready.post())
            stream_linear(K, pe, DT, lambda k: K.x[:, k, 0:T], DT, T, g_ready, g_free)
            stream_linear(K, pe, DT, lambda k: p_in[:, k, :], 2, T, p_ready, p_free)
            for b in range(2):
                for half in range(2):
                    for k in range(4):
                        ins = nc.tensor.transpose(bank[4 + half][:, k * P:(k + 1) * P], K.x[:, 4 * half + k, b * P:(b + 1) * P], K.con["eye"][:, :])
                ins.then_inc(*rows_ready.post())
                pe.wait_ge(*rows_done.take())
            pe.wait_ge(*chosen.take())
            nc.tensor.matmul(bank[6][:, 0:NE], con["before"][:, :], K.chosen[:, 0, 0:NE], start=True, stop=True)
            nc.tensor.matmul(bank[6][:, NE:2 * NE], K.con["ones"][:, :], K.chosen[:, 0, 0:NE], start=True, stop=False)
            nc.tensor.matmul(bank[6][:, NE:2 * NE], con["before"][:, :], K.chosen[:, 1, 0:NE], start=False, stop=True)
            for b in range(2):
                ins = nc.tensor.matmul(bank[6][:, 2 * NE:3 * NE], K.con["ones"][:, :], K.chosen[:, b, 0:NE], start=b == 0, stop=b == 1)
            ins.then_inc(*placed.post())
            pe.wait_ge(*gates_rows.take())
            for b in range(2):
                ins = nc.tensor.transpose(bank[4][0:NE, b * P:(b + 1) * P], K.gates_rows[:, b, 0:NE], K.con["eye"][:, :])
            ins.then_inc(*turned.post())
            pe.wait_ge(*gates_ready.take())
            for j in range(DT):
                if j >= 4:
                    pe.wait_ge(*b_free.take())
                nc.tensor.matmul(bank[j % 4][:, 0:T], bd[:, j * P:(j + 1) * P], K.gates[:, :], start=True, stop=True).then_inc(*b_ready.post())
            pe.wait_ge(*b_free.take(4))

        @block.scalar
        def _(act):
            act.wait_ge(*shifted.take())
            for b in range(2):
                ins = act.activation(e[:, b, :], logits[:, b, :], ACT.Exp, bias=first[:, b:b + 1])
            ins.then_inc(*exps.post())
            for j in range(DT):
                act.wait_ge(*g_ready.take())
                act.activation(sig[:, j, :], bank[j % 4][:, 0:T], ACT.Sigmoid).then_inc(*g_free.post())
            for b in range(2):
                act.wait_ge(*rows_ready.take())
                act.activation(K.x_rows[:, b, 0:512], bank[4][:, :], ACT.Copy)
                act.activation(K.x_rows[:, b, 512:1024], bank[5][:, :], ACT.Copy).then_inc(*rows_done.post())

        @block.vector
        def _(dve):
            then = linker(dve, link)
            dve.wait_ge(K.small_loaded, loads)
            dve.wait_ge(*lg_ready.take(2))
            for b in range(2):
                then(dve.tensor_tensor(out=logits[:, b, :], in0=bank[4 + b][:, 0:NE], in1=rb[:, :], op=ALU.add))
                then(dve.max(top[:, b, :], logits[:, b, :]))
                then(dve.tensor_scalar(first[:, b:b + 1], top[:, b, 0:1], -1.0, None, ALU.mult))
                then(dve.memset(top[:, b, 4:8], -3e38))
                then(dve.match_replace(rest[:, b, :], in_to_replace=top[:, b, :], in_values=logits[:, b, :], imm_value=-3e38))
            dve.tensor_tensor(out=K.chosen[:, :, 0:NE], in0=rest[:, :, :], in1=logits[:, :, :], op=ALU.not_equal).then_inc(*chosen.post())
            dve.wait_ge(*chosen.posted())
            dve.drain().then_inc(*shifted.post())
            dve.wait_ge(*exps.take())
            then(dve.tensor_tensor(out=e[:, :, :], in0=e[:, :, :], in1=K.chosen[:, :, 0:NE], op=ALU.mult))
            then(dve.tensor_reduce(out=total[:, :], in_=e[:, :, :], axis=AX.X, op=ALU.add))
            then(dve.reciprocal(total[:, :], total[:, :]))
            for b in range(2):
                ins = dve.tensor_scalar(K.gates_rows[:, b, 0:NE], e[:, b, :], total[:, b:b + 1], None, ALU.mult)
            ins.then_inc(*gates_rows.post())
            for j in range(DT):
                dve.wait_ge(*sig_sb.take())
                dve.wait_ge(*p_ready.take())
                dve.tensor_tensor(out=sig[:, j, :], in0=sig[:, j, :], in1=bank[j % 4][:, 0:T], op=ALU.mult).then_inc(*p_free.post())
            dve.wait_ge(*p_free.posted())
            then(dve.scalar_tensor_tensor(out=K.acc[:, :, :], in0=K.x[:, :, 0:T], scalar=ALPHA, in1=sig[:, :, :], op0=ALU.mult, op1=ALU.add))
            dve.wait_ge(*placed.take())
            then(dve.tensor_copy(K.place[:, :, 0:NE], bank[6][:, 0:2 * NE].rearrange("p (b e) -> p b e", b=2)))
            for t in (K.chosen, K.place, K.gates_rows):
                then(dve.memset(t[:, :, NE:NE + 1], 0.0))
            then(dve.tensor_copy(K.load_of[:, :], bank[6][:, 2 * NE:3 * NE]))
            dve.wait_ge(*turned.take())
            dve.tensor_copy(K.gates[:, :], bank[4][0:NE, 0:T]).then_inc(*gates_ready.post())
            for j in range(DT):
                dve.wait_ge(*b_ready.take())
                dve.tensor_tensor(out=K.acc[:, j, :], in0=K.acc[:, j, :], in1=bank[j % 4][:, 0:T], op=ALU.add).then_inc(*b_free.post())
    end_stage(K)


def experts(K):
    nc, block, bank = K.nc, K.block, K.bank
    T, S, HW = T1, SLOTS_SMALL, D // 2
    with ExitStack() as st:
        def sb(name, shape):
            return st.enter_context(nc.sbuf_tensor("expert_" + name, shape, F32))

        con = load_constants(K, st, "experts")
        bgu = sb("b_gu", [NE, 2 * D])
        load(K, [(bgu[:, :], K.dram["expert_b_gu"])])
        loads = 16 * K.small_loads
        sel = sb("select", [NE, P])
        pick, spread = sb("pick", [P, 2, S]), sb("spread_rows", [P, 2, 2, S])
        spread_t, xs, xt = sb("spread", [P, T]), sb("x_slots", [P, HW]), sb("x_slots_t", [P, 4, P])
        ht_few, ys = sb("hidden_slots_t", [P, 4, P]), sb("y_slots", [P, HW])
        gate, sg, h = sb("gate_part", [P, 4, HW]), sb("sigmoid", [P, 4, HW]), sb("hidden", [P, 4, HW])
        ht, pad = sb("hidden_t", [P, DT, T]), sb("pad", [P, 8])
        sel_ready, pick_ready, spread_ready, gathered, xs_sb, xt_ready, xt_sb, gate_ready, up_ready, gate_sb, sig_ready, h_ready, ht_ready, ht_sb, y_ready, ys_sb, \
            out_ready, link = (new_signal(K, "ex_" + n) for n in (
                "select", "pick", "spread", "gathered", "x_slots_sb", "x_turned", "x_turned_sb", "gate_ready", "up_ready", "gate_sb", "sigmoid", "hidden",
                "hidden_turned", "hidden_turned_sb", "y_ready", "y_slots_sb", "out_ready", "dve_chain"))
        assert K.weights.at % (CHUNK_TILES * SLOTS) == 0
        LINKS = 6
        rows = (slice(0, S), slice(S, 2 * S))

        def both(eng, i, signals, body):
            tokens = eng.value_load(K.load_of[0:1, bass.ds(i, 1)], min_val=0, max_val=T)
            saved, at, pending = counters(signals), K.weights.at, K.weights.pending
            with eng.If(tokens < FEW + 1):
                body(True)
            ended = counters(signals)
            set_counters(signals, saved)
            if eng is nc.tensor:
                K.weights.at, K.weights.pending = at, pending
            with eng.Else():
                body(False)
            assert counters(signals) == ended, (counters(signals), ended)

        def few_linear(pe, out, x, bias, signal):
            for g in range(2):
                if bias is not None:
                    matmul(K, out[rows[g], :], sel[:, 0:S], bgu[:, bias + g * HW:bias + (g + 1) * HW], True, False)
            for k in range(DT):
                w = K.weights.take(pe, DT)
                for g in range(2):
                    matmul(K, out[rows[g], :], x[:, k % 4, k // 4 * S:k // 4 * S + S], w[:, g * HW:(g + 1) * HW],
                           bias is None and k == 0, k == DT - 1, signal if g and k == DT - 1 else None)

        def many_linear(pe, out, x, bias, signal):
            for b in range(2):
                for g in range(2):
                    if bias is not None:
                        matmul(K, bank[out + 2 * b + g][:, :], sel[:, :], bgu[:, bias + g * HW:bias + (g + 1) * HW], True, False)
            for k in range(DT):
                w = K.weights.take(pe, DT)
                for b in range(2):
                    for g in range(2):
                        matmul(K, bank[out + 2 * b + g][:, :], x(k)[:, b * P:(b + 1) * P], w[:, g * HW:(g + 1) * HW],
                               bias is None and k == 0, k == DT - 1, signal if b and g and k == DT - 1 else None)

        @block.tensor
        def _(pe):
            eye = K.con["eye"][:, :]

            def gather_next(pe):
                pe.wait_ge(*pick_ready.take())
                for b in range(2):
                    for g in range(2):
                        ins = nc.tensor.matmul(bank[3][rows[g], :], pick[:, b, :], K.x_rows[:, b, g * HW:(g + 1) * HW], start=b == 0, stop=b == 1)
                ins.then_inc(*gathered.post())

            def turn_next(pe):
                pe.wait_ge(*xs_sb.take())
                for j in range(4):
                    ins = nc.tensor.transpose(bank[4][:, j * P:(j + 1) * P], xs[:, j * P:(j + 1) * P], eye)
                ins.then_inc(*xt_ready.post())

            def few(pe):
                pe.wait_ge(*sel_ready.take())
                pe.wait_ge(*xt_sb.take())
                few_linear(pe, bank[0], xt, 0, gate_ready)
                few_linear(pe, bank[1], xt, D, up_ready)
                pe.wait_ge(*spread_ready.take())
                for b in range(2):
                    nc.tensor.transpose(bank[2][:, b * P:(b + 1) * P], spread[:, b, :, :].rearrange("p a s -> p (a s)"), eye)
                gather_next(pe)
                pe.wait_ge(*h_ready.take())
                for j in range(4):
                    ins = nc.tensor.transpose(bank[5][:, j * P:(j + 1) * P], h[:, 0, j * P:(j + 1) * P], eye)
                ins.then_inc(*ht_ready.post())
                turn_next(pe)
                pe.wait_ge(*ht_sb.take())
                few_linear(pe, bank[2], ht_few, None, y_ready)
                pe.wait_ge(*ys_sb.take())
                for b in range(2):
                    for g in range(2):
                        ins = nc.tensor.matmul(bank[4 + 2 * b + g][:, :], spread_t[rows[g], b * P:(b + 1) * P], ys[rows[g], :], start=True, stop=True)
                ins.then_inc(*out_ready.post())

            def many(pe):
                pe.wait_ge(*sel_ready.take())
                pe.wait_ge(*xt_sb.take())
                many_linear(pe, 0, lambda k: K.x[:, k, 0:T], 0, gate_ready)
                pe.wait_ge(*spread_ready.take())
                many_linear(pe, 4, lambda k: K.x[:, k, 0:T], D, up_ready)
                pe.wait_ge(*h_ready.take())
                gather_next(pe)
                turn_next(pe)
                for b in range(2):
                    for k in range(DT):
                        ins = nc.tensor.transpose(bank[2 * b + k // 4][:, k % 4 * P:(k % 4 + 1) * P], h[:, 2 * b + k // 4, k % 4 * P:(k % 4 + 1) * P], eye)
                ins.then_inc(*ht_ready.post())
                pe.wait_ge(*ht_sb.take())
                many_linear(pe, 4, lambda k: ht[:, k, :], None, y_ready)
                pe.wait_ge(*ys_sb.take())
                pe.nop().then_inc(*out_ready.post())

            taken = [(sel_ready, 1), (xs_sb, 1), (xt_sb, 1), (spread_ready, 1), (pick_ready, 1), (h_ready, 1), (ht_sb, 1), (ys_sb, 1)]
            posted = [gathered, xt_ready, gate_ready, up_ready, ht_ready, y_ready, out_ready]
            pe.wait_ge(K.small_loaded, loads)
            gather_next(pe)
            turn_next(pe)
            with pe.Fori(0, NE) as i:
                for q, n in taken:
                    q.begin(i, n)
                K.weights.turn = (i, EXPERT_TILES // CHUNK_TILES // SLOTS)
                both(pe, i, [q for q, _ in taken] + posted, lambda is_few: few(pe) if is_few else many(pe))
                K.weights.turn = None
                for q, _ in taken:
                    q.end(NE)
            K.weights.at += EXPERT_TILES * (NE - 1)

        @block.scalar
        def _(act):
            def copy_next(act):
                act.wait_ge(*xt_ready.take())
                act.activation(flat(xt[:, :, :]), bank[4][:, :], ACT.Copy).then_inc(*xt_sb.post())

            def few(act):
                act.wait_ge(*gate_sb.take())
                act.activation(sg[:, 0, :], gate[:, 0, :], ACT.Sigmoid, scale=1.702).then_inc(*sig_ready.post())
                act.wait_ge(*ht_ready.take())
                act.activation(flat(ht_few[:, :, :]), bank[5][:, :], ACT.Copy).then_inc(*ht_sb.post())
                copy_next(act)
                act.wait_ge(*y_ready.take())
                act.activation(ys[:, :], bank[2][:, :], ACT.Copy).then_inc(*ys_sb.post())

            def many(act):
                act.wait_ge(*gate_sb.take())
                act.activation(flat(sg[:, :, :]), flat(gate[:, :, :]), ACT.Sigmoid, scale=1.702).then_inc(*sig_ready.post())
                copy_next(act)
                act.wait_ge(*ht_ready.take())
                for b in range(2):
                    for half in range(2):
                        ins = act.activation(ht[:, 4 * half:4 * half + 4, b * P:(b + 1) * P],
                                             bank[2 * b + half][:, :].rearrange("p (k t) -> p k t", t=P), ACT.Copy)
                ins.then_inc(*ht_sb.post())
                act.wait_ge(*y_ready.take())
                act.nop().then_inc(*ys_sb.post())

            taken = [(xt_ready, 1), (gate_sb, 1), (ht_ready, 1), (y_ready, 1)]
            copy_next(act)
            with act.Fori(0, NE) as i:
                for q, n in taken:
                    q.begin(i, n)
                both(act, i, [q for q, _ in taken] + [xt_sb, sig_ready, ht_sb, ys_sb], lambda is_few: few(act) if is_few else many(act))
                for q, _ in taken:
                    q.end(NE)

        @block.vector
        def _(dve):
            then = linker(dve, link)
            dve.wait_ge(K.small_loaded, loads)
            then(dve.memset(K.moe[:, :, :], 0.0))

            def even_out(dve, before):
                while link.posts < before + LINKS:
                    dve.memset(pad[:, link.posts - before:link.posts - before + 1], 0.0).then_inc(*link.post())

            def pick_next(dve, e):
                for b in range(2):
                    ins = dve.tensor_scalar(pick[:, b, :], con["slots"][:, :], K.place[:, b, e], K.chosen[:, b, e], ALU.is_equal, ALU.mult)
                ins.then_inc(*pick_ready.post())

            def select_next(dve, e):
                dve.tensor_copy(sel[:, :], K.con["eye"][0:NE, e].to_broadcast([NE, P])).then_inc(*sel_ready.post())

            def few(dve, e, after):
                before = link.posts
                pick_next(dve, after)
                for b in range(2):
                    slots = con["slots"][:, :].rearrange("p (a s) -> p a s", a=1).to_broadcast([P, 2, S])
                    ins = dve.tensor_scalar(spread[:, b, :, :], slots, K.place[:, b, e], K.gates_rows[:, b, e], ALU.is_equal, ALU.mult)
                ins.then_inc(*spread_ready.post())
                dve.wait_ge(*gate_ready.take())
                dve.tensor_scalar(gate[:, 0, :], bank[0][:, :], 7.0, None, ALU.min).then_inc(*gate_sb.post())
                dve.wait_ge(*sig_ready.take())
                then(dve.tensor_tensor(out=gate[:, 0, :], in0=gate[:, 0, :], in1=sg[:, 0, :], op=ALU.mult))
                dve.wait_ge(*up_ready.take())
                then(dve.tensor_scalar(h[:, 0, :], bank[1][:, :], 7.0, -7.0, ALU.min, ALU.max))
                dve.scalar_tensor_tensor(out=h[:, 0, :], in0=h[:, 0, :], scalar=1.0, in1=gate[:, 0, :], op0=ALU.add, op1=ALU.mult)\
                   .then_inc(*h_ready.post())
                dve.wait_ge(*gathered.take())
                dve.tensor_copy(spread_t[:, :], bank[2][:, 0:T])
                dve.tensor_copy(xs[:, :], bank[3][:, :]).then_inc(*xs_sb.post())
                select_next(dve, after)
                dve.wait_ge(*out_ready.take())
                for n in range(4):
                    part = K.moe[:, n // 2, n % 2 * HW:(n % 2 + 1) * HW]
                    ins = dve.tensor_tensor(out=part, in0=part, in1=bank[4 + n][:, :], op=ALU.add)
                then(ins)
                even_out(dve, before)

            def many(dve, e, after):
                before = link.posts
                pick_next(dve, after)
                dve.memset(pad[:, 0:1], 0.0).then_inc(*spread_ready.post())
                dve.wait_ge(*gate_ready.take())
                for n in range(4):
                    ins = dve.tensor_scalar(gate[:, n, :], bank[n][:, :], 7.0, None, ALU.min)
                ins.then_inc(*gate_sb.post())
                dve.wait_ge(*sig_ready.take())
                then(dve.tensor_tensor(out=flat(gate[:, :, :]), in0=flat(gate[:, :, :]), in1=flat(sg[:, :, :]), op=ALU.mult))
                dve.wait_ge(*up_ready.take())
                for n in range(4):
                    ins = dve.tensor_scalar(h[:, n, :], bank[4 + n][:, :], 7.0, -7.0, ALU.min, ALU.max)
                then(ins)
                dve.scalar_tensor_tensor(out=flat(h[:, :, :]), in0=flat(h[:, :, :]), scalar=1.0, in1=flat(gate[:, :, :]), op0=ALU.add, op1=ALU.mult)\
                   .then_inc(*h_ready.post())
                dve.wait_ge(*gathered.take())
                dve.tensor_copy(xs[:, :], bank[3][:, :]).then_inc(*xs_sb.post())
                select_next(dve, after)
                dve.wait_ge(*out_ready.take())
                for n in range(4):
                    part = K.moe[:, n // 2, n % 2 * HW:(n % 2 + 1) * HW]
                    ins = dve.scalar_tensor_tensor(out=part, in0=bank[4 + n][:, :], scalar=K.gates_rows[:, n // 2, e], in1=part,
                                                   op0=ALU.mult, op1=ALU.add)
                then(ins)
                even_out(dve, before)

            taken = [(gathered, 1), (gate_ready, 1), (sig_ready, 1), (up_ready, 1), (out_ready, 1)]
            pick_next(dve, slice(0, 1))
            select_next(dve, slice(0, 1))
            dve.wait_ge(*gathered.take())
            dve.tensor_copy(xs[:, :], bank[3][:, :]).then_inc(*xs_sb.post())
            with dve.Fori(0, NE) as i:
                e, after = bass.ds(i, 1), bass.ds(i + 1, 1)
                for q, n in taken:
                    q.begin(i, n)
                link.begin(i, LINKS, posts=True)
                both(dve, i, [q for q, _ in taken] + [link, sel_ready, pick_ready, spread_ready, xs_sb, gate_sb, h_ready],
                     lambda is_few: few(dve, e, after) if is_few else many(dve, e, after))
                for q, _ in taken:
                    q.end(NE)
                link.end(NE, posts=True)
    end_stage(K)


def second_norm(K):
    nc, block, bank, col = K.nc, K.block, K.bank, K.col
    with ExitStack() as st:
        ln = Norm(K, st, "l2", K.acc[:, :, :], K.acc[:, :, :], K.con["ones"][:, :], D, 1e-5, whole=True)
        link, normed = new_signal(K, "l2_dve_chain"), new_signal(K, "l2_normed")
        load(K, [(K.x[:, :, 0:META], K.dram["meta"])])
        loads = 16 * K.small_loads

        turned = new_signal(K, "l2_turned")

        @block.tensor
        def _(pe):
            for j in range(DT):
                for b in range(2):
                    ins = nc.tensor.transpose(bank[j // 2][:, j % 2 * T1 + b * P:j % 2 * T1 + (b + 1) * P], K.moe[:, b, j * P:(j + 1) * P],
                                              K.con["eye"][:, :])
                if j % 2:
                    ins.then_inc(*turned.post())
            ln.pe(pe)

        @block.scalar
        def _(act):
            ln.act(act)

        @block.vector
        def _(dve):
            then = linker(dve, link)
            for j in range(4):
                dve.wait_ge(*turned.take())
                part = flat(K.acc[:, 2 * j:2 * j + 2, :])
                then(dve.tensor_tensor(out=part, in0=part, in1=bank[j][:, :], op=ALU.add))
            ln.dve(dve, link, normed)
            dve.wait_ge(*normed.posted())
            for j in range(DT):
                then(dve.tensor_scalar(K.x[:, j, META:T2], K.acc[:, j, :], col("ln2_g", j), col("ln2_b", j), ALU.mult, ALU.add))
            dve.wait_ge(K.small_loaded, loads)
    end_stage(K)


def rms_of_x(K, st, name, hn):
    rms = Norm(K, st, name, K.x[:, :, :], hn, K.con["ones"][:, :], D, 1e-6, mean=False, whole=True)
    normed, hn_ready, link = new_signal(K, name + "_normed"), new_signal(K, name + "_hn"), new_signal(K, name + "_dve_chain")

    def vector(dve, gain, layer):
        rms.dve(dve, link, normed)
        dve.wait_ge(*normed.posted())
        for j in range(DT):
            ins = dve.tensor_scalar(hn[:, j, :], hn[:, j, :], K.col(gain, layer * DT + j), None, ALU.mult)
            ins.then_inc(*(hn_ready if j == DT - 1 else link).post())

    def tensor(pe):
        rms.pe(pe)
        pe.wait_ge(*hn_ready.take())

    return tensor, rms.act, vector


def swiglu(K, gain, layer):
    nc, block, bank = K.nc, K.block, K.bank
    T = T2
    name = f"{gain[:4]}_{layer}"
    with ExitStack() as st:
        def sb(n, shape):
            return st.enter_context(nc.sbuf_tensor(name + n, shape, F32))

        hn, h = sb("_hn", [P, DT, T]), sb("_h", [P, FFT, T])
        s = sb("_silu", [P, 2, T])
        tensor, scalar, vector = rms_of_x(K, st, name, hn[:, :, :])
        gu_ready, s_ready, h_free, h_ready, y_ready, y_free = \
            (new_signal(K, name + n) for n in ("_gu_ready", "_silu_ready", "_gu_free", "_h_ready", "_y_ready", "_y_free"))
        s_used = h_free.reader()

        @block.tensor
        def _(pe):
            tensor(pe)
            for j in range(FFT):
                if j >= 2:
                    pe.wait_ge(*h_free.take())
                for half in range(2):
                    for k in range(DT):
                        matmul(K, bank[2 * (j % 2) + half][:, 0:T], K.weights.take(pe), hn[:, k, :], k == 0, k == DT - 1,
                               gu_ready if half and k == DT - 1 else None)
            pe.wait_ge(*h_free.take(2))
            stream_linear(K, pe, DT, lambda k: h[:, k, :], FFT, T, y_ready, y_free)

        @block.scalar
        def _(act):
            scalar(act)
            for j in range(FFT):
                act.wait_ge(*gu_ready.take())
                if j >= 2:
                    act.wait_ge(*s_used.take())
                act.activation(s[:, j % 2, :], bank[2 * (j % 2)][:, 0:T], ACT.Silu).then_inc(*s_ready.post())

        @block.vector
        def _(dve):
            vector(dve, gain, layer)
            for j in range(FFT):
                dve.wait_ge(*s_ready.take())
                dve.tensor_tensor(out=h[:, j, :], in0=s[:, j % 2, :], in1=bank[2 * (j % 2) + 1][:, 0:T], op=ALU.mult).then_inc(*h_free.post())
            for j in range(DT):
                dve.wait_ge(*y_ready.take())
                dve.scalar_tensor_tensor(out=K.x[:, j, :], in0=bank[j % 4][:, 0:T], scalar=0.5, in1=K.x[:, j, :], op0=ALU.mult, op1=ALU.add)\
                    .then_inc(*y_free.post())
    end_stage(K)


class Attention:

    def __init__(self, K, st, name, q, k, v, mask, out, sink=None):
        self.K, self.q, self.k, self.v, self.mask, self.out, self.sink = K, q, k, v, mask, out, sink
        sb = lambda n, s: st.enter_context(K.nc.sbuf_tensor(name + n, s, F32))
        self.s, self.p = sb("_scores", [P, 2, T2]), sb("_probs", [P, 2, T2])
        self.mx, self.total, self.extra = sb("_neg_max", [P, 2]), sb("_total", [P, 2]), sb("_sink", [P, 2])
        self.pt = sb("_probs_t", [P, 2, 3, P])
        self.s_ready, self.max_ready, self.e_ready, self.p_ready, self.t_ready, self.pt_ready, self.o_ready, self.o_free, self.chain, self.ac = \
            (new_signal(K, name + n) for n in ("_scores_ready", "_max", "_exps", "_probs_ready", "_turned", "_turned_sb", "_out_ready",
                                          "_out_free", "_chain", "_act_chain"))

    def turns(self):
        return [(h, qt, q0, qn) for h in range(8) for qt, (q0, qn) in enumerate(Q3)]

    def tensor(self, pe):
        K, nc, bank = self.K, self.K.nc, self.K.bank
        all_turns = self.turns()

        def scores(n):
            h, _, q0, qn = all_turns[n]
            nc.tensor.matmul(bank[n % 2][0:qn, 0:T2], self.q(h)[:, q0:q0 + qn], self.k(h), start=True, stop=True).then_inc(*self.s_ready.post())

        scores(0)
        for n, (h, qt, q0, qn) in enumerate(all_turns):
            pe.wait_ge(*self.p_ready.take())
            if n + 1 < len(all_turns):
                scores(n + 1)
            for kt, (k0, kn) in enumerate(Q3):
                ins = nc.tensor.transpose(bank[2 + n % 2][0:kn, kt * P:kt * P + qn], self.p[0:qn, n % 2, k0:k0 + kn], K.con["eye"][0:qn, 0:qn])
            ins.then_inc(*self.t_ready.post())
            pe.wait_ge(*self.pt_ready.take())
            if n >= 2:
                pe.wait_ge(*self.o_free.take())
            r = 64 * (h % 2)
            for kt, (k0, kn) in enumerate(Q3):
                ins = nc.tensor.matmul(bank[4 + n % 2][r:r + 64, 0:qn], self.v(h, kt)[0:kn, :], self.pt[0:kn, n % 2, kt, 0:qn],
                                       start=kt == 0, stop=kt == 2)
            ins.then_inc(*self.o_ready.post())
        pe.wait_ge(*self.o_free.take(2))

    def scalar(self, act):
        K, bank = self.K, self.K.bank
        for n, (h, qt, q0, qn) in enumerate(self.turns()):
            b = n % 2
            act.wait_ge(*self.max_ready.take())
            if self.sink is not None:
                act.activation(self.extra[0:qn, b:b + 1], self.sink[0:qn, h:h + 1], ACT.Exp, bias=self.mx[0:qn, b:b + 1])
            act.activation(self.p[0:qn, b, :], self.s[0:qn, b, :], ACT.Exp, bias=self.mx[0:qn, b:b + 1],
                           accum_out=self.total[0:qn, b:b + 1]).then_inc(*self.e_ready.post())
            act.wait_ge(*self.t_ready.take())
            if qn == P:
                act.activation(self.pt[:, b, 0:2, :].rearrange("p a q -> p (a q)"), bank[2 + b][:, 0:2 * P], ACT.Copy)
            else:
                for kt in range(2):
                    act.activation(self.pt[:, b, kt, 0:qn], bank[2 + b][:, kt * P:kt * P + qn], ACT.Copy)
            act.activation(self.pt[0:T2 - 256, b, 2, 0:qn], bank[2 + b][0:T2 - 256, 2 * P:2 * P + qn], ACT.Copy).then_inc(*self.pt_ready.post())

    def vector(self, dve):
        K, bank = self.K, self.K.bank
        then = linker(dve, self.chain)
        for n, (h, qt, q0, qn) in enumerate(self.turns()):
            b = n % 2
            dve.wait_ge(*self.s_ready.take())
            then(dve.scalar_tensor_tensor(out=self.s[0:qn, b, :], in0=bank[b][0:qn, 0:T2], scalar=0.125, in1=self.mask(qt)[0:qn, :],
                                          op0=ALU.mult, op1=ALU.add))
            mx = self.mx[0:qn, b:b + 1]
            then(dve.tensor_reduce(out=mx, in_=self.s[0:qn, b, :], axis=AX.X, op=ALU.max))
            if self.sink is not None:
                then(dve.tensor_tensor(out=mx, in0=mx, in1=self.sink[0:qn, h:h + 1], op=ALU.max))
            dve.tensor_scalar(mx, mx, -1.0, None, ALU.mult).then_inc(*self.max_ready.post())
            dve.wait_ge(*self.e_ready.take())
            total = self.total[0:qn, b:b + 1]
            if self.sink is not None:
                then(dve.tensor_tensor(out=total, in0=total, in1=self.extra[0:qn, b:b + 1], op=ALU.add))
            then(dve.reciprocal(total, total))
            dve.tensor_scalar(self.p[0:qn, b, :], self.p[0:qn, b, :], total, None, ALU.mult).then_inc(*self.p_ready.post())
            dve.wait_ge(*self.o_ready.take())
            r = 64 * (h % 2)
            dve.tensor_copy(self.out[r:r + 64, h // 2, q0:q0 + qn], bank[4 + b][r:r + 64, 0:qn]).then_inc(*self.o_free.post())


def even_mixer(K):
    nc, block, bank, col = K.nc, K.block, K.bank, K.col
    T = T2
    with ExitStack() as outer:
        def sb(st, name, shape):
            return st.enter_context(nc.sbuf_tensor("even_" + name, shape, F32))

        y = sb(outer, "y", [P, 12, T])
        bq = sb(outer, "bq_bk", [P, 8, T])
        bg = sb(outer, "bg", [P, 8, T])
        bv = sb(outer, "bv", [P, 3, D])
        with ExitStack() as st:
            con = load_constants(K, st, "even")
            wiw, gains = sb(st, "w_iw", [P, DT, 8]), sb(st, "gains", [P, 2])
            load(K, [(wiw[:, :, :], K.dram["ev_w_iw"]), (gains[:, :], K.dram["ev_gains"])])
            loads = 16 * K.small_loads
            hn = sb(st, "hn", [P, DT, T])
            aqk, iq = sb(st, "aq_ak", [P, 8, T]), sb(st, "iq_ik", [P, 5, T])
            av = sb(st, "av", [P, 3, W])
            with ExitStack() as early:
                tensor, scalar, vector = rms_of_x(K, early, "even", hn[:, :, :])
            iw = sb(st, "iw", [P, 3, 8])
            work, score, r, top = sb(st, "work", [P, T]), sb(st, "score", [P, 3, T]), sb(st, "relu", [P, 2, T]), sb(st, "top", [P, 8])
            z_ready, z_free, v_ready, v_free, iw_ready = (new_signal(K, "ev_" + n) for n in ("z_ready", "z_free", "v_ready", "v_free", "iw"))
            z_sb, v_sb = z_free.reader(), v_free.reader()
            ix_ready, ix_free, link, masks, qk_ready = (new_signal(K, "ev_" + n) for n in ("index_ready", "index_free", "dve_chain", "masks", "qk_ready"))
            sq, rs = sb(st, "qk_squares", [P, 2, T]), sb(st, "qk_rstd", [P, 2, T])
            sq_ready, ss_ready, ss_free, var, root = (new_signal(K, "ev_" + n) for n in ("sq", "ss", "ss_read", "var", "root"))
            attn = Attention(K, st, "dsa", lambda h: aqk[64 * (h % 2):64 * (h % 2) + 64, h // 2, :],
                             lambda h: aqk[64 * (h % 2):64 * (h % 2) + 64, 4 + h // 2, :],
                             lambda h, kt: av[:, kt, 64 * h:64 * h + 64], lambda qt: score[:, qt, :], y)

            @block.tensor
            def _(pe):
                tensor(pe)
                stream_linear(K, pe, 29, lambda k: hn[:, k, :], DT, T, z_ready, z_free)
                for _ in range(3):
                    stream_tokens(K, pe, lambda k: hn[:, k, :], Q3, 4, v_ready, v_free, (4, 5, 6))
                pe.wait_ge(K.small_loaded, loads)
                for qt, (q0, qn) in enumerate(Q3):
                    for k in range(DT):
                        ins = nc.tensor.matmul(bank[7][0:qn, 8 * qt:8 * qt + 8], hn[:, k, q0:q0 + qn], wiw[:, k, :], start=k == 0, stop=k == DT - 1)
                ins.then_inc(*iw_ready.post())
                n = 0
                for qt, (q0, qn) in enumerate(Q3):
                    for h in range(8):
                        if n >= 4:
                            pe.wait_ge(*ix_free.take())
                        rr = slice(64 * (h % 2), 64 * (h % 2) + 64)
                        nc.tensor.matmul(bank[n % 4][0:qn, 0:T], iq[rr, h // 2, q0:q0 + qn], iq[rr, 4, :], start=True, stop=True).then_inc(*ix_ready.post())
                        n += 1
                pe.wait_ge(*ix_free.take(4))
                for j in range(8):
                    pe.wait_ge(*sq_ready.take())
                    nc.tensor.matmul(bank[j % 2][:, 0:T], K.con["ones_pair"][:, :], sq[:, j % 2, :], start=True, stop=True).then_inc(*ss_ready.post())
                pe.wait_ge(*qk_ready.take())
                attn.tensor(pe)

            @block.scalar
            def _(act):
                scalar(act)
                for j in range(29):
                    dst = aqk[:, j, :] if j < 8 else iq[:, j - 8, :] if j < 13 else bq[:, j - 13, :] if j < 21 else bg[:, j - 21, :]
                    act.wait_ge(*z_ready.take())
                    act.activation(dst, bank[j % 4][:, 0:T], ACT.Silu if j >= 21 else ACT.Copy).then_inc(*z_free.post())
                for half in range(3):
                    for b, (t0, tn) in enumerate(Q3):
                        act.wait_ge(*v_ready.take())
                        dst = av[0:tn, b, :] if half == 0 else bv[0:tn, b, (half - 1) * 512:half * 512]
                        act.activation(dst, bank[4 + b][0:tn, :], ACT.Copy).then_inc(*v_free.post())
                for j in range(8):
                    act.wait_ge(*var.take())
                    act.activation(rs[:, j % 2, :], rs[:, j % 2, :], ACT.Sqrt).then_inc(*root.post())
                attn.scalar(act)

            @block.vector
            def _(dve):
                then = linker(dve, link)
                vector(dve, "mix_norm_2", 0)
                dve.wait_ge(K.small_loaded, loads)
                dve.wait_ge(*z_sb.take(29))
                dve.wait_ge(*v_sb.take(9))
                dve.wait_ge(*iw_ready.take())
                for qt, (q0, qn) in enumerate(Q3):
                    then(dve.tensor_scalar(iw[0:qn, qt, :], bank[7][0:qn, 8 * qt:8 * qt + 8], 8 ** -0.5 * 64 ** -0.5, None, ALU.mult))
                n = 0
                for qt, (q0, qn) in enumerate(Q3):
                    s = score[0:qn, qt, :]
                    for h in range(8):
                        dve.wait_ge(*ix_ready.take())
                        dst = s if h == 0 else r[0:qn, h % 2, :]
                        dve.tensor_scalar(dst, bank[n % 4][0:qn, 0:T], 0.0, iw[0:qn, qt, h:h + 1], ALU.max, ALU.mult).then_inc(*ix_free.post())
                        dve.wait_ge(*ix_free.posted())
                        if h:
                            then(dve.tensor_tensor(out=s, in0=s, in1=r[0:qn, h % 2, :], op=ALU.add))
                        n += 1
                    m = con["dsa_mask"][0:qn, qt * T:(qt + 1) * T]
                    then(dve.tensor_tensor(out=s, in0=s, in1=m, op=ALU.add))
                    src = s
                    for _ in range(TOPK2 // 8):
                        then(dve.max(top[0:qn, :], src))
                        then(dve.match_replace(work[0:qn, :], in_to_replace=top[0:qn, :], in_values=src, imm_value=-3e38))
                        src = work[0:qn, :]
                    then(dve.tensor_tensor(out=work[0:qn, :], in0=work[0:qn, :], in1=s, op=ALU.is_equal))
                    then(dve.scalar_tensor_tensor(out=s, in0=work[0:qn, :], scalar=NEG, in1=m, op0=ALU.mult, op1=ALU.add))
                for j in range(8):
                    dve.tensor_tensor(out=sq[:, j % 2, :], in0=aqk[:, j, :], in1=aqk[:, j, :], op=ALU.mult).then_inc(*sq_ready.post())
                    dve.wait_ge(*ss_ready.take())
                    dve.tensor_scalar(rs[:, j % 2, :], bank[j % 2][:, 0:T], 1.0 / 64, 1e-6, ALU.mult, ALU.add).then_inc(*var.post())
                    dve.wait_ge(*root.take())
                    then(dve.reciprocal(rs[:, j % 2, :], rs[:, j % 2, :]))
                    then(dve.scalar_tensor_tensor(out=aqk[:, j, :], in0=aqk[:, j, :], scalar=gains[:, j // 4:j // 4 + 1], in1=rs[:, j % 2, :],
                                                  op0=ALU.mult, op1=ALU.mult))
                dve.drain().then_inc(*qk_ready.post())
                attn.vector(dve)
        end_stage(K)
        retention(K, outer, bq, bg, bv, y)
        out_projection(K, "ev", y, 12)


def retention(K, outer, bqk, bg, bv, y):
    nc, block, bank = K.nc, K.block, K.bank
    T = T2
    with ExitStack() as st:
        def sb(name, shape):
            return st.enter_context(nc.sbuf_tensor("ret_" + name, shape, F32))

        con = load_constants(K, st, "ret")
        loads = 16 * K.small_loads
        t1, t2 = sb("cos_part", [P, 2, T]), sb("sin_part", [P, 2, T])
        s = sb("scores", [P, 2, 3, T])
        r_ready, r_free, rotated, s_ready, s_sb, o_ready, o_free, link, normed = \
            (new_signal(K, "re_" + n) for n in ("turned", "turned_read", "rotated", "scores_ready", "scores_sb", "out_ready", "out_free", "chain", "normed"))
        sq, rs = sb("qk_squares", [P, 2, T]), sb("qk_rstd", [P, 2, T])
        sq_ready, ss_ready, var, root = (new_signal(K, "re_" + n) for n in ("sq", "ss", "var", "root"))

        @block.tensor
        def _(pe):
            pe.wait_ge(K.small_loaded, loads)
            for j in range(8):
                if j >= 2:
                    pe.wait_ge(*r_free.take())
                nc.tensor.matmul(bank[j % 2][:, 0:T], con["rot"][:, :], bqk[:, j, :], start=True, stop=True).then_inc(*r_ready.post())
            pe.wait_ge(*r_free.take(2))
            pe.wait_ge(*rotated.take())
            for h in range(8):
                rr = slice(64 * (h % 2), 64 * (h % 2) + 64)
                for jt, (j0, jn) in enumerate(Q3):
                    ins = nc.tensor.matmul(bank[jt + 3 * (h % 2)][0:jn, 0:T], bqk[rr, 4 + h // 2, j0:j0 + jn], bqk[rr, h // 2, :], start=True, stop=True)
                ins.then_inc(*s_ready.post())
                pe.wait_ge(*s_sb.take())
                for jt, (j0, jn) in enumerate(Q3):
                    ins = nc.tensor.matmul(bank[6 + h % 2][:, 0:T], bv[0:jn, jt, h * P:(h + 1) * P], s[0:jn, h % 2, jt, :], start=jt == 0, stop=jt == 2)
                ins.then_inc(*o_ready.post())
                pe.wait_ge(*o_free.take())
            for j in range(8):
                pe.wait_ge(*sq_ready.take())
                nc.tensor.matmul(bank[j % 2][:, 0:T], K.con["ones"][:, :], sq[:, j % 2, :], start=True, stop=True).then_inc(*ss_ready.post())

        @block.scalar
        def _(act):
            for j in range(8):
                act.wait_ge(*var.take())
                act.activation(rs[:, j % 2, :], rs[:, j % 2, :], ACT.Sqrt).then_inc(*root.post())

        @block.vector
        def _(dve):
            then = linker(dve, link)
            dve.wait_ge(K.small_loaded, loads)
            for j in range(8):
                b = j % 2
                dve.wait_ge(*r_ready.take())
                dve.tensor_tensor(out=t2[:, b, :], in0=bank[b][:, 0:T], in1=con["sin"][:, :], op=ALU.mult).then_inc(*r_free.post())
                then(dve.tensor_tensor(out=t1[:, b, :], in0=bqk[:, j, :], in1=con["cos"][:, :], op=ALU.mult))
                then(dve.tensor_tensor(out=t1[:, b, :], in0=t1[:, b, :], in1=t2[:, b, :], op=ALU.add))
                scale = con["ret_q" if j < 4 else "ret_k"][:, (j % 4) * T:(j % 4 + 1) * T]
                then(dve.tensor_tensor(out=bqk[:, j, :], in0=t1[:, b, :], in1=scale, op=ALU.mult))
            dve.drain().then_inc(*rotated.post())
            for h in range(8):
                dve.wait_ge(*s_ready.take())
                for jt, (j0, jn) in enumerate(Q3):
                    ins = dve.tensor_tensor(out=s[0:jn, h % 2, jt, :], in0=bank[jt + 3 * (h % 2)][0:jn, 0:T],
                                            in1=con["ret_mask"][0:jn, jt * T:(jt + 1) * T], op=ALU.mult)
                ins.then_inc(*s_sb.post())
                dve.wait_ge(*o_ready.take())
                dve.tensor_copy(y[:, 4 + h, :], bank[6 + h % 2][:, 0:T]).then_inc(*o_free.post())
            dve.wait_ge(*o_free.posted())
            for j in range(8):
                o = y[:, 4 + j, :]
                dve.tensor_tensor(out=sq[:, j % 2, :], in0=o, in1=o, op=ALU.mult).then_inc(*sq_ready.post())
                then(dve.tensor_tensor(out=o, in0=o, in1=bg[:, j, :], op=ALU.mult))
                dve.wait_ge(*ss_ready.take())
                dve.tensor_scalar(rs[:, j % 2, :], bank[j % 2][:, 0:T], 1.0 / P, 1e-6, ALU.mult, ALU.add).then_inc(*var.post())
                dve.wait_ge(*root.take())
                then(dve.reciprocal(rs[:, j % 2, :], rs[:, j % 2, :]))
                then(dve.tensor_tensor(out=o, in0=o, in1=rs[:, j % 2, :], op=ALU.mult))
    end_stage(K)


def out_projection(K, name, y, n_in):
    block, bank = K.block, K.bank
    ready, free = new_signal(K, name + "_proj_ready"), new_signal(K, name + "_proj_free")

    @block.tensor
    def _(pe):
        stream_linear(K, pe, DT, lambda k: y[:, k, :], n_in, T2, ready, free)

    @block.vector
    def _(dve):
        for j in range(DT):
            dve.wait_ge(*ready.take())
            dve.tensor_tensor(out=K.x[:, j, :], in0=K.x[:, j, :], in1=bank[j % 4][:, 0:T2], op=ALU.add).then_inc(*free.post())
    end_stage(K)


def odd_mixer(K):
    nc, block, bank, col = K.nc, K.block, K.bank, K.col
    T = T2
    with ExitStack() as st:
        def sb(name, shape):
            return st.enter_context(nc.sbuf_tensor("odd_" + name, shape, F32))

        con = load_constants(K, st, "odd")
        gains, sinks, dmix = sb("gains", [P, 2]), sb("sinks", [P, 8]), sb("d_mix", [P, 4, P])
        load(K, [(gains[:, :], K.dram["od_gains"]), (sinks[:, :], K.dram["od_sinks"]), (dmix[:, :, :], K.dram["od_mix"])])
        loads = 16 * K.small_loads
        y, hn = sb("y", [P, 8, T]), sb("hn", [P, DT, T])
        cqk, cv = sb("cq_ck", [P, 6, T]), sb("cv", [P, 3, P])
        PAD = 16
        dx, s0, s1 = sb("dx", [P, 4, PAD + T]), sb("window_a", [P, PAD + T]), sb("window_b", [P, PAD + T])
        pooled = sb("pooled", [P, 4, T])
        sq, rs = sb("qk_squares", [P, 2, T]), sb("qk_rstd", [P, 2, T])
        tensor, scalar, vector = rms_of_x(K, st, "odd", hn[:, :, :])
        z_ready, z_free, v_ready, v_free, link = (new_signal(K, "od_" + n) for n in ("z_ready", "z_free", "v_ready", "v_free", "chain"))
        z_sb, v_sb = z_free.reader(), v_free.reader()
        sq_ready, ss_ready, var, root, qk_ready = (new_signal(K, "od_" + n) for n in ("sq", "ss", "var", "root", "qk_ready"))
        pool_ready, mix_ready, mix_free = (new_signal(K, "od_" + n) for n in ("pooled", "mixed", "mixed_read"))
        attn = Attention(K, st, "swa", lambda h: cqk[64 * (h % 2):64 * (h % 2) + 64, h // 2, :],
                         lambda h: cqk[64 * (h % 2):64 * (h % 2) + 64, 4 + h // 4, :],
                         lambda h, kt: cv[:, kt, 64 * (h // 4):64 * (h // 4) + 64],
                         lambda qt: con["swa_mask"][:, qt * T:(qt + 1) * T], y, sink=sinks)

        @block.tensor
        def _(pe):
            tensor(pe)
            stream_linear(K, pe, 10, lambda k: hn[:, k, :], DT, T, z_ready, z_free)
            stream_tokens(K, pe, lambda k: hn[:, k, :], Q3, 1, v_ready, v_free, (4, 5, 6))
            pe.wait_ge(K.small_loaded, loads)
            for j in range(6):
                pe.wait_ge(*sq_ready.take())
                nc.tensor.matmul(bank[j % 2][:, 0:T], K.con["ones_pair"][:, :], sq[:, j % 2, :], start=True, stop=True).then_inc(*ss_ready.post())
            pe.wait_ge(*pool_ready.take())
            for j in range(4):
                nc.tensor.matmul(bank[2 + j][:, 0:T], dmix[:, j, :], pooled[:, j, :], start=True, stop=True).then_inc(*mix_ready.post())
            pe.wait_ge(*mix_free.take())
            pe.wait_ge(*qk_ready.take())
            attn.tensor(pe)

        @block.scalar
        def _(act):
            scalar(act)
            for j in range(10):
                act.wait_ge(*z_ready.take())
                act.activation(cqk[:, j, :] if j < 6 else dx[:, j - 6, PAD:PAD + T], bank[j % 4][:, 0:T], ACT.Copy).then_inc(*z_free.post())
            for b, (t0, tn) in enumerate(Q3):
                act.wait_ge(*v_ready.take())
                act.activation(cv[0:tn, b, :], bank[4 + b][0:tn, 0:P], ACT.Copy).then_inc(*v_free.post())
            for j in range(6):
                act.wait_ge(*var.take())
                act.activation(rs[:, j % 2, :], rs[:, j % 2, :], ACT.Sqrt).then_inc(*root.post())
            attn.scalar(act)

        @block.vector
        def _(dve):
            then = linker(dve, link)
            vector(dve, "mix_norm_2", 1)
            for t in (s0, s1):
                then(dve.memset(t[:, 0:PAD], 0.0))
            then(dve.memset(dx[:, :, 0:PAD], 0.0))
            dve.wait_ge(K.small_loaded, loads)
            dve.wait_ge(*z_sb.take(10))
            dve.wait_ge(*v_sb.take(3))
            for j in range(6):
                dve.tensor_tensor(out=sq[:, j % 2, :], in0=cqk[:, j, :], in1=cqk[:, j, :], op=ALU.mult).then_inc(*sq_ready.post())
                dve.wait_ge(*ss_ready.take())
                dve.tensor_scalar(rs[:, j % 2, :], bank[j % 2][:, 0:T], 1.0 / 64, 1e-6, ALU.mult, ALU.add).then_inc(*var.post())
                dve.wait_ge(*root.take())
                then(dve.reciprocal(rs[:, j % 2, :], rs[:, j % 2, :]))
                then(dve.scalar_tensor_tensor(out=cqk[:, j, :], in0=cqk[:, j, :], scalar=gains[:, j // 4:j // 4 + 1], in1=rs[:, j % 2, :],
                                              op0=ALU.mult, op1=ALU.mult))
            for j in range(4):
                src = dx[:, j, :]
                for step in range(j + 1):
                    dst = (s0, s1)[step % 2]
                    sh = 2 ** step
                    then(dve.tensor_tensor(out=dst[:, PAD:PAD + T], in0=src[:, PAD:PAD + T], in1=src[:, PAD - sh:PAD + T - sh], op=ALU.add))
                    src = dst[:, :]
                then(dve.tensor_tensor(out=pooled[:, j, :], in0=src[:, PAD:PAD + T], in1=con["pool_inv"][:, j * T:(j + 1) * T], op=ALU.mult))
                then(dve.tensor_tensor(out=pooled[:, j, :], in0=pooled[:, j, :], in1=dx[:, j, PAD:PAD + T], op=ALU.subtract))
            dve.drain().then_inc(*pool_ready.post())
            for j in range(4):
                dve.wait_ge(*mix_ready.take())
                ins = dve.tensor_scalar(y[:, 4 + j, :], bank[2 + j][:, 0:T], col("od_d_scale_2", j), None, ALU.mult)
            ins.then_inc(*mix_free.post())
            dve.drain().then_inc(*qk_ready.post())
            attn.vector(dve)
        end_stage(K)
        out_projection(K, "od", y, 8)


STAGES = [rwkv_branch, hgrn_branch, mlstm_branch, lru_branch, merge, router_and_ple, experts, second_norm,
          lambda K: swiglu(K, "ffn1_norm_2", 0), even_mixer, lambda K: swiglu(K, "ffn2_norm_2", 0),
          lambda K: swiglu(K, "ffn1_norm_2", 1), odd_mixer, lambda K: swiglu(K, "ffn2_norm_2", 1)]

SMALL = {"rwkv_w2a2": (P, W), "rwkv_g2": (P, W), "mlstm_w_gates": (P, DT, 8), "mlstm_gate_bias": (4, 2), "lru_w": (P, 8, P),
         "router_w": (P, DT, NE), "router_b": (P, NE), "p": (P, 2, T1), "expert_b_down": (NE, D), "expert_b_gu": (NE, 2 * D), "meta": (P, DT, META),
         "ev_w_iw": (P, DT, 8), "ev_gains": (P, 2), "od_gains": (P, 2), "od_sinks": (P, 8), "od_mix": (P, 4, P)}


def build(nc, upto=len(STAGES)):
    K = Kernel()
    K.nc = nc

    def dram(name, shape, kind="ExternalInput"):
        return nc.dram_tensor(name, list(shape), F32, kind=kind).ap()

    stream = dram("weight_stream", (N_CHUNKS, P, CHUNK_TILES * P))
    x_in = dram("x_t", (P, DT, T1))
    cols_in = dram("columns", (P, N_COLS))
    K.dram = {n: dram("in_" + n, s) for n, s in SMALL.items()}
    K.const_dram = {n: dram("const_" + n, v.shape) for n, v in constants().items()}
    out = dram("out_t", (P, DT, T1), "ExternalOutput")
    with ExitStack() as ctx:
        def sb(name, shape):
            return ctx.enter_context(nc.sbuf_tensor(name, shape, F32))

        sem = lambda name: ctx.enter_context(nc.semaphore(name))
        K.new_semaphore, K.spare, K.counts = sem, [], []
        K.bank = [ctx.enter_context(nc.psum_tensor(f"bank{i}", [P, 512], F32)) for i in range(8)]
        ring = sb("weight_ring", [P, SLOTS, CHUNK_TILES * P])
        K.x = sb("x", [P, DT, T2])
        K.cols = sb("columns_sb", [P, N_COLS])
        K.col = lambda name, j: K.cols[:, COL_AT[name] + j:COL_AT[name] + j + 1]
        loaded = [sem(f"weights_loaded{i}") for i in range(SLOTS)]
        used = [sem(f"weights_used{i}") for i in range(SLOTS)]
        K.weights = Weights(ring, loaded, used)
        K.small_loaded, K.small_loads = sem("small_loaded"), 0
        K.x_loaded, K.cols_loaded, K.stage_done, stored = sem("x_loaded"), sem("cols_loaded"), sem("stage_done"), sem("stored")
        K.stages = 0
        K.block = ctx.enter_context(nc.Block())

        @K.block.sync
        def _(sp):
            sp.dma_start(K.x[:, :, 0:T1], x_in).then_inc(K.x_loaded, 16)
            sp.dma_start(K.cols[:, :], cols_in).then_inc(K.cols_loaded, 16)
            for slot in range(SLOTS):
                sp.dma_start(ring[:, slot, :], stream[slot, :, :]).then_inc(loaded[slot], 16)
            with sp.Fori(1, K_ROUNDS[0]) as i:
                for slot in range(SLOTS):
                    sp.wait_ge(used[slot], i)
                    sp.dma_start(ring[:, slot, :], stream[bass.ds(i * SLOTS + slot, 1), :, :].rearrange("a p n -> (a p) n"))\
                        .then_inc(loaded[slot], 16)

        K.con = {c: sb("c_" + c, [P, K.const_dram[c].shape[1]]) for c in CONST_SETS["all"]}
        load(K, [(K.con[c][:, :], K.const_dram[c]) for c in CONST_SETS["all"]])
        with ExitStack() as first:
            K.y_branch = first.enter_context(nc.sbuf_tensor("y_branches", [P, 4, WT, T1], F32))
            for s in STAGES[:min(upto, 5)]:
                s(K)
        with ExitStack() as moe:
            K.gates = moe.enter_context(nc.sbuf_tensor("gates", [NE, T1], F32))
            K.chosen, K.gates_rows, K.place = (moe.enter_context(nc.sbuf_tensor(n, [P, 2, NE + 1], F32)) for n in ("chosen", "gate_rows", "place"))
            K.x_rows = moe.enter_context(nc.sbuf_tensor("x_rows", [P, 2, D], F32))
            K.moe = moe.enter_context(nc.sbuf_tensor("moe_rows", [P, 2, D], F32))
            K.load_of = moe.enter_context(nc.sbuf_tensor("tokens_of_expert", [P, NE], mybir.dt.int32))
            K.acc = moe.enter_context(nc.sbuf_tensor("moe_sum", [P, DT, T1], F32))
            for s in STAGES[5:min(upto, 8)]:
                s(K)
        for s in STAGES[8:upto]:
            s(K)
        n = K.stages

        @K.block.scalar
        def _(act):
            act.dma_start(out, K.x[:, :, META:T2]).then_inc(stored, 16)
            act.wait_ge(stored, 16)
    return K


K_ROUNDS = [N_CHUNKS // SLOTS]


def layout(inputs):
    a = {k: np.asarray(v) for k, v in inputs.items()}
    kt = lambda w: w.reshape(-1, P, w.shape[-1]).transpose(1, 0, 2)
    ev = a["ev_w_in_2"][0]
    od = a["od_w_in_2"][0]
    src = {"ev_ik": np.concatenate([ev[:, 2048:2112]] * 2, 1),
           "od_ck": np.concatenate([od[:, 512:576]] * 2 + [od[:, 576:640]] * 2, 1)}
    stream = np.empty((N_CHUNKS, P, CHUNK_TILES, P), np.float32)
    at = 0
    for name, idx, ks, cols, order in tile_groups():
        w = src[name] if name in src else a[name] if idx is None else a[name][idx]
        for c0 in range(0, 1):
            n = len(ks) * len(cols)
            if order == "nk":
                seq = [(k, c) for c in cols for k in ks]
            else:
                seq = [(k, c) for k in ks for c in cols]
            for q, (k, c) in enumerate(seq):
                t = at + q
                stream[t // CHUNK_TILES, :, t % CHUNK_TILES, :] = w[k * P:(k + 1) * P, c:c + P]
            at += n
    arrays = {"weight_stream": stream.reshape(N_CHUNKS, P, CHUNK_TILES * P)}
    arrays["x_t"] = a["x"][0].T.reshape(DT, P, T1).transpose(1, 0, 2)
    arrays["columns"] = np.concatenate([a[n].reshape(-1, P).T for n, _ in COLUMNS], 1)
    small = {
        "rwkv_w2a2": np.concatenate([a["rwkv_w2"][0], a["rwkv_a2"][0]], 0), "rwkv_g2": a["rwkv_g2"][0],
        "mlstm_w_gates": kt(a["w_in_first"][:, 1792 + 2048 + 2048:1792 + 2048 + 2056]),
        "mlstm_gate_bias": np.stack([a["mlstm_i_bias"][0], a["mlstm_f_bias"][0]], 1),
        "router_w": kt(a["router_w"][0]), "router_b": np.broadcast_to(a["router_b"][0], (P, NE)),
        "p": a["p"][0, 0].T.reshape(2, P, T1).transpose(1, 0, 2), "expert_b_down": a["expert_b_down"][0],
        "expert_b_gu": a["expert_b_gu"][0],
        "meta": a["meta_tokens_2"].T.reshape(DT, P, META).transpose(1, 0, 2),
        "ev_w_iw": kt(ev[:, 2112:2120]),
        "ev_gains": np.stack([np.concatenate([a[n][0]] * 2) for n in ("ev_a_q_norm_2", "ev_a_k_norm_2")], 1),
        "od_gains": np.stack([np.concatenate([a[n][0]] * 2) for n in ("od_c_q_norm_2", "od_c_k_norm_2")], 1),
        "od_sinks": np.broadcast_to(a["od_c_sinks_2"][0], (P, 8)), "od_mix": a["od_d_mix_2"][0].transpose(1, 0, 2),
    }
    lru = np.zeros((P, 8, P), np.float32)
    for f, name in enumerate(("lru_wx", "lru_wa")):
        for b in range(8):
            r = 64 * (b % 2)
            lru[r:r + 64, 4 * f + b // 2, r:r + 64] = a[name][0, b]
    small["lru_w"] = lru
    arrays.update({"in_" + n: v for n, v in small.items()})
    arrays.update({"const_" + n: v for n, v in constants().items()})
    return {k: np.ascontiguousarray(v) for k, v in arrays.items()}


def kernel(**inputs):
    import concourse.bacc as bacc
    from concourse.bass_utils import run_bass_kernel_spmd

    nc = bacc.Bacc("TRN2", target_bir_lowering=False, num_devices=1)
    arrays = layout(inputs)
    build(nc)
    r = run_bass_kernel_spmd(nc, [arrays], core_ids=[0])
    y = r.results[0]["out_t"]
    return np.ascontiguousarray(y.transpose(1, 0, 2).reshape(D, T1).T.reshape(1, T1, D))
```

```python
from contextlib import ExitStack

import numpy as np

import concourse.bass as bass
from concourse import mybir

F32 = mybir.dt.float32
ALU = mybir.AluOpType
ACT = mybir.ActivationFunctionType
AX = mybir.AxisListType

P = 128
T1 = 256
META = 16
T2 = T1 + META
D = 1024
DT = D // P
W = 512
WT = W // P
NE = 32
CHUNK_TILES = 32
SLOTS = 6
EXPERT_TILES = 3 * DT * DT
FF = 2816
FFT = FF // P
RC = 16
TOPK2 = 64
FEW = 64
SLOTS_SMALL = FEW
NEG = -1e30
ALPHA = 2.0 ** 0.25
Q3 = [(0, 128), (128, 128), (256, T2 - 256)]


def tile_groups():
    r_cols = 1792
    b0, c0 = r_cols, r_cols + 2048
    d0 = c0 + 2048 + 8
    g0 = d0 + 1024
    out = []

    def per_out(name, idx, k, cols):
        out.append((name, idx, k, list(cols), "nk"))

    def per_in(name, idx, k, cols):
        out.append((name, idx, k, list(cols), "kn"))

    kx = range(DT)
    per_out("w_in_first", None, kx, range(0, r_cols, P))
    per_out("w_in_first", None, kx, [*range(b0, b0 + 1024, P), *range(b0 + 1536, b0 + 2048, P)])
    per_in("w_in_first", None, kx, range(b0 + 1024, b0 + 1536, P))
    per_out("w_in_first", None, kx, [*range(c0, c0 + 1024, P), *range(c0 + 1536, c0 + 2048, P)])
    per_in("w_in_first", None, kx, range(c0 + 1024, c0 + 1536, P))
    per_out("w_in_first", None, kx, range(d0, d0 + 1024, P))
    for d in range(DT):
        for n in range(4):
            per_out("w_in_first", None, kx, [g0 + n * D + d * P])
            per_out("w_branch", (0, n), range(WT), [d * P])
    per_out("w_out", (0,), kx, range(0, D, P))
    per_out("ple_gate_w", (0,), kx, range(0, D, P))
    per_out("ple_proj_w", (0,), range(2), range(0, D, P))
    for e in range(NE):
        per_in("expert_w_gu", (0, e), kx, range(0, D, P))
        per_in("expert_w_gu", (0, e), kx, range(D, 2 * D, P))
        per_in("expert_w_down", (0, e), kx, range(0, D, P))

    def ffn(name, layer):
        per_out(name + "_w_in_2", (layer,), kx, [c for j in range(FFT) for c in (j * P, FF + j * P)])
        per_out(name + "_w_out_2", (layer,), range(FFT), range(0, D, P))

    ffn("ffn1", 0)
    per_out("ev_w_in_2", (0,), kx, range(0, 1024, P))
    per_out("ev_w_in_2", (0,), kx, range(1536, 2048, P))
    per_out("ev_ik", None, kx, [0])
    per_out("ev_w_in_2", (0,), kx, range(2120, 3144, P))
    per_out("ev_w_in_2", (0,), kx, range(4168, 5192, P))
    per_in("ev_w_in_2", (0,), kx, range(1024, 1536, P))
    per_in("ev_w_in_2", (0,), kx, range(3144, 3656, P))
    per_in("ev_w_in_2", (0,), kx, range(3656, 4168, P))
    per_out("ev_w_out_2", (0,), range(12), range(0, D, P))
    ffn("ffn2", 0)
    ffn("ffn1", 1)
    per_out("od_w_in_2", (0,), kx, range(0, 512, P))
    per_out("od_ck", None, kx, [0, P])
    per_out("od_w_in_2", (0,), kx, range(768, 1280, P))
    per_out("od_w_in_2", (0,), kx, [640])
    per_out("od_w_out_2", (0,), kx, range(0, D, P))
    ffn("ffn2", 1)
    return out


N_TILES = sum(len(g[2]) * len(g[3]) for g in tile_groups())
N_CHUNKS = N_TILES // CHUNK_TILES
assert N_TILES % (CHUNK_TILES * SLOTS) == 0

HEAD_ROWS = 16
COLUMNS = [("rwkv_mu", 14), ("rwkv_w0", 4), ("rwkv_a0", 4), ("rwkv_k_k", 4), ("rwkv_k_a", 4), ("rwkv_r_k", 4),
           ("rwkv_lnx_g", 4), ("rwkv_lnx_b", 4), ("hgrn_norm_w", 4), ("mlstm_conv_w", 32), ("mlstm_conv_b", 8),
           ("mlstm_norm_w", 4), ("lru_conv_w", 16), ("lru_conv_b", 4), ("lru_bx", 4), ("lru_ba", 4),
           ("lru_lambda", 4), ("ln1_g", 8), ("ln1_b", 8), ("ln2_g", 8), ("ln2_b", 8), 
           ("ffn1_norm_2", 16), ("mix_norm_2", 16), ("ffn2_norm_2", 16), ("od_d_scale_2", 4)]
COL_AT = {}
_n = 0
for _name, _tiles in COLUMNS:
    COL_AT[_name] = _n
    _n += _tiles
N_COLS = _n


def constants():
    i = np.arange(P)
    c = {}
    c["eye"] = np.eye(P)
    c["ones"] = np.ones((P, P))
    c["before"] = (i[:, None] < i[None]) * 1.0
    c["slots"] = np.ones((P, 1)) * np.arange(SLOTS_SMALL)
    c["ones_pair"] = (i[:, None] // 64 == i[None] // 64) * 1.0
    row, tiles = np.arange(HEAD_ROWS), range(8)
    c["pair_gather"] = np.concatenate([(2 * j + i[:, None] // 64 == row[None]) * 1.0 for j in tiles], 1)
    c["pair_spread"] = np.concatenate([(2 * j + i[None] // 64 == i[:, None]) * 1.0 for j in tiles], 1)
    c["head_gather"] = np.concatenate([np.ones((P, 1)) * (j == row[None]) for j in tiles], 1)
    c["head_spread"] = np.concatenate([(i[:, None] == j) * np.ones((1, P)) for j in tiles], 1)
    rot = np.zeros((P, P))
    for h in (0, 64):
        for d in range(32):
            rot[h + 32 + d, h + d] = -1.0
            rot[h + d, h + 32 + d] = 1.0
    c["rot"] = rot
    t = np.arange(T1)
    every = np.ones((P, 1))
    c["restart_rwkv"] = every * (t % RC != 0)
    c["restart_row"] = every * (t != 0)
    pair, tm, col_pair, col_tm = i // RC % 4, i % RC, i[:64] // RC, i[:64] % RC
    same = pair[:, None] == col_pair[None]
    strict, upto = same & (tm[:, None] < col_tm[None]), same & (tm[:, None] <= col_tm[None])
    c["rwkv_before"] = np.concatenate([strict, upto], 1) * 1.0
    c["rwkv_after"] = (same & (tm[:, None] > col_tm[None])) * 1.0
    c["rwkv_one"] = (same & (tm[:, None] == col_tm[None])) * 1.0
    c["rwkv_pair"] = np.repeat(pair[:, None] == np.arange(4)[None], 64, 1) * 1.0
    levels = [np.eye(P)]
    for l in range(1, 8):
        b, half = 2 ** l, 2 ** (l - 1)
        levels.append((i[:, None] // b == i[None] // b) * (i[:, None] % b < half) * (i[None] % b >= half) * 1.0)
    c["hgrn_levels"] = np.concatenate(levels, 1)
    c["mlstm_mask"] = np.concatenate([np.where((i[:, None] + s) <= t[None], 0.0, NEG) for s in (0, P)], 1)
    c["row_select"] = np.concatenate([(i == h)[:, None] * np.ones((1, P)) for h in range(4)], 1)
    tok = np.arange(T2)
    ck = (tok + 48) // 64
    qi = [np.minimum(q0 + i, T2 - 1) for q0, _ in Q3]
    c["dsa_mask"] = np.concatenate([np.where(ck[None] <= ck[q][:, None], 0.0, NEG) for q in qi], 1)
    c["swa_mask"] = np.concatenate([
        np.where((tok[None] < META) | ((ck[None] >= 1) & (ck[None] <= ck[q][:, None]) & (ck[None] >= ck[q][:, None] - 2)),
                 0.0, NEG) for q in qi], 1)
    c["ret_mask"] = np.concatenate([(q[:, None] <= tok[None]) * 1.0 for q in qi], 1)
    inv = 1.0 / (10000.0 ** (np.arange(0, 64, 2, dtype=np.float32) / np.float32(64)))
    ang = tok.astype(np.float32)[None] * inv.astype(np.float32)[i % 32][:, None]
    c["cos"], c["sin"] = np.cos(ang), np.sin(ang)
    lg = np.log(1.0 - 2.0 ** (-5.0 - np.arange(8)))
    hd = 2 * np.arange(4)[None] + (i // 64)[:, None]
    c["ret_q"] = np.exp(tok[None, None] * lg[hd][:, :, None]).reshape(P, -1)
    c["ret_k"] = (np.exp(-tok[None, None] * lg[hd][:, :, None]) * 64 ** -0.5).reshape(P, -1)
    c["pool_inv"] = np.concatenate([every / np.minimum(tok + 1, w) for w in (2, 4, 8, 16)], 1)
    return {k: np.ascontiguousarray(v, dtype=np.float32) for k, v in c.items()}


CONST_SETS = {"all": ["eye", "ones", "ones_pair"],
              "router": ["before"], "experts": ["slots"],
              "rwkv": ["restart_rwkv", "rwkv_before", "rwkv_after", "rwkv_one", "rwkv_pair"],
              "hgrn": ["restart_row", "hgrn_levels"],
              "mlstm": ["mlstm_mask", "row_select"],
              "even": ["dsa_mask", "pair_gather", "pair_spread"],
              "ret": ["rot", "cos", "sin", "ret_q", "ret_k"], "ret_heads": ["ret_mask", "head_gather", "head_spread"],
              "odd": ["swa_mask", "pool_inv", "pair_gather", "pair_spread"]}


class Signal:

    def __init__(self, sem, count=0):
        self.sem, self.posts, self.takes, self.turn, self.turn_post = sem, count, count, None, None
        self.start = count

    def reader(self):
        return Signal(self.sem, self.start)

    def post(self):
        self.posts += 1
        return self.sem, 1

    def take(self, n=1):
        self.takes += n
        return self.sem, self._value(self.takes, self.turn)

    def posted(self):
        return self.sem, self._value(self.posts, self.turn_post)

    @staticmethod
    def _value(n, turn):
        return n if turn is None else turn[0] * turn[1] + n

    def begin(self, i, per, posts=False):
        if posts:
            self.turn_post, self._p0 = (i, per), self.posts
        else:
            self.turn, self._t0 = (i, per), self.takes

    def end(self, times, posts=False):
        if posts:
            per, self.turn_post = self.turn_post[1], None
            assert self.posts - self._p0 == per, (self.sem, "posts", self.posts - self._p0, per)
            self.posts = self._p0 + per * times
        else:
            per, self.turn = self.turn[1], None
            assert self.takes - self._t0 == per, (self.sem, "takes", self.takes - self._t0, per)
            self.takes = self._t0 + per * times


def counters(signals):
    return [(q.posts, q.takes) for q in signals]


def set_counters(signals, saved):
    for q, (posts, takes) in zip(signals, saved):
        q.posts, q.takes = posts, takes


class Weights:

    def __init__(self, ring, loaded, used):
        self.ring, self.loaded, self.used, self.at, self.pending, self.turn = ring, loaded, used, 0, None, None

    def take(self, pe, n=1):
        chunk, place = divmod(self.at, CHUNK_TILES)
        slot = chunk % SLOTS
        assert place + n <= CHUNK_TILES
        if place == 0:
            uses = chunk // SLOTS + 1
            if self.turn is not None:
                uses = self.turn[0] * self.turn[1] + uses
            pe.wait_ge(self.loaded[slot], uses * 16)
            assert self.pending is None
            if chunk:
                self.pending = (chunk - 1) % SLOTS
        self.at += n
        return self.ring[:, slot, place * P:(place + n) * P]


class Kernel:
    pass


def new_signal(K, name):
    sem, count = K.spare.pop() if K.spare else (K.new_semaphore(name), 0)
    K.counts.append(Signal(sem, count))
    return K.counts[-1]


def recycle(K):
    K.spare += [(s.sem, s.posts) for s in K.counts if s.takes in (s.start, s.posts)]
    K.counts = []


def matmul(K, out, lhsT, rhs, start, stop, signal=None):
    ins = K.nc.tensor.matmul(out, lhsT, rhs, start=start, stop=stop)
    if signal is not None:
        ins.then_inc(*signal.post())
    elif K.weights.pending is not None:
        ins.then_inc(K.weights.used[K.weights.pending], 1)
        K.weights.pending = None
    return ins


def stream_linear(K, pe, n_out, x, k_tiles, tokens, ready, free, banks=(0, 1, 2, 3), side=None, x_ready=None):
    for j in range(n_out):
        if j >= len(banks):
            pe.wait_ge(*free.take())
        for k in range(k_tiles):
            if j == 0 and x_ready is not None:
                pe.wait_ge(*x_ready.take())
            matmul(K, K.bank[banks[j % len(banks)]][:, 0:tokens], K.weights.take(pe), x(k), k == 0, k == k_tiles - 1,
                   ready if k == k_tiles - 1 else None)
            if side is not None and (k + 1) % (k_tiles // 2) == 0:
                side(2 * j + (k + 1) // (k_tiles // 2) - 1)
    pe.wait_ge(*free.take(min(n_out, len(banks))))


def stream_tokens(K, pe, x, tiles, n, ready, free, banks):
    for k in range(DT):
        w = K.weights.take(pe, n)
        for b, (t0, tn) in enumerate(tiles):
            matmul(K, K.bank[banks[b]][0:tn, 0:n * P], x(k)[:, t0:t0 + tn], w, k == 0, k == DT - 1,
                   ready if k == DT - 1 else None)
    pe.wait_ge(*free.take(len(tiles)))


def flat(ap):
    return ap.rearrange("p a t -> p (a t)")


def linker(eng, chain):
    def then(ins):
        ins.then_inc(*chain.post())
        eng.wait_ge(*chain.posted())
    return then


class Norm:

    def __init__(self, K, st, name, x, out, lhsT, count, eps, mean=True, whole=False, banks=(4, 5)):
        self.K, self.x, self.out, self.lhsT, self.count, self.eps, self.mean, self.whole = \
            K, x, out, lhsT, count, eps, mean, whole
        self.banks = banks
        self.n, self.t = x.shape[1], x.shape[2]
        cols = self.t if whole else self.n * self.t
        self.cols = cols
        self.sq = st.enter_context(K.nc.sbuf_tensor(name + "_squares", [P, self.n, self.t], F32))
        self.rstd = st.enter_context(K.nc.sbuf_tensor(name + "_rstd", [P, cols], F32))
        self.given = new_signal(K, name + "_norm_given")
        self.summed = new_signal(K, name + "_norm_summed")
        self.var = new_signal(K, name + "_norm_var")
        self.root = new_signal(K, name + "_norm_root")

    def _parts(self):
        if self.whole:
            return [(self.banks[0], 0, self.t)]
        per = 512 // self.t
        return [(self.banks[i // per], i, min(per, self.n - i)) for i in range(0, self.n, per)]

    def _sums(self, src):
        if self.whole:
            for k in range(self.n):
                matmul(self.K, self.K.bank[self.banks[0]][:, 0:self.t], self.lhsT, src[:, k, :], k == 0, k == self.n - 1,
                       self.summed if k == self.n - 1 else None)
        else:
            parts = self._parts()
            for q, (b, i, m) in enumerate(parts):
                matmul(self.K, self.K.bank[b][:, 0:m * self.t], self.lhsT, flat(src[:, i:i + m, :]), True, True,
                       self.summed)

    def pe(self, pe):
        pe.wait_ge(*self.given.take())
        if self.mean:
            self._sums(self.x)
            pe.wait_ge(*self.given.take())
        self._sums(self.sq)

    def act(self, act):
        act.wait_ge(*self.var.take())
        act.activation(self.rstd[:, :], self.rstd[:, :], ACT.Sqrt).then_inc(*self.root.post())

    def dve(self, dve, chain, last):
        K, c = self.K, 1.0 / self.count
        if self.mean:
            dve.drain().then_inc(*self.given.post())
            if self.whole:
                dve.wait_ge(*self.summed.take())
                dve.tensor_scalar(self.rstd[:, :], K.bank[self.banks[0]][:, 0:self.t], c, None, ALU.mult).then_inc(*chain.post())
                dve.wait_ge(*chain.posted())
                mean = self.rstd[:, :].rearrange("p (a t) -> p a t", a=1).to_broadcast([P, self.n, self.t])
                dve.tensor_tensor(out=self.out, in0=self.x, in1=mean, op=ALU.subtract).then_inc(*chain.post())
            else:
                parts = self._parts()
                dve.wait_ge(*self.summed.take(len(parts)))
                for b, i, m in parts:
                    dve.scalar_tensor_tensor(out=flat(self.out[:, i:i + m, :]), in0=K.bank[b][:, 0:m * self.t], scalar=-c,
                                             in1=flat(self.x[:, i:i + m, :]), op0=ALU.mult, op1=ALU.add).then_inc(*chain.post())
            dve.wait_ge(*chain.posted())
            src = self.out
        else:
            src = self.x
        dve.tensor_tensor(out=self.sq[:, :, :], in0=src, in1=src, op=ALU.mult).then_inc(*self.given.post())
        parts = self._parts()
        dve.wait_ge(*self.summed.take(len(parts)))
        for b, i, m in parts:
            o = self.rstd[:, 0:self.t] if self.whole else self.rstd[:, i * self.t:(i + m) * self.t]
            s = self.t if self.whole else m * self.t
            ins = dve.tensor_scalar(o, K.bank[b][:, 0:s], c, self.eps, ALU.mult, ALU.add)
            ins.then_inc(*(self.var if (b, i, m) == parts[-1] else chain).post())
        dve.wait_ge(*self.root.take())
        dve.reciprocal(self.rstd[:, :], self.rstd[:, :]).then_inc(*chain.post())
        dve.wait_ge(*chain.posted())
        r = self.rstd[:, :].rearrange("p (a t) -> p a t", t=self.t)
        if self.whole:
            r = r.to_broadcast([P, self.n, self.t])
        dve.tensor_tensor(out=self.out, in0=src, in1=r, op=ALU.mult).then_inc(*last.post())


class HeadNorm:

    def __init__(self, K, st, name, n, squares, gather, spread, count, sum_bank, banks):
        self.K, self.n, self.squares, self.gather_by, self.spread_by, self.count, self.sum_bank, self.banks = \
            K, n, squares, gather, spread, count, sum_bank, banks
        self.rows = st.enter_context(K.nc.sbuf_tensor(name + "_head_rms", [HEAD_ROWS, T2], F32))
        self.squared, self.gathered, self.var, self.root, self.inverse, self.ready, self.free, self.chain = \
            (new_signal(K, name + n) for n in ("_squared", "_gathered", "_var", "_root", "_inverse", "_spread", "_spread_read", "_norm_chain"))

    def gather(self, pe, j):
        pe.wait_ge(*self.squared.take())
        ins = self.K.nc.tensor.matmul(self.K.bank[self.sum_bank][0:HEAD_ROWS, 0:T2], self.gather_by[:, j * HEAD_ROWS:(j + 1) * HEAD_ROWS],
                                      self.squares[:, j, :], start=j == 0, stop=j == self.n - 1)
        if j == self.n - 1:
            ins.then_inc(*self.gathered.post())

    def spread(self, pe, j):
        if j == 0:
            pe.wait_ge(*self.inverse.take())
        if j >= len(self.banks):
            pe.wait_ge(*self.free.take())
        self.K.nc.tensor.matmul(self.K.bank[self.banks[j % len(self.banks)]][:, 0:T2], self.spread_by[0:HEAD_ROWS, j * P:(j + 1) * P],
                                self.rows[:, :], start=True, stop=True).then_inc(*self.ready.post())
        if j == self.n - 1:
            pe.wait_ge(*self.free.take(len(self.banks)))

    def scalar(self, act):
        act.wait_ge(*self.var.take())
        act.activation(self.rows[:, :], self.rows[:, :], ACT.Sqrt).then_inc(*self.root.post())

    def vector(self, dve):
        dve.wait_ge(*self.gathered.take())
        dve.tensor_scalar(self.rows[:, :], self.K.bank[self.sum_bank][0:HEAD_ROWS, 0:T2], 1.0 / self.count, 1e-6, ALU.mult, ALU.add)\
           .then_inc(*self.var.post())
        dve.wait_ge(*self.root.take())
        dve.reciprocal(self.rows[:, :], self.rows[:, :]).then_inc(*self.inverse.post())

    def spread_to(self, dve, j):
        dve.wait_ge(*self.ready.take())
        return self.K.bank[self.banks[j % len(self.banks)]][:, 0:T2]


def end_stage(K):
    K.stages += 1
    n = K.stages
    recycle(K)

    @K.block.tensor
    def _(pe):
        pe.drain().then_inc(K.stage_done, 1)
        pe.wait_ge(K.stage_done, 3 * n)

    @K.block.scalar
    def _(act):
        act.drain().then_inc(K.stage_done, 1)
        act.wait_ge(K.stage_done, 3 * n)

    @K.block.vector
    def _(dve):
        dve.drain().then_inc(K.stage_done, 1)
        dve.wait_ge(K.stage_done, 3 * n)

    @K.block.gpsimd
    def _(pool):
        pool.wait_ge(K.stage_done, 3 * n)


def constant_buffers(K, st, name):
    out = {}
    for c in CONST_SETS[name]:
        out[c] = st.enter_context(K.nc.sbuf_tensor(f"c_{name}_{c}", [P, K.const_dram[c].shape[1]], F32))
    return out


def fill_constants(K, out):
    load(K, [(buffer[:, :], K.const_dram[c]) for c, buffer in out.items()])


def load_constants(K, st, name):
    out = constant_buffers(K, st, name)
    fill_constants(K, out)
    return out


def load(K, pairs):
    @K.block.gpsimd
    def _(pool):
        for dst, src in pairs:
            pool.dma_start(dst, src).then_inc(K.small_loaded, 16)
    K.small_loads += len(pairs)


def log_sigmoid(K, st, name, x, out):
    a = st.enter_context(K.nc.sbuf_tensor(name + "_abs", list(x.shape), F32))
    abs_ready, soft_ready = new_signal(K, name + "_abs_ready"), new_signal(K, name + "_soft_ready")

    def dve_abs(dve):
        dve.scalar_tensor_tensor(out=a[:, :], in0=x, scalar=-1.0, in1=x, op0=ALU.mult, op1=ALU.max)\
           .then_inc(*abs_ready.post())

    def act_log(act, chain):
        act.wait_ge(*abs_ready.take())
        act.activation(a[:, :], a[:, :], ACT.Exp, scale=-1.0).then_inc(*chain.post())
        act.wait_ge(*chain.posted())
        act.activation(a[:, :], a[:, :], ACT.Ln, bias=1.0).then_inc(*soft_ready.post())

    def dve_log(dve, last):
        dve.wait_ge(*soft_ready.take())
        dve.scalar_tensor_tensor(out=out, in0=x, scalar=0.0, in1=a[:, :], op0=ALU.min, op1=ALU.subtract)\
           .then_inc(*last.post())

    return dve_abs, act_log, dve_log


def rwkv_branch(K):
    nc, block, bank, col = K.nc, K.block, K.bank, K.col
    T = T1
    y = K.y_branch[:, 0]
    with ExitStack() as st:
        def sb(name, shape):
            return st.enter_context(nc.sbuf_tensor("rwkv_" + name, shape, F32))

        con = load_constants(K, st, "rwkv")
        w2a2, g2 = sb("w2a2", [P, W]), sb("g2", [P, W])
        load(K, [(w2a2[:, :], K.dram["rwkv_w2a2"]), (g2[:, :], K.dram["rwkv_g2"])])
        loads = 16 * K.small_loads

        zs = sb("shifted", [P, 14, T])
        g, lsum, lprev, sq = (sb(n, [P, 4, T]) for n in ("g", "log_sum", "log_prev", "kk_sq"))
        ew = lsum
        ops = sb("chunk_inputs", [P, 5, 4, T + RC])
        at, rt, bt, kt = (ops[:, n, :, 0:T] for n in range(4))
        with ExitStack() as early:
            z = early.enter_context(nc.sbuf_tensor("rwkv_z", [P, 14, T + 1], F32))
            diff = early.enter_context(nc.sbuf_tensor("rwkv_diff", [P, T], F32))
        with ExitStack() as middle:
            tw, sg, av, lw, kk, nrm, en = (middle.enter_context(nc.sbuf_tensor("rwkv_" + n, shape, F32)) for n, shape in (
                ("tanh_w", [64, T]), ("sig_g", [P, T]), ("a", [P, 4, T]), ("log_w", [P, 4, T]), ("kk", [P, 4, T]),
                ("kk_norm", [P, 4, T]), ("exp_neg", [P, 4, T])))
        bonus = sq
        r, k, v = zs[:, 0:4, :], zs[:, 4:8, :], zs[:, 8:12, :]

        z_ready, z_free = new_signal(K, "rw_z_ready"), new_signal(K, "rw_z_free")
        z_sb = z_free.reader()
        shifted, gates_in = new_signal(K, "rw_shifted"), new_signal(K, "rw_gates_in")
        lora_ready, lora_free, lora_out = new_signal(K, "rw_lora_ready"), new_signal(K, "rw_lora_free"), new_signal(K, "rw_lora_out")
        sums_ready, exps_ready = new_signal(K, "rw_log_sums"), new_signal(K, "rw_exps")
        sq_ready, ss_ready, nrm_ready = new_signal(K, "rw_sq"), new_signal(K, "rw_ss"), new_signal(K, "rw_nrm")
        rk_ready, bonus_ready = new_signal(K, "rw_rk"), new_signal(K, "rw_bonus")
        link, alink, gates_in_dve = new_signal(K, "rw_dve_chain"), new_signal(K, "rw_act_chain"), new_signal(K, "rw_low_rank_shifted")

        @block.tensor
        def _(pe):
            pe.wait_ge(K.x_loaded, 16)
            stream_linear(K, pe, 14, lambda k: K.x[:, k, 0:T], DT, T, z_ready, z_free)
            pe.wait_ge(*gates_in.take())
            pe.wait_ge(*shifted.take())
            pe.wait_ge(K.small_loaded, loads)
            for j in range(12):
                if j >= 4:
                    pe.wait_ge(*lora_free.take())
                f, q = divmod(j, 4)
                a, x = [(w2a2[0:64, q * P:(q + 1) * P], tw[:, :]), (w2a2[64:P, q * P:(q + 1) * P], zs[64:P, 12, :]),
                        (g2[:, q * P:(q + 1) * P], sg[:, :])][f]
                matmul(K, bank[j % 4][:, 0:T], a, x, True, True, lora_ready)
            pe.wait_ge(*lora_free.take(4))
            pe.wait_ge(*sq_ready.take())
            for q in range(2):
                matmul(K, bank[q][:, :], K.con["ones_pair"][:, :], flat(sq[:, 2 * q:2 * q + 2, :]), True, True, ss_ready)
            pe.wait_ge(*rk_ready.take())
            for q in range(2):
                matmul(K, bank[q][:, :], K.con["ones_pair"][:, :], flat(kk[:, 2 * q:2 * q + 2, :]), True, True, bonus_ready)

        @block.scalar
        def _(act):
            for j in range(14):
                act.wait_ge(*z_ready.take())
                act.activation(z[:, j, 1:T + 1], bank[j % 4][:, 0:T], ACT.Copy).then_inc(*z_free.post())
            act.wait_ge(*gates_in_dve.take())
            act.activation(tw[:, :], zs[0:64, 12, :], ACT.Tanh).then_inc(*alink.post())
            act.activation(sg[:, :], zs[:, 13, :], ACT.Sigmoid).then_inc(*gates_in.post())
            for j in range(12):
                f, q = divmod(j, 4)
                act.wait_ge(*lora_ready.take())
                if f == 0:
                    act.activation(lw[:, q, :], bank[j % 4][:, 0:T], ACT.Sigmoid, bias=col("rwkv_w0", q)).then_inc(*lora_free.post())
                elif f == 1:
                    act.activation(av[:, q, :], bank[j % 4][:, 0:T], ACT.Sigmoid, bias=col("rwkv_a0", q)).then_inc(*lora_free.post())
                else:
                    act.activation(g[:, q, :], bank[j % 4][:, 0:T], ACT.Copy).then_inc(*lora_free.post())
            act.drain().then_inc(*lora_out.post())
            act.wait_ge(*sums_ready.take())
            act.activation(flat(en[:, :, :]), flat(lsum[:, :, :]), ACT.Exp, scale=-1.0).then_inc(*alink.post())
            act.wait_ge(*alink.posted())
            act.activation(flat(ew[:, :, :]), flat(lsum[:, :, :]), ACT.Exp).then_inc(*alink.post())
            act.activation(flat(lprev[:, :, :]), flat(lprev[:, :, :]), ACT.Exp).then_inc(*exps_ready.post())
            act.wait_ge(*ss_ready.take(2))
            for q in range(2):
                act.activation(flat(nrm[:, 2 * q:2 * q + 2, :]), bank[q][:, :], ACT.Sqrt).then_inc(*(nrm_ready if q else alink).post())

        @block.vector
        def _(dve):
            then = linker(dve, link)

            then(dve.memset(z[:, :, 0:1], 0.0))
            dve.wait_ge(K.small_loaded, loads)
            dve.wait_ge(K.cols_loaded, 16)
            for j in range(14):
                dve.wait_ge(*z_sb.take())
                then(dve.tensor_tensor(out=diff[:, :], in0=z[:, j, 0:T], in1=z[:, j, 1:T + 1], op=ALU.subtract))
                ins = dve.scalar_tensor_tensor(out=zs[:, j, :], in0=diff[:, :], scalar=col("rwkv_mu", j), in1=z[:, j, 1:T + 1],
                                               op0=ALU.mult, op1=ALU.add)
                if j < 12:
                    ins.then_inc(*link.post())
                elif j == 12:
                    ins.then_inc(*shifted.post())
                else:
                    ins.then_inc(*gates_in_dve.post())
                dve.wait_ge(*(link if j < 12 else shifted if j == 12 else gates_in_dve).posted())
            dve.wait_ge(*lora_out.take())
            then(dve.tensor_scalar(flat(lw[:, :, :]), flat(lw[:, :, :]), -float(np.exp(-0.5)), None, ALU.mult))
            for q in range(4):
                ins = dve.tensor_tensor_scan(out=lsum[:, q, :], data0=con["restart_rwkv"][:, :], data1=lw[:, q, :],
                                             initial=0.0, op0=ALU.mult, op1=ALU.add)
                then(ins)
            dve.tensor_tensor(out=lprev[:, :, :], in0=lsum[:, :, :], in1=lw[:, :, :], op=ALU.subtract).then_inc(*sums_ready.post())
            for q in range(4):
                then(dve.tensor_scalar(kk[:, q, :], k[:, q, :], col("rwkv_k_k", q), None, ALU.mult))
            dve.tensor_tensor(out=sq[:, :, :], in0=kk[:, :, :], in1=kk[:, :, :], op=ALU.mult).then_inc(*sq_ready.post())
            for q in range(4):
                then(dve.tensor_scalar(kt[:, q, :], av[:, q, :], -1.0, col("rwkv_k_a", q), ALU.add, ALU.mult))
            then(dve.tensor_copy(ops[:, 4, :, 0:T], v))
            then(dve.scalar_tensor_tensor(out=kt[:, :, :], in0=kt[:, :, :], scalar=1.0, in1=k, op0=ALU.add, op1=ALU.mult))
            dve.wait_ge(*nrm_ready.take())
            then(dve.tensor_scalar(nrm[:, :, :], nrm[:, :, :], 1e-12, None, ALU.max))
            then(dve.reciprocal(nrm[:, :, :], nrm[:, :, :]))
            then(dve.tensor_tensor(out=nrm[:, :, :], in0=kk[:, :, :], in1=nrm[:, :, :], op=ALU.mult))
            dve.wait_ge(*exps_ready.take())
            then(dve.scalar_tensor_tensor(out=at[:, :, :], in0=nrm[:, :, :], scalar=-1.0, in1=lprev[:, :, :], op0=ALU.mult, op1=ALU.mult))
            then(dve.tensor_tensor(out=bt[:, :, :], in0=nrm[:, :, :], in1=av[:, :, :], op=ALU.mult))
            then(dve.tensor_tensor(out=bt[:, :, :], in0=bt[:, :, :], in1=en[:, :, :], op=ALU.mult))
            then(dve.tensor_tensor(out=rt[:, :, :], in0=r, in1=ew[:, :, :], op=ALU.mult))
            then(dve.tensor_tensor(out=kk[:, :, :], in0=r, in1=kt[:, :, :], op=ALU.mult))
            for q in range(4):
                ins = dve.tensor_scalar(kk[:, q, :], kk[:, q, :], col("rwkv_r_k", q), None, ALU.mult)
                if q < 3:
                    then(ins)
                else:
                    ins.then_inc(*rk_ready.post())
            then(dve.tensor_tensor(out=kt[:, :, :], in0=kt[:, :, :], in1=en[:, :, :], op=ALU.mult))
            dve.wait_ge(*bonus_ready.take(2))
            for q in range(2):
                then(dve.tensor_tensor(out=flat(bonus[:, 2 * q:2 * q + 2, :]), in0=bank[q][:, :], in1=flat(v[:, 2 * q:2 * q + 2, :]), op=ALU.mult))

        rwkv_chunks(K, st, con, ops, ew, y)

        ln = Norm(K, st, "rw", y, y, K.con["ones_pair"][:, :], 64, 64e-5)
        normed = new_signal(K, "rw_normed")

        @block.tensor
        def _(pe):
            ln.pe(pe)

        @block.scalar
        def _(act):
            ln.act(act)

        @block.vector
        def _(dve):
            then = linker(dve, link)

            ln.dve(dve, link, normed)
            dve.wait_ge(*normed.posted())
            for q in range(4):
                then(dve.tensor_scalar(y[:, q, :], y[:, q, :], col("rwkv_lnx_g", q), col("rwkv_lnx_b", q), ALU.mult, ALU.add))
            then(dve.tensor_tensor(out=y, in0=y, in1=bonus[:, :, :], op=ALU.add))
            then(dve.tensor_tensor(out=y, in0=y, in1=g[:, :, :], op=ALU.mult))
    end_stage(K)


def rwkv_chunks(K, st, con, ops, ew, y):
    nc, block, bank = K.nc, K.block, K.bank
    NCH, R = T1 // RC, 64

    def sb(name, shape):
        return st.enter_context(nc.sbuf_tensor("rwkv_" + name, shape, F32))

    cur = sb("chunk", [P, 5, R])
    xar = sb("ar_by_pair", [P, 2, 4 * (R + RC)])
    state = sb("state", [P, 4, 64])
    mt_b, mt_k, m_b = sb("mt_b", [P, 2, R]), sb("mt_k", [P, 2, R]), sb("m_b", [P, R])
    rows_vbk = sb("rows_vbk", [P, 3, 64])
    v_by, u_by = sb("v_by_pair", [P, 4, 64]), sb("u_by_pair", [P, 4, 64])
    m2, m2t, m4, m4t, m8 = (sb(n, [P, R]) for n in ("m2", "m2t", "m4", "m4t", "m8"))
    x1, x2, x4, x8 = (sb(n, [P, R]) for n in ("x1", "x2", "x4", "x8"))
    rhs, u, y_rows = sb("rhs", [P, 64]), sb("u", [P, 64]), sb("y_rows", [P, 64])
    to_pe, to_dve, rows_ready, rows_sb, y_sb, y_turned, y_done, chain = (
        new_signal(K, "rwc_" + n) for n in ("for_tensor", "for_vector", "rows_ready", "rows_sb", "y_rows", "y_turned", "y_done", "chain"))
    rows_too = rows_sb.reader()
    halves = (slice(0, 64), slice(64, P))
    eye = K.con["eye"]

    def product(out, lhsT, rhs, start=True, stop=True):
        for h in halves:
            ins = nc.tensor.matmul(out(h), lhsT(h), rhs(h), start=start, stop=stop)
        return ins

    def gate(b=0):
        nc.tensor.matmul(bank[b][0:32, 511:512], eye[:, 0:32], eye[:, 0:1], start=True, stop=True)

    @block.tensor
    def _(pe):
        def products_of_inputs():
            gate()
            ar = lambda h: cur[h, 0:2, :].rearrange("p a n -> p (a n)")
            product(lambda h: bank[0][h, 0:2 * R], lambda h: cur[h, 2, :], ar)
            product(lambda h: bank[1][h, 0:2 * R], lambda h: cur[h, 3, :], ar)
            product(lambda h: bank[2][h, 0:R], lambda h: cur[h, 0, :], lambda h: cur[h, 2, :]).then_inc(*to_dve.post())

        def rows_by_step():
            for n, x in enumerate((4, 2, 3)):
                ins = product(lambda h: bank[3][h, n * 64:(n + 1) * 64], lambda h: cur[h, x, :], lambda h: eye[h, h])
            ins.then_inc(*rows_ready.post())

        pe.wait_ge(*to_pe.take())
        products_of_inputs()
        rows_by_step()
        with pe.Fori(0, NCH) as i:
            to_pe.begin(i, 7)
            rows_sb.begin(i, 1)
            y_sb.begin(i, 1)
            of_state = lambda a, p, first: product(lambda h: bank[6 + a][h, 0:64], lambda h: xar[h, a, p * R:(p + 1) * R],
                                                   lambda h: state[h, p, :], first, False)
            pe.wait_ge(*to_pe.take())
            gate()
            product(lambda h: bank[0][h, 0:R], lambda h: mt_b[h, 0, :], lambda h: m_b[h, :])
            product(lambda h: bank[1][h, 0:R], lambda h: m_b[h, :], lambda h: mt_b[h, 0, :]).then_inc(*to_dve.post())
            for p in range(4):
                of_state(0, p, p == 0)
            for p in range(4):
                of_state(1, p, p == 0)
            pe.wait_ge(*to_pe.take())
            pe.wait_ge(*rows_sb.take())
            gate()
            product(lambda h: bank[1][h, 0:R], lambda h: m2[h, :], lambda h: x1[h, :])
            product(lambda h: bank[2][h, 0:R], lambda h: m2t[h, :], lambda h: m2[h, :])
            product(lambda h: bank[3][h, 0:R], lambda h: m2[h, :], lambda h: m2t[h, :]).then_inc(*to_dve.post())
            v = lambda h: rows_vbk[h, 0, :]
            product(lambda h: bank[6][h, 0:64], lambda h: mt_k[h, 0, :], v, False, True).then_inc(*to_dve.post())
            product(lambda h: bank[7][h, 0:64], lambda h: mt_k[h, 1, :], v, False, False)
            growth = lambda h: bank[5][h, 0:256]
            by = lambda x: lambda h: x[h, :, :].rearrange("p a v -> p (a v)")
            pe.wait_ge(*to_pe.take())
            gate()
            product(lambda h: bank[0][h, 0:R], lambda h: m4t[h, :], lambda h: m4[h, :])
            product(lambda h: bank[1][h, 0:R], lambda h: m4[h, :], lambda h: x2[h, :]).then_inc(*to_dve.post())
            product(growth, lambda h: rows_vbk[h, 2, :], by(v_by), True, False)
            pe.wait_ge(*to_pe.take())
            gate()
            product(lambda h: bank[1][h, 0:R], lambda h: m8[h, :], lambda h: x4[h, :]).then_inc(*to_dve.post())
            pe.wait_ge(*to_pe.take(2))
            gate()
            product(lambda h: bank[6][h, 0:64], lambda h: x8[h, :], lambda h: rhs[h, :]).then_inc(*to_dve.post())
            products_of_inputs()
            pe.wait_ge(*to_pe.take())
            gate()
            product(lambda h: bank[7][h, 0:64], lambda h: mt_b[h, 1, :], lambda h: u[h, :], False, True).then_inc(*y_turned.post())
            product(growth, lambda h: rows_vbk[h, 1, :], by(u_by), False, True).then_inc(*to_dve.post())
            rows_by_step()
            pe.wait_ge(*y_sb.take())
            gate(4)
            product(lambda h: bank[4][h, 0:64], lambda h: y_rows[h, :], lambda h: eye[h, h]).then_inc(*y_turned.post())
            for q in (to_pe, rows_sb, y_sb):
                q.end(NCH)

    @block.scalar
    def _(act):
        with act.Fori(0, NCH) as i:
            rows_ready.begin(i, 1)
            y_turned.begin(i, 2)
            y_done.begin(i, 1, posts=True)
            act.wait_ge(*rows_ready.take())
            act.activation(rows_vbk[:, :, :].rearrange("p a v -> p (a v)"), bank[3][:, 0:192], ACT.Copy).then_inc(*rows_sb.post())
            act.wait_ge(*y_turned.take())
            act.activation(y_rows[:, :], bank[7][:, 0:64], ACT.Copy).then_inc(*y_sb.post())
            act.wait_ge(*y_turned.take())
            act.activation(y[:, :, bass.ds(i * RC, RC)], bank[4][:, 0:64].rearrange("p (a t) -> p a t", a=4), ACT.Copy)\
               .then_inc(*y_done.post())
            rows_ready.end(NCH)
            y_turned.end(NCH)
            y_done.end(NCH, posts=True)

    @block.vector
    def _(dve):
        then = linker(dve, chain)
        then(dve.memset(xar[:, :, :], 0.0))
        then(dve.memset(state[:, :, :], 0.0))
        pair = con["rwkv_pair"][:, :].rearrange("p (a v) -> p a v", a=4)

        def by_pair(x):
            return x.rearrange("p (a v) -> p a v", a=1).to_broadcast([P, 4, 64])

        then(dve.memset(ops[:, :, :, T1:T1 + RC], 0.0))

        def inputs(now):
            for a in range(2):
                own = xar[:, a, :].rearrange("p (a n) -> p a n", a=4)[:, :, 0:RC]
                dve.tensor_copy(own, ops[:, a, :, now])
            dve.tensor_copy(cur[:, :, :].rearrange("p n (q t) -> p (n q) t", t=RC),
                            ops[:, :, :, now].rearrange("p n q t -> p (n q) t")).then_inc(*to_pe.post())

        inputs(slice(0, RC))
        dve.wait_ge(*to_dve.take())
        with dve.Fori(0, NCH) as i:
            to_dve.begin(i, 8)
            rows_too.begin(i, 1)
            chain.begin(i, 3, posts=True)
            then(dve.tensor_tensor(out=flat(mt_b[:, :, :]), in0=bank[0][:, 0:2 * R], in1=con["rwkv_before"][:, :], op=ALU.mult))
            dve.tensor_tensor(out=flat(mt_k[:, :, :]), in0=bank[1][:, 0:2 * R], in1=con["rwkv_before"][:, :], op=ALU.mult)
            dve.tensor_tensor(out=m_b[:, :], in0=bank[2][:, 0:R], in1=con["rwkv_after"][:, :], op=ALU.mult).then_inc(*to_pe.post())
            dve.wait_ge(*rows_too.take())
            dve.tensor_tensor(out=v_by[:, :, :], in0=by_pair(rows_vbk[:, 0, :]), in1=pair, op=ALU.mult)
            dve.tensor_tensor(out=x1[:, :], in0=mt_b[:, 0, :], in1=con["rwkv_one"][:, :], op=ALU.add)
            dve.wait_ge(*to_dve.take())
            dve.tensor_copy(m2[:, :], bank[0][:, 0:R])
            dve.tensor_copy(m2t[:, :], bank[1][:, 0:R]).then_inc(*to_pe.post())
            dve.wait_ge(*to_dve.take())
            dve.tensor_tensor(out=x2[:, :], in0=x1[:, :], in1=bank[1][:, 0:R], op=ALU.add)
            dve.tensor_copy(m4[:, :], bank[2][:, 0:R])
            dve.tensor_copy(m4t[:, :], bank[3][:, 0:R]).then_inc(*to_pe.post())
            dve.wait_ge(*to_dve.take())
            dve.tensor_copy(rhs[:, :], bank[6][:, 0:64])
            dve.wait_ge(*to_dve.take())
            dve.tensor_tensor(out=x4[:, :], in0=x2[:, :], in1=bank[1][:, 0:R], op=ALU.add)
            dve.tensor_copy(m8[:, :], bank[0][:, 0:R]).then_inc(*to_pe.post())
            inputs(bass.ds(i * RC + RC, RC))
            dve.wait_ge(*to_dve.take())
            dve.tensor_tensor(out=x8[:, :], in0=x4[:, :], in1=bank[1][:, 0:R], op=ALU.add).then_inc(*to_pe.post())
            dve.wait_ge(*to_dve.take())
            dve.tensor_copy(u[:, :], bank[6][:, 0:64])
            dve.tensor_tensor(out=u_by[:, :, :], in0=by_pair(bank[6][:, 0:64]), in1=pair, op=ALU.mult).then_inc(*to_pe.post())
            dve.wait_ge(*to_dve.take(2))
            then(dve.tensor_tensor(out=flat(state[:, :, :]), in0=flat(state[:, :, :]), in1=bank[5][:, 0:256], op=ALU.add))
            decay = ew[:, :, bass.ds(i * RC + RC - 1, 1)].to_broadcast([P, 4, 64])
            then(dve.tensor_tensor(out=state[:, :, :], in0=state[:, :, :], in1=decay, op=ALU.mult))
            to_dve.end(NCH)
            rows_too.end(NCH)
            chain.end(NCH, posts=True)
        dve.wait_ge(*y_done.posted())


def hgrn_branch(K):
    nc, block, bank, col = K.nc, K.block, K.bank, K.col
    T = T1
    y = K.y_branch[:, 1]
    with ExitStack() as st:
        def sb(name, shape):
            return st.enter_context(nc.sbuf_tensor("hgrn_" + name, shape, F32))

        con = load_constants(K, st, "hgrn")
        loads = 16 * K.small_loads
        q, f, k, g = sb("q", [P, 4, T]), sb("f", [P, 4, T]), sb("k", [P, 4, T]), sb("g", [P, 4, T])
        v = sb("v", [P, 2, W])
        lf, c = sb("log_f", [P, 4, T]), sb("cum_log", [P, 4, T])
        eq, ek = sb("decay_q", [P, 4 * T]), sb("decay_k", [P, 4 * T])
        q_levels, k_levels = sb("q_level", [P, 2, 4 * T]), sb("k_level", [P, 2, 4 * T])
        attn, cross = sb("attn", [P, 8, P]), sb("attn_cross", [P, 4, P])
        part = sb("attn_part", [P, 4, P])
        z_ready, z_free = new_signal(K, "hg_z_ready"), new_signal(K, "hg_z_free")
        v_ready, v_free, inputs = new_signal(K, "hg_v_ready"), new_signal(K, "hg_v_free"), new_signal(K, "hg_inputs")
        diffs, exps, level_ready, level_done = (new_signal(K, "hg_" + n) for n in ("diffs", "exps", "level_ready", "level_done"))
        attn_ready, o_ready, normed = new_signal(K, "hg_attn_ready"), new_signal(K, "hg_o_ready"), new_signal(K, "hg_normed")
        cum = new_signal(K, "hg_cum")
        link, alink = new_signal(K, "hg_dve_chain"), new_signal(K, "hg_act_chain")
        dve_abs, act_log, dve_log = log_sigmoid(K, st, "hg", flat(f[:, :, :]), flat(lf[:, :, :]))
        rms = Norm(K, st, "hg", y, y, K.con["ones"][:, :], P, 1e-6, mean=False)

        @block.tensor
        def _(pe):
            stream_linear(K, pe, 12, lambda kt: K.x[:, kt, 0:T], DT, T, z_ready, z_free)
            stream_tokens(K, pe, lambda kt: K.x[:, kt, :], [(0, P), (P, P)], 4, v_ready, v_free, (4, 5))
            for level in range(9):
                pe.wait_ge(*level_ready.take())
                ql, kl = q_levels[:, level % 2, :], k_levels[:, level % 2, :]
                if level < 8:
                    for h in range(4):
                        for b in range(2):
                            at = h * T + b * P
                            ins = nc.tensor.matmul(bank[(2 * h + b) // 4 + 2 * (level % 2)][:, (2 * h + b) % 4 * P:(2 * h + b) % 4 * P + P],
                                                   kl[:, at:at + P], ql[:, at:at + P], start=True, stop=True)
                else:
                    for h in range(4):
                        ins = nc.tensor.matmul(bank[h // 4 + 2 * (level % 2)][:, h % 4 * P:h % 4 * P + P],
                                               kl[:, h * T:h * T + P], ql[:, h * T + P:h * T + 2 * P], start=True, stop=True)
                ins.then_inc(*level_done.post())
            pe.wait_ge(*attn_ready.take())
            for h in range(4):
                o = bank[4 + h // 2][:, h % 2 * T:(h % 2 + 1) * T]
                cols = slice(h * P, (h + 1) * P)
                nc.tensor.matmul(o[:, 0:P], v[:, 0, cols], attn[:, 2 * h, :], start=True, stop=True)
                nc.tensor.matmul(o[:, P:2 * P], v[:, 0, cols], cross[:, h, :], start=True, stop=False)
                ins = nc.tensor.matmul(o[:, P:2 * P], v[:, 1, cols], attn[:, 2 * h + 1, :], start=False, stop=True)
            ins.then_inc(*o_ready.post())
            rms.pe(pe)

        @block.scalar
        def _(act):
            for j in range(12):
                act.wait_ge(*z_ready.take())
                dst, fn = [(q, ACT.Silu), (f, ACT.Copy), (g, ACT.Silu)][j // 4]
                act.activation(dst[:, j % 4, :], bank[j % 4][:, 0:T], fn).then_inc(*z_free.post())
            for b in range(2):
                act.wait_ge(*v_ready.take())
                act.activation(v[:, b, :], bank[4 + b][:, :], ACT.Copy).then_inc(*v_free.post())
            act.wait_ge(*z_free.posted())
            act.activation(flat(k[:, :, :]), flat(f[:, :, :]), ACT.Sigmoid, scale=-1.0).then_inc(*inputs.post())
            act_log(act, alink)
            for level in range(1, 9):
                act.wait_ge(*diffs.take())
                half, size = 2 ** level // 2, 2 ** level
                right = eq[:, :].rearrange("p (b s) -> p b s", s=size)[:, :, half:size]
                left = ek[:, :].rearrange("p (b s) -> p b s", s=size)[:, :, 0:half]
                act.activation(right, right, ACT.Exp).then_inc(*alink.post())
                act.activation(left, left, ACT.Exp).then_inc(*exps.post())
            rms.act(act)

        def add_level(dve, then, level):
            dve.wait_ge(*level_done.take())
            mask = con["hgrn_levels"][:, level * P:(level + 1) * P].rearrange("p (a t) -> p a t", a=1).to_broadcast([P, 4, P]) if level < 8 else None
            for b in range(2):
                src = bank[b + 2 * (level % 2)][:, :].rearrange("p (a t) -> p a t", t=P)
                if level == 0:
                    then(dve.tensor_tensor(out=attn[:, 4 * b:4 * b + 4, :], in0=src, in1=mask, op=ALU.mult))
                elif level < 8:
                    then(dve.tensor_tensor(out=part[:, :, :], in0=src, in1=mask, op=ALU.mult))
                    then(dve.tensor_tensor(out=attn[:, 4 * b:4 * b + 4, :], in0=attn[:, 4 * b:4 * b + 4, :], in1=part[:, :, :], op=ALU.add))
                elif b == 0:
                    then(dve.tensor_copy(cross[:, :, :], src))

        @block.vector
        def _(dve):
            then = linker(dve, link)
            dve.wait_ge(K.small_loaded, loads)
            for t in (eq[:, :], ek[:, :], q_levels[:, :, :], k_levels[:, :, :]):
                then(dve.memset(t, 0.0))
            dve.wait_ge(*inputs.take())
            dve_abs(dve)
            dve_log(dve, cum)
            dve.wait_ge(*cum.posted())
            for h in range(4):
                then(dve.tensor_tensor_scan(out=c[:, h, :], data0=con["restart_row"][:, :], data1=lf[:, h, :],
                                            initial=0.0, op0=ALU.mult, op1=ALU.add))
            qf, kf, cf = flat(q[:, :, :]), flat(k[:, :, :]), flat(c[:, :, :])

            def halves(x, level):
                half, size = 2 ** level // 2, 2 ** level
                b = x.rearrange("p (b s) -> p b s", s=size)
                return b[:, :, 0:half], b[:, :, half:size], b[:, :, half - 1:half].to_broadcast([P, 4 * T // size, half])

            def exponents(level):
                left, right, middle = halves(cf, level)
                then(dve.tensor_tensor(out=halves(eq[:, :], level)[1], in0=right, in1=middle, op=ALU.subtract))
                dve.tensor_tensor(out=halves(ek[:, :], level)[0], in0=middle, in1=left, op=ALU.subtract).then_inc(*diffs.post())

            dve.tensor_copy(q_levels[:, 0, :], qf)
            dve.tensor_copy(k_levels[:, 0, :], kf).then_inc(*level_ready.post())
            exponents(1)
            for level in range(1, 9):
                ql, kl = q_levels[:, level % 2, :], k_levels[:, level % 2, :]
                dve.wait_ge(*exps.take())
                dve.tensor_tensor(out=halves(ql, level)[1], in0=halves(qf, level)[1], in1=halves(eq[:, :], level)[1], op=ALU.mult)
                dve.tensor_tensor(out=halves(kl, level)[0], in0=halves(kf, level)[0], in1=halves(ek[:, :], level)[0], op=ALU.mult)\
                   .then_inc(*level_ready.post())
                if level < 8:
                    dve.wait_ge(*level_ready.posted())
                    exponents(level + 1)
                add_level(dve, then, level - 1)
            add_level(dve, then, 8)
            dve.drain().then_inc(*attn_ready.post())
            dve.wait_ge(*o_ready.take())
            for b in range(2):
                then(dve.tensor_copy(flat(y[:, 2 * b:2 * b + 2, :]), bank[4 + b][:, :]))
            rms.dve(dve, link, normed)
            dve.wait_ge(*normed.posted())
            for h in range(4):
                then(dve.scalar_tensor_tensor(out=y[:, h, :], in0=y[:, h, :], scalar=col("hgrn_norm_w", h), in1=g[:, h, :],
                                              op0=ALU.mult, op1=ALU.mult))
    end_stage(K)


def conv(K, dve, then, x, out, n, w, b, T, x_ready):
    for j in range(n):
        dve.wait_ge(*x_ready.take())
        then(dve.tensor_scalar(out[:, j, :], x[:, j, 0:T], K.col(w, j), K.col(b, j), ALU.mult, ALU.add))
        for s in range(1, 4):
            then(dve.scalar_tensor_tensor(out=out[:, j, :], in0=x[:, j, s:s + T], scalar=K.col(w, s * n + j), in1=out[:, j, :],
                                          op0=ALU.mult, op1=ALU.add))


def mlstm_branch(K):
    nc, block, bank, col = K.nc, K.block, K.bank, K.col
    T = T1
    y = K.y_branch[:, 2]
    with ExitStack() as st:
        def sb(name, shape):
            return st.enter_context(nc.sbuf_tensor("mlstm_" + name, shape, F32))

        con = load_constants(K, st, "mlstm")
        wg, gb = sb("w_gates", [P, DT, 8]), sb("gate_bias", [4, 2])
        load(K, [(wg[:, :, :], K.dram["mlstm_w_gates"]), (gb[:, :], K.dram["mlstm_gate_bias"])])
        loads = 16 * K.small_loads
        z = sb("z", [P, 8, T + 3])
        qk = sb("qk", [P, 8, T])
        o = sb("o", [P, 4, T])
        v = sb("v", [P, 2, W])
        ig, fg, lf, fc, gs, mx = (sb(n, [4, T]) for n in ("i", "f", "log_f", "cum_f", "g", "max_g"))
        rows = sb("rows", [4, 2, T])
        g_cols = sb("g_cols", [P, 2, 4])
        mneg, emt = sb("neg_max", [P, 4, T]), sb("exp_neg_m", [P, 4, T])
        arg, wgt, s = sb("arg", [P, 8, T]), sb("weights", [P, 8, T]), sb("scores", [P, 8, T])
        den = sb("den", [P, 4, T])
        z_ready, z_free = new_signal(K, "ml_z_ready"), new_signal(K, "ml_z_free")
        v_ready, v_free = new_signal(K, "ml_v_ready"), new_signal(K, "ml_v_free")
        z_sb, convolved, qk_ready = z_free.reader(), new_signal(K, "ml_convolved"), new_signal(K, "ml_qk_ready")
        gate_ready, gate_free = new_signal(K, "ml_gate_ready"), new_signal(K, "ml_gate_free")
        rows_ready, minus_m, em, bc_ready, bc_done = (new_signal(K, "ml_" + n) for n in ("rows_ready", "m", "exp_m", "rows_everywhere", "rows_copied"))
        arg_ready, w_ready, s_ready, s_done, h_ready, h_done, normed = \
            (new_signal(K, "ml_" + n) for n in ("arg", "weights", "products", "scores", "sums", "sums_read", "normed"))
        link, alink, fdone = new_signal(K, "ml_dve_chain"), new_signal(K, "ml_act_chain"), new_signal(K, "ml_log_f")
        dve_abs, act_log, dve_log = log_sigmoid(K, st, "ml", fg[:, :], lf[:, :])
        ln = Norm(K, st, "ml", y, y, K.con["ones"][:, :], P, 1e-6)

        @block.tensor
        def _(pe):

            def side(n):
                if n == 3:
                    pe.wait_ge(K.small_loaded, loads)
                    for f in range(2):
                        for kt in range(DT):
                            ins = nc.tensor.matmul(bank[6 + f][0:4, 0:T], wg[:, kt, 4 * f:4 * f + 4], K.x[:, kt, 0:T],
                                                   start=kt == 0, stop=kt == DT - 1)
                        ins.then_inc(*gate_ready.post())

            stream_linear(K, pe, 12, lambda kt: K.x[:, kt, 0:T], DT, T, z_ready, z_free, side=side)
            pe.wait_ge(*rows_ready.take())
            for b in range(2):
                nc.tensor.transpose(bank[2][:, 4 * b:4 * b + 4], gs[:, b * P:(b + 1) * P], K.con["eye"][0:4, 0:4])
            for h in range(4):
                ins = nc.tensor.matmul(bank[4 + h][:, :], con["row_select"][0:4, h * P:(h + 1) * P], rows[:, :, :].rearrange("p a t -> p (a t)"),
                                       start=True, stop=True)
            ins.then_inc(*bc_ready.post())
            stream_tokens(K, pe, lambda kt: K.x[:, kt, :], [(0, P), (P, P)], 4, v_ready, v_free, (0, 1))
            pe.wait_ge(*qk_ready.take())
            pe.wait_ge(*bc_done.take())
            for h in range(4):
                for b in range(2):
                    ins = nc.tensor.matmul(bank[h][:, b * T:(b + 1) * T], qk[:, 4 + h, b * P:(b + 1) * P], qk[:, h, :], start=True, stop=True)
            ins.then_inc(*s_ready.post())
            pe.wait_ge(*s_done.take())
            for h in range(4):
                for b in range(2):
                    nc.tensor.matmul(bank[4 + h][:, 0:T], v[:, b, h * P:(h + 1) * P], s[:, 2 * h + b, :], start=b == 0, stop=b == 1)
                for b in range(2):
                    ins = nc.tensor.matmul(bank[4 + h][:, T:2 * T], K.con["ones"][:, :], s[:, 2 * h + b, :], start=b == 0, stop=b == 1)
            ins.then_inc(*h_ready.post())
            pe.wait_ge(*h_done.take())
            ln.pe(pe)

        @block.scalar
        def _(act):
            for j in range(12):
                act.wait_ge(*z_ready.take())
                if j < 8:
                    act.activation(z[:, j, 3:T + 3], bank[j % 4][:, 0:T], ACT.Copy).then_inc(*z_free.post())
                else:
                    act.activation(o[:, j - 8, :], bank[j % 4][:, 0:T], ACT.Sigmoid).then_inc(*z_free.post())
                if j == 2:
                    act.wait_ge(K.small_loaded, loads)
                    act.wait_ge(*gate_ready.take(2))
                    act.activation(ig[:, :], bank[6][0:4, 0:T], ACT.Identity, bias=gb[:, 0:1]).then_inc(*alink.post())
                    act.activation(fg[:, :], bank[7][0:4, 0:T], ACT.Identity, bias=gb[:, 1:2]).then_inc(*gate_free.post())
                elif j == 4:
                    act_log(act, alink)
                elif j == 6:
                    act.wait_ge(*minus_m.take())
                    act.activation(rows[:, 1, :], rows[:, 1, :], ACT.Exp).then_inc(*em.post())
            act.wait_ge(*convolved.take())
            act.activation(flat(qk[:, :, :]), flat(qk[:, :, :]), ACT.Silu).then_inc(*alink.post())
            act.wait_ge(*alink.posted())
            act.activation(flat(qk[:, 4:8, :]), flat(qk[:, 4:8, :]), ACT.Copy, scale=P ** -0.5).then_inc(*qk_ready.post())
            act.wait_ge(*arg_ready.take())
            for h in range(4):
                for b in range(2):
                    ins = act.activation(wgt[:, 2 * h + b, :], arg[:, 2 * h + b, :], ACT.Exp, bias=g_cols[:, b, h:h + 1])
            ins.then_inc(*w_ready.post())
            for b in range(2):
                act.wait_ge(*v_ready.take())
                act.activation(v[:, b, :], bank[b][:, :], ACT.Copy).then_inc(*v_free.post())
            ln.act(act)

        @block.vector
        def _(dve):
            then = linker(dve, link)
            then(dve.memset(z[:, :, 0:3], 0.0))
            dve.wait_ge(*gate_free.take())
            dve.wait_ge(K.small_loaded, loads)
            dve_abs(dve)
            dve_log(dve, fdone)
            dve.wait_ge(*fdone.posted())
            ones = K.con["ones"][0:4, 0:1].to_broadcast([4, T])
            then(dve.tensor_tensor_scan(out=fc[:, :], data0=ones, data1=lf[:, :], initial=0.0, op0=ALU.mult, op1=ALU.add))
            then(dve.tensor_tensor(out=gs[:, :], in0=ig[:, :], in1=fc[:, :], op=ALU.subtract))
            then(dve.tensor_tensor_scan(out=mx[:, :], data0=ones, data1=gs[:, :], initial=-3e38, op0=ALU.mult, op1=ALU.max))
            then(dve.tensor_scalar(rows[:, 0, :], mx[:, :], -1.0, None, ALU.mult))
            dve.tensor_tensor(out=rows[:, 1, :], in0=rows[:, 0, :], in1=fc[:, :], op=ALU.subtract).then_inc(*minus_m.post())
            dve.wait_ge(*em.take())
            dve.drain().then_inc(*rows_ready.post())
            conv(K, dve, then, z, qk, 8, "mlstm_conv_w", "mlstm_conv_b", T, z_sb)
            dve.drain().then_inc(*convolved.post())
            dve.wait_ge(*bc_ready.take())
            then(dve.tensor_copy(g_cols[:, :, :].rearrange("p a h -> p (a h)"), bank[2][:, 0:8]))
            for h in range(4):
                for b in range(2):
                    then(dve.tensor_tensor(out=arg[:, 2 * h + b, :], in0=bank[4 + h][:, 0:T], in1=con["mlstm_mask"][:, b * T:(b + 1) * T], op=ALU.add))
                then(dve.tensor_copy(emt[:, h, :], bank[4 + h][:, T:2 * T]))
            dve.drain().then_inc(*arg_ready.post())
            dve.drain().then_inc(*bc_done.post())
            dve.wait_ge(*s_ready.take())
            dve.wait_ge(*w_ready.take())
            for h in range(4):
                ins = dve.tensor_tensor(out=flat(s[:, 2 * h:2 * h + 2, :]), in0=bank[h][:, :], in1=flat(wgt[:, 2 * h:2 * h + 2, :]), op=ALU.mult)
            ins.then_inc(*s_done.post())
            dve.wait_ge(*h_ready.take())
            for h in range(4):
                then(dve.tensor_copy(den[:, h, :], bank[4 + h][:, T:2 * T]))
                then(dve.scalar_tensor_tensor(out=den[:, h, :], in0=den[:, h, :], scalar=-1.0, in1=den[:, h, :], op0=ALU.mult, op1=ALU.max))
            then(dve.tensor_tensor(out=den[:, :, :], in0=den[:, :, :], in1=emt[:, :, :], op=ALU.max))
            then(dve.reciprocal(den[:, :, :], den[:, :, :]))
            for h in range(4):
                then(dve.tensor_tensor(out=y[:, h, :], in0=bank[4 + h][:, 0:T], in1=den[:, h, :], op=ALU.mult))
            dve.drain().then_inc(*h_done.post())
            ln.dve(dve, link, normed)
            dve.wait_ge(*normed.posted())
            for h in range(4):
                then(dve.scalar_tensor_tensor(out=y[:, h, :], in0=y[:, h, :], scalar=col("mlstm_norm_w", h), in1=o[:, h, :],
                                              op0=ALU.mult, op1=ALU.mult))
    end_stage(K)


def lru_branch(K):
    nc, block, bank, col = K.nc, K.block, K.bank, K.col
    T = T1
    y = K.y_branch[:, 3]
    with ExitStack() as st:
        def sb(name, shape):
            return st.enter_context(nc.sbuf_tensor("lru_" + name, shape, F32))

        wx = sb("wx_wa", [P, 8, P])
        load(K, [(wx[:, :, :], K.dram["lru_w"])])
        loads = 16 * K.small_loads
        z, xc = sb("z", [P, 4, T + 3]), sb("convolved", [P, 4, T])
        gelu, gx, ga = sb("gelu", [P, 4, T]), sb("gate_x", [P, 4, T]), sb("gate_a", [P, 4, T])
        a, m, r = sb("a", [P, 4, T]), sb("mult", [P, 4, T]), sb("r", [P, 4, T])
        ls = sb("log_sig_lambda", [P, 4])
        z_ready, z_free, convolved = (new_signal(K, "lr_" + n) for n in ("z_ready", "z_free", "convolved"))
        z_sb = z_free.reader()
        g_ready, g_free, g_sb = new_signal(K, "lr_gates_ready"), new_signal(K, "lr_gates_free"), new_signal(K, "lr_gates_sb")
        la, exps, var, root = (new_signal(K, "lr_" + n) for n in ("log_a", "exps", "one_minus", "root"))
        link, alink, ldone = new_signal(K, "lr_dve_chain"), new_signal(K, "lr_act_chain"), new_signal(K, "lr_lambda")
        lam = K.cols[:, COL_AT["lru_lambda"]:COL_AT["lru_lambda"] + 4]
        dve_abs, act_log, dve_log = log_sigmoid(K, st, "lr", lam, ls[:, :])

        @block.tensor
        def _(pe):

            def gate(j):
                if j >= 4:
                    pe.wait_ge(*g_free.take())
                nc.tensor.matmul(bank[4 + j % 4][:, 0:T], wx[:, j, :], xc[:, j % 4, :], start=True, stop=True).then_inc(*g_ready.post())

            def side(n):
                if n == 12:
                    pe.wait_ge(K.small_loaded, loads)
                    pe.wait_ge(*convolved.take())
                if n >= 12:
                    gate(n - 12)

            stream_linear(K, pe, 8, lambda kt: K.x[:, kt, 0:T], DT, T, z_ready, z_free, side=side)
            for j in range(4, 8):
                gate(j)
            pe.wait_ge(*g_free.take(4))

        @block.scalar
        def _(act):
            act_log(act, alink)
            for j in range(8):
                act.wait_ge(*z_ready.take())
                if j < 4:
                    act.activation(z[:, j, 3:T + 3], bank[j % 4][:, 0:T], ACT.Copy).then_inc(*z_free.post())
                else:
                    act.activation(gelu[:, j - 4, :], bank[j % 4][:, 0:T], ACT.Gelu_apprx_tanh).then_inc(*z_free.post())
            for j in range(8):
                act.wait_ge(*g_ready.take())
                act.activation((gx if j < 4 else ga)[:, j % 4, :], bank[4 + j % 4][:, 0:T], ACT.Sigmoid,
                               bias=col("lru_bx" if j < 4 else "lru_ba", j % 4)).then_inc(*g_free.post())
            act.drain().then_inc(*g_sb.post())
            act.wait_ge(*la.take())
            act.activation(flat(m[:, :, :]), flat(a[:, :, :]), ACT.Tanh).then_inc(*alink.post())
            act.wait_ge(*alink.posted())
            act.activation(flat(a[:, :, :]), flat(a[:, :, :]), ACT.Exp).then_inc(*exps.post())
            act.wait_ge(*var.take())
            act.activation(flat(m[:, :, :]), flat(m[:, :, :]), ACT.Sqrt).then_inc(*root.post())

        @block.vector
        def _(dve):
            then = linker(dve, link)
            dve_abs(dve)
            dve_log(dve, ldone)
            dve.wait_ge(*ldone.posted())
            then(dve.memset(z[:, :, 0:3], 0.0))
            conv(K, dve, then, z, xc, 4, "lru_conv_w", "lru_conv_b", T, z_sb)
            dve.drain().then_inc(*convolved.post())
            dve.wait_ge(*g_sb.take())
            for j in range(4):
                then(dve.tensor_scalar(a[:, j, :], ga[:, j, :], ls[:, j:j + 1], 8.0, ALU.mult, ALU.mult))
            dve.drain().then_inc(*la.post())
            then(dve.tensor_tensor(out=gx[:, :, :], in0=gx[:, :, :], in1=xc[:, :, :], op=ALU.mult))
            dve.wait_ge(*exps.take())
            then(dve.tensor_scalar(r[:, :, :], m[:, :, :], -1.0, 1.0, ALU.mult, ALU.add))
            then(dve.reciprocal(r[:, :, :], r[:, :, :]))
            dve.scalar_tensor_tensor(out=m[:, :, :], in0=m[:, :, :], scalar=-2.0, in1=r[:, :, :], op0=ALU.mult, op1=ALU.mult).then_inc(*var.post())
            dve.wait_ge(*root.take())
            then(dve.memset(m[:, :, 0:1], 1.0))
            then(dve.tensor_tensor(out=m[:, :, :], in0=m[:, :, :], in1=gx[:, :, :], op=ALU.mult))
            for j in range(4):
                then(dve.tensor_tensor_scan(out=r[:, j, :], data0=a[:, j, :], data1=m[:, j, :], initial=0.0, op0=ALU.mult, op1=ALU.add))
            then(dve.tensor_tensor(out=y, in0=r[:, :, :], in1=gelu[:, :, :], op=ALU.mult))
    end_stage(K)


def merge(K):
    nc, block, bank, col = K.nc, K.block, K.bank, K.col
    T = T1
    with ExitStack() as st:
        def sb(name, shape):
            return st.enter_context(nc.sbuf_tensor("merge_" + name, shape, F32))

        gate, prod = sb("gate", [P, 2, T]), sb("product", [P, 2, T])
        merged = sb("merged", [P, DT, T])
        g_ready, b_ready, g_sb, b_free = (new_signal(K, "mg_" + n) for n in ("gate_ready", "branch_ready", "gate_sb", "branch_free"))
        p_free, merged_ready, o_ready, o_free, normed = (new_signal(K, "mg_" + n) for n in ("gate_free", "merged", "out_ready", "out_free", "normed"))
        link = new_signal(K, "mg_dve_chain")
        g_free = g_sb.reader()
        x = K.x[:, :, 0:T]
        ln = Norm(K, st, "l1", x, x, K.con["ones"][:, :], D, 1e-5, whole=True)

        @block.tensor
        def _(pe):
            for i in range(4 * DT):
                if i >= 2:
                    pe.wait_ge(*g_free.take())
                for k in range(DT):
                    matmul(K, bank[i % 2][:, 0:T], K.weights.take(pe), K.x[:, k, 0:T], k == 0, k == DT - 1, g_ready if k == DT - 1 else None)
                if i >= 2:
                    pe.wait_ge(*b_free.take())
                for k in range(WT):
                    matmul(K, bank[2 + i % 2][:, 0:T], K.weights.take(pe), K.y_branch[:, i % 4, k, :], k == 0, k == WT - 1,
                           b_ready if k == WT - 1 else None)
            pe.wait_ge(*g_free.take(2))
            pe.wait_ge(*b_free.take(2))
            pe.wait_ge(*merged_ready.take())
            stream_linear(K, pe, DT, lambda k: merged[:, k, :], DT, T, o_ready, o_free)
            ln.pe(pe)

        @block.scalar
        def _(act):
            for i in range(4 * DT):
                act.wait_ge(*g_ready.take())
                if i >= 2:
                    act.wait_ge(*p_free.take())
                act.activation(gate[:, i % 2, :], bank[i % 2][:, 0:T], ACT.Sigmoid).then_inc(*g_sb.post())
            act.wait_ge(*p_free.take(2))
            ln.act(act)

        @block.vector
        def _(dve):
            then = linker(dve, link)
            for i in range(4 * DT):
                d, n = divmod(i, 4)
                dve.wait_ge(*g_sb.take())
                dve.wait_ge(*b_ready.take())
                dst = merged[:, d, :] if n == 0 else prod[:, i % 2, :]
                dve.tensor_tensor(out=dst, in0=bank[2 + i % 2][:, 0:T], in1=gate[:, i % 2, :], op=ALU.mult).then_inc(*b_free.post())
                dve.wait_ge(*b_free.posted())
                if n:
                    ins = dve.tensor_tensor(out=merged[:, d, :], in0=merged[:, d, :], in1=prod[:, i % 2, :], op=ALU.add)
                else:
                    ins = dve.engine_nop()
                ins.then_inc(*p_free.post())
                dve.wait_ge(*p_free.posted())
            dve.drain().then_inc(*merged_ready.post())
            for j in range(DT):
                dve.wait_ge(*o_ready.take())
                dve.scalar_tensor_tensor(out=x[:, j, :], in0=x[:, j, :], scalar=ALPHA, in1=bank[j % 4][:, 0:T], op0=ALU.mult, op1=ALU.add)\
                    .then_inc(*o_free.post())
            dve.wait_ge(*o_free.posted())
            ln.dve(dve, link, normed)
            dve.wait_ge(*normed.posted())
            for j in range(DT):
                then(dve.tensor_scalar(x[:, j, :], x[:, j, :], col("ln1_g", j), col("ln1_b", j), ALU.mult, ALU.add))
    end_stage(K)


def router_and_ple(K):
    nc, block, bank = K.nc, K.block, K.bank
    T = T1
    with ExitStack() as st:
        def sb(name, shape):
            return st.enter_context(nc.sbuf_tensor("router_" + name, shape, F32))

        rw, rb = sb("w", [P, DT, NE]), sb("bias", [P, NE])
        p_in, bd = sb("p", [P, 2, T]), sb("b_down", [NE, D])
        load(K, [(rw[:, :, :], K.dram["router_w"]), (rb[:, :], K.dram["router_b"]), (p_in[:, :, :], K.dram["p"]),
                 (bd[:, :], K.dram["expert_b_down"])])
        logits, rest, e = sb("logits", [P, 2, NE]), sb("rest", [P, 2, NE]), sb("exp", [P, 2, NE])
        top, first, total = sb("top", [P, 2, 8]), sb("neg_first", [P, 2]), sb("total", [P, 2])
        sig = sb("ple_gate", [P, DT, T])
        lg_ready, shifted, exps, gates_rows, turned, gates_ready = \
            (new_signal(K, "rt_" + n) for n in ("logits", "top", "exps", "gates", "turned", "gates_in_place"))
        chosen, placed, rows_ready, rows_done = (new_signal(K, "rt_" + n) for n in ("chosen", "places", "token_rows", "rows_copied"))
        con = load_constants(K, st, "router")
        loads = 16 * K.small_loads
        g_ready, g_free, p_ready, p_free, b_ready, b_free = \
            (new_signal(K, "rt_" + n) for n in ("ple_gate_ready", "ple_gate_free", "ple_ready", "ple_free", "bias_ready", "bias_free"))
        link = new_signal(K, "rt_dve_chain")
        sig_sb = g_free.reader()

        @block.tensor
        def _(pe):
            pe.wait_ge(K.small_loaded, loads)
            for b in range(2):
                for k in range(DT):
                    ins = nc.tensor.matmul(bank[4 + b][:, 0:NE], K.x[:, k, b * P:(b + 1) * P], rw[:, k, :], start=k == 0, stop=k == DT - 1)
                ins.then_inc(*lg_ready.post())
            stream_linear(K, pe, DT, lambda k: K.x[:, k, 0:T], DT, T, g_ready, g_free)
            stream_linear(K, pe, DT, lambda k: p_in[:, k, :], 2, T, p_ready, p_free)
            for b in range(2):
                for half in range(2):
                    for k in range(4):
                        ins = nc.tensor.transpose(bank[4 + half][:, k * P:(k + 1) * P], K.x[:, 4 * half + k, b * P:(b + 1) * P], K.con["eye"][:, :])
                ins.then_inc(*rows_ready.post())
                pe.wait_ge(*rows_done.take())
            pe.wait_ge(*chosen.take())
            nc.tensor.matmul(bank[6][:, 0:NE], con["before"][:, :], K.chosen[:, 0, 0:NE], start=True, stop=True)
            nc.tensor.matmul(bank[6][:, NE:2 * NE], K.con["ones"][:, :], K.chosen[:, 0, 0:NE], start=True, stop=False)
            nc.tensor.matmul(bank[6][:, NE:2 * NE], con["before"][:, :], K.chosen[:, 1, 0:NE], start=False, stop=True)
            for b in range(2):
                ins = nc.tensor.matmul(bank[6][:, 2 * NE:3 * NE], K.con["ones"][:, :], K.chosen[:, b, 0:NE], start=b == 0, stop=b == 1)
            ins.then_inc(*placed.post())
            pe.wait_ge(*gates_rows.take())
            for b in range(2):
                ins = nc.tensor.transpose(bank[4][0:NE, b * P:(b + 1) * P], K.gates_rows[:, b, 0:NE], K.con["eye"][:, :])
            ins.then_inc(*turned.post())
            pe.wait_ge(*gates_ready.take())
            for j in range(DT):
                if j >= 4:
                    pe.wait_ge(*b_free.take())
                nc.tensor.matmul(bank[j % 4][:, 0:T], bd[:, j * P:(j + 1) * P], K.gates[:, :], start=True, stop=True).then_inc(*b_ready.post())
            pe.wait_ge(*b_free.take(4))

        @block.scalar
        def _(act):
            act.wait_ge(*shifted.take())
            for b in range(2):
                ins = act.activation(e[:, b, :], logits[:, b, :], ACT.Exp, bias=first[:, b:b + 1])
            ins.then_inc(*exps.post())
            for j in range(DT):
                act.wait_ge(*g_ready.take())
                act.activation(sig[:, j, :], bank[j % 4][:, 0:T], ACT.Sigmoid).then_inc(*g_free.post())
            for b in range(2):
                act.wait_ge(*rows_ready.take())
                act.activation(K.x_rows[:, b, 0:512], bank[4][:, :], ACT.Copy)
                act.activation(K.x_rows[:, b, 512:1024], bank[5][:, :], ACT.Copy).then_inc(*rows_done.post())

        @block.vector
        def _(dve):
            then = linker(dve, link)
            dve.wait_ge(K.small_loaded, loads)
            dve.wait_ge(*lg_ready.take(2))
            for b in range(2):
                then(dve.tensor_tensor(out=logits[:, b, :], in0=bank[4 + b][:, 0:NE], in1=rb[:, :], op=ALU.add))
                then(dve.max(top[:, b, :], logits[:, b, :]))
                then(dve.tensor_scalar(first[:, b:b + 1], top[:, b, 0:1], -1.0, None, ALU.mult))
                then(dve.memset(top[:, b, 4:8], -3e38))
                then(dve.match_replace(rest[:, b, :], in_to_replace=top[:, b, :], in_values=logits[:, b, :], imm_value=-3e38))
            dve.tensor_tensor(out=K.chosen[:, :, 0:NE], in0=rest[:, :, :], in1=logits[:, :, :], op=ALU.not_equal).then_inc(*chosen.post())
            dve.wait_ge(*chosen.posted())
            dve.drain().then_inc(*shifted.post())
            dve.wait_ge(*exps.take())
            then(dve.tensor_tensor(out=e[:, :, :], in0=e[:, :, :], in1=K.chosen[:, :, 0:NE], op=ALU.mult))
            then(dve.tensor_reduce(out=total[:, :], in_=e[:, :, :], axis=AX.X, op=ALU.add))
            then(dve.reciprocal(total[:, :], total[:, :]))
            for b in range(2):
                ins = dve.tensor_scalar(K.gates_rows[:, b, 0:NE], e[:, b, :], total[:, b:b + 1], None, ALU.mult)
            ins.then_inc(*gates_rows.post())
            for j in range(DT):
                dve.wait_ge(*sig_sb.take())
                dve.wait_ge(*p_ready.take())
                dve.tensor_tensor(out=sig[:, j, :], in0=sig[:, j, :], in1=bank[j % 4][:, 0:T], op=ALU.mult).then_inc(*p_free.post())
            dve.wait_ge(*p_free.posted())
            then(dve.scalar_tensor_tensor(out=K.acc[:, :, :], in0=K.x[:, :, 0:T], scalar=ALPHA, in1=sig[:, :, :], op0=ALU.mult, op1=ALU.add))
            dve.wait_ge(*placed.take())
            then(dve.tensor_copy(K.place[:, :, 0:NE], bank[6][:, 0:2 * NE].rearrange("p (b e) -> p b e", b=2)))
            for t in (K.chosen, K.place, K.gates_rows):
                then(dve.memset(t[:, :, NE:NE + 1], 0.0))
            then(dve.tensor_copy(K.load_of[:, :], bank[6][:, 2 * NE:3 * NE]))
            dve.wait_ge(*turned.take())
            dve.tensor_copy(K.gates[:, :], bank[4][0:NE, 0:T]).then_inc(*gates_ready.post())
            for j in range(DT):
                dve.wait_ge(*b_ready.take())
                dve.tensor_tensor(out=K.acc[:, j, :], in0=K.acc[:, j, :], in1=bank[j % 4][:, 0:T], op=ALU.add).then_inc(*b_free.post())
    end_stage(K)


def experts(K):
    nc, block, bank = K.nc, K.block, K.bank
    T, S, HW = T1, SLOTS_SMALL, D // 2
    with ExitStack() as st:
        def sb(name, shape):
            return st.enter_context(nc.sbuf_tensor("expert_" + name, shape, F32))

        con = load_constants(K, st, "experts")
        bgu = sb("b_gu", [NE, 2 * D])
        load(K, [(bgu[:, :], K.dram["expert_b_gu"])])
        loads = 16 * K.small_loads
        sel = sb("select", [NE, P])
        pick, spread = sb("pick", [P, 2, S]), sb("spread_rows", [P, 2, 2, S])
        spread_t, xs, xt = sb("spread", [P, T]), sb("x_slots", [P, HW]), sb("x_slots_t", [P, 4, P])
        ht_few, ys = sb("hidden_slots_t", [P, 4, P]), sb("y_slots", [P, HW])
        gate, sg, h = sb("gate_part", [P, 4, HW]), sb("sigmoid", [P, 4, HW]), sb("hidden", [P, 4, HW])
        ht, pad = sb("hidden_t", [P, DT, T]), sb("pad", [P, 8])
        sel_ready, pick_ready, spread_ready, gathered, xs_sb, xt_ready, xt_sb, gate_ready, up_ready, gate_sb, sig_ready, h_ready, ht_ready, ht_sb, y_ready, ys_sb, \
            out_ready, link = (new_signal(K, "ex_" + n) for n in (
                "select", "pick", "spread", "gathered", "x_slots_sb", "x_turned", "x_turned_sb", "gate_ready", "up_ready", "gate_sb", "sigmoid", "hidden",
                "hidden_turned", "hidden_turned_sb", "y_ready", "y_slots_sb", "out_ready", "dve_chain"))
        assert K.weights.at % (CHUNK_TILES * SLOTS) == 0
        LINKS = 6
        rows = (slice(0, S), slice(S, 2 * S))

        def both(eng, i, signals, body):
            tokens = eng.value_load(K.load_of[0:1, bass.ds(i, 1)], min_val=0, max_val=T)
            saved, at, pending = counters(signals), K.weights.at, K.weights.pending
            with eng.If(tokens < FEW + 1):
                body(True)
            ended = counters(signals)
            set_counters(signals, saved)
            if eng is nc.tensor:
                K.weights.at, K.weights.pending = at, pending
            with eng.Else():
                body(False)
            assert counters(signals) == ended, (counters(signals), ended)

        def few_linear(pe, out, x, bias, signal):
            for g in range(2):
                if bias is not None:
                    matmul(K, out[rows[g], :], sel[:, 0:S], bgu[:, bias + g * HW:bias + (g + 1) * HW], True, False)
            for k in range(DT):
                w = K.weights.take(pe, DT)
                for g in range(2):
                    matmul(K, out[rows[g], :], x[:, k % 4, k // 4 * S:k // 4 * S + S], w[:, g * HW:(g + 1) * HW],
                           bias is None and k == 0, k == DT - 1, signal if g and k == DT - 1 else None)

        def many_linear(pe, out, x, bias, signal):
            for b in range(2):
                for g in range(2):
                    if bias is not None:
                        matmul(K, bank[out + 2 * b + g][:, :], sel[:, :], bgu[:, bias + g * HW:bias + (g + 1) * HW], True, False)
            for k in range(DT):
                w = K.weights.take(pe, DT)
                for b in range(2):
                    for g in range(2):
                        matmul(K, bank[out + 2 * b + g][:, :], x(k)[:, b * P:(b + 1) * P], w[:, g * HW:(g + 1) * HW],
                               bias is None and k == 0, k == DT - 1, signal if b and g and k == DT - 1 else None)

        @block.tensor
        def _(pe):
            eye = K.con["eye"][:, :]

            def gather_next(pe):
                pe.wait_ge(*pick_ready.take())
                for b in range(2):
                    for g in range(2):
                        ins = nc.tensor.matmul(bank[3][rows[g], :], pick[:, b, :], K.x_rows[:, b, g * HW:(g + 1) * HW], start=b == 0, stop=b == 1)
                ins.then_inc(*gathered.post())

            def turn_next(pe):
                pe.wait_ge(*xs_sb.take())
                for j in range(4):
                    ins = nc.tensor.transpose(bank[4][:, j * P:(j + 1) * P], xs[:, j * P:(j + 1) * P], eye)
                ins.then_inc(*xt_ready.post())

            def few(pe):
                pe.wait_ge(*sel_ready.take())
                pe.wait_ge(*xt_sb.take())
                few_linear(pe, bank[0], xt, 0, gate_ready)
                few_linear(pe, bank[1], xt, D, up_ready)
                pe.wait_ge(*spread_ready.take())
                for b in range(2):
                    nc.tensor.transpose(bank[2][:, b * P:(b + 1) * P], spread[:, b, :, :].rearrange("p a s -> p (a s)"), eye)
                gather_next(pe)
                pe.wait_ge(*h_ready.take())
                for j in range(4):
                    ins = nc.tensor.transpose(bank[5][:, j * P:(j + 1) * P], h[:, 0, j * P:(j + 1) * P], eye)
                ins.then_inc(*ht_ready.post())
                turn_next(pe)
                pe.wait_ge(*ht_sb.take())
                few_linear(pe, bank[2], ht_few, None, y_ready)
                pe.wait_ge(*ys_sb.take())
                for b in range(2):
                    for g in range(2):
                        ins = nc.tensor.matmul(bank[4 + 2 * b + g][:, :], spread_t[rows[g], b * P:(b + 1) * P], ys[rows[g], :], start=True, stop=True)
                ins.then_inc(*out_ready.post())

            def many(pe):
                pe.wait_ge(*sel_ready.take())
                pe.wait_ge(*xt_sb.take())
                many_linear(pe, 0, lambda k: K.x[:, k, 0:T], 0, gate_ready)
                pe.wait_ge(*spread_ready.take())
                many_linear(pe, 4, lambda k: K.x[:, k, 0:T], D, up_ready)
                pe.wait_ge(*h_ready.take())
                gather_next(pe)
                turn_next(pe)
                for b in range(2):
                    for k in range(DT):
                        ins = nc.tensor.transpose(bank[2 * b + k // 4][:, k % 4 * P:(k % 4 + 1) * P], h[:, 2 * b + k // 4, k % 4 * P:(k % 4 + 1) * P], eye)
                ins.then_inc(*ht_ready.post())
                pe.wait_ge(*ht_sb.take())
                many_linear(pe, 4, lambda k: ht[:, k, :], None, y_ready)
                pe.wait_ge(*ys_sb.take())
                pe.nop().then_inc(*out_ready.post())

            taken = [(sel_ready, 1), (xs_sb, 1), (xt_sb, 1), (spread_ready, 1), (pick_ready, 1), (h_ready, 1), (ht_sb, 1), (ys_sb, 1)]
            posted = [gathered, xt_ready, gate_ready, up_ready, ht_ready, y_ready, out_ready]
            pe.wait_ge(K.small_loaded, loads)
            gather_next(pe)
            turn_next(pe)
            with pe.Fori(0, NE) as i:
                for q, n in taken:
                    q.begin(i, n)
                K.weights.turn = (i, EXPERT_TILES // CHUNK_TILES // SLOTS)
                both(pe, i, [q for q, _ in taken] + posted, lambda is_few: few(pe) if is_few else many(pe))
                K.weights.turn = None
                for q, _ in taken:
                    q.end(NE)
            K.weights.at += EXPERT_TILES * (NE - 1)

        @block.scalar
        def _(act):
            def copy_next(act):
                act.wait_ge(*xt_ready.take())
                act.activation(flat(xt[:, :, :]), bank[4][:, :], ACT.Copy).then_inc(*xt_sb.post())

            def few(act):
                act.wait_ge(*gate_sb.take())
                act.activation(sg[:, 0, :], gate[:, 0, :], ACT.Sigmoid, scale=1.702).then_inc(*sig_ready.post())
                act.wait_ge(*ht_ready.take())
                act.activation(flat(ht_few[:, :, :]), bank[5][:, :], ACT.Copy).then_inc(*ht_sb.post())
                copy_next(act)
                act.wait_ge(*y_ready.take())
                act.activation(ys[:, :], bank[2][:, :], ACT.Copy).then_inc(*ys_sb.post())

            def many(act):
                act.wait_ge(*gate_sb.take())
                act.activation(flat(sg[:, :, :]), flat(gate[:, :, :]), ACT.Sigmoid, scale=1.702).then_inc(*sig_ready.post())
                copy_next(act)
                act.wait_ge(*ht_ready.take())
                for b in range(2):
                    for half in range(2):
                        ins = act.activation(ht[:, 4 * half:4 * half + 4, b * P:(b + 1) * P],
                                             bank[2 * b + half][:, :].rearrange("p (k t) -> p k t", t=P), ACT.Copy)
                ins.then_inc(*ht_sb.post())
                act.wait_ge(*y_ready.take())
                act.nop().then_inc(*ys_sb.post())

            taken = [(xt_ready, 1), (gate_sb, 1), (ht_ready, 1), (y_ready, 1)]
            copy_next(act)
            with act.Fori(0, NE) as i:
                for q, n in taken:
                    q.begin(i, n)
                both(act, i, [q for q, _ in taken] + [xt_sb, sig_ready, ht_sb, ys_sb], lambda is_few: few(act) if is_few else many(act))
                for q, _ in taken:
                    q.end(NE)

        @block.vector
        def _(dve):
            then = linker(dve, link)
            dve.wait_ge(K.small_loaded, loads)
            then(dve.memset(K.moe[:, :, :], 0.0))

            def even_out(dve, before):
                while link.posts < before + LINKS:
                    dve.memset(pad[:, link.posts - before:link.posts - before + 1], 0.0).then_inc(*link.post())

            def pick_next(dve, e):
                for b in range(2):
                    ins = dve.tensor_scalar(pick[:, b, :], con["slots"][:, :], K.place[:, b, e], K.chosen[:, b, e], ALU.is_equal, ALU.mult)
                ins.then_inc(*pick_ready.post())

            def select_next(dve, e):
                dve.tensor_copy(sel[:, :], K.con["eye"][0:NE, e].to_broadcast([NE, P])).then_inc(*sel_ready.post())

            def few(dve, e, after):
                before = link.posts
                pick_next(dve, after)
                for b in range(2):
                    slots = con["slots"][:, :].rearrange("p (a s) -> p a s", a=1).to_broadcast([P, 2, S])
                    ins = dve.tensor_scalar(spread[:, b, :, :], slots, K.place[:, b, e], K.gates_rows[:, b, e], ALU.is_equal, ALU.mult)
                ins.then_inc(*spread_ready.post())
                dve.wait_ge(*gate_ready.take())
                dve.tensor_scalar(gate[:, 0, :], bank[0][:, :], 7.0, None, ALU.min).then_inc(*gate_sb.post())
                dve.wait_ge(*sig_ready.take())
                then(dve.tensor_tensor(out=gate[:, 0, :], in0=gate[:, 0, :], in1=sg[:, 0, :], op=ALU.mult))
                dve.wait_ge(*up_ready.take())
                then(dve.tensor_scalar(h[:, 0, :], bank[1][:, :], 7.0, -7.0, ALU.min, ALU.max))
                dve.scalar_tensor_tensor(out=h[:, 0, :], in0=h[:, 0, :], scalar=1.0, in1=gate[:, 0, :], op0=ALU.add, op1=ALU.mult)\
                   .then_inc(*h_ready.post())
                dve.wait_ge(*gathered.take())
                dve.tensor_copy(spread_t[:, :], bank[2][:, 0:T])
                dve.tensor_copy(xs[:, :], bank[3][:, :]).then_inc(*xs_sb.post())
                select_next(dve, after)
                dve.wait_ge(*out_ready.take())
                for n in range(4):
                    part = K.moe[:, n // 2, n % 2 * HW:(n % 2 + 1) * HW]
                    ins = dve.tensor_tensor(out=part, in0=part, in1=bank[4 + n][:, :], op=ALU.add)
                then(ins)
                even_out(dve, before)

            def many(dve, e, after):
                before = link.posts
                pick_next(dve, after)
                dve.memset(pad[:, 0:1], 0.0).then_inc(*spread_ready.post())
                dve.wait_ge(*gate_ready.take())
                for n in range(4):
                    ins = dve.tensor_scalar(gate[:, n, :], bank[n][:, :], 7.0, None, ALU.min)
                ins.then_inc(*gate_sb.post())
                dve.wait_ge(*sig_ready.take())
                then(dve.tensor_tensor(out=flat(gate[:, :, :]), in0=flat(gate[:, :, :]), in1=flat(sg[:, :, :]), op=ALU.mult))
                dve.wait_ge(*up_ready.take())
                for n in range(4):
                    ins = dve.tensor_scalar(h[:, n, :], bank[4 + n][:, :], 7.0, -7.0, ALU.min, ALU.max)
                then(ins)
                dve.scalar_tensor_tensor(out=flat(h[:, :, :]), in0=flat(h[:, :, :]), scalar=1.0, in1=flat(gate[:, :, :]), op0=ALU.add, op1=ALU.mult)\
                   .then_inc(*h_ready.post())
                dve.wait_ge(*gathered.take())
                dve.tensor_copy(xs[:, :], bank[3][:, :]).then_inc(*xs_sb.post())
                select_next(dve, after)
                dve.wait_ge(*out_ready.take())
                for n in range(4):
                    part = K.moe[:, n // 2, n % 2 * HW:(n % 2 + 1) * HW]
                    ins = dve.scalar_tensor_tensor(out=part, in0=bank[4 + n][:, :], scalar=K.gates_rows[:, n // 2, e], in1=part,
                                                   op0=ALU.mult, op1=ALU.add)
                then(ins)
                even_out(dve, before)

            taken = [(gathered, 1), (gate_ready, 1), (sig_ready, 1), (up_ready, 1), (out_ready, 1)]
            pick_next(dve, slice(0, 1))
            select_next(dve, slice(0, 1))
            dve.wait_ge(*gathered.take())
            dve.tensor_copy(xs[:, :], bank[3][:, :]).then_inc(*xs_sb.post())
            with dve.Fori(0, NE) as i:
                e, after = bass.ds(i, 1), bass.ds(i + 1, 1)
                for q, n in taken:
                    q.begin(i, n)
                link.begin(i, LINKS, posts=True)
                both(dve, i, [q for q, _ in taken] + [link, sel_ready, pick_ready, spread_ready, xs_sb, gate_sb, h_ready],
                     lambda is_few: few(dve, e, after) if is_few else many(dve, e, after))
                for q, _ in taken:
                    q.end(NE)
                link.end(NE, posts=True)
    end_stage(K)


def second_norm(K):
    nc, block, bank, col = K.nc, K.block, K.bank, K.col
    with ExitStack() as st:
        ln = Norm(K, st, "l2", K.acc[:, :, :], K.acc[:, :, :], K.con["ones"][:, :], D, 1e-5, whole=True)
        link, normed = new_signal(K, "l2_dve_chain"), new_signal(K, "l2_normed")
        load(K, [(K.x[:, :, 0:META], K.dram["meta"])])
        loads = 16 * K.small_loads

        turned, x_new = new_signal(K, "l2_turned"), new_signal(K, "l2_x")

        @block.tensor
        def _(pe):
            for j in range(DT):
                for b in range(2):
                    ins = nc.tensor.transpose(bank[j // 2][:, j % 2 * T1 + b * P:j % 2 * T1 + (b + 1) * P], K.moe[:, b, j * P:(j + 1) * P],
                                              K.con["eye"][:, :])
                if j % 2:
                    ins.then_inc(*turned.post())
            ln.pe(pe)
            for j in range(DT):
                K.rms.gather(pe, j)

        @block.scalar
        def _(act):
            ln.act(act)
            act.wait_ge(K.small_loaded, loads)
            for j in range(DT):
                act.wait_ge(*x_new.take())
                K.rms.square(act, j)

        @block.vector
        def _(dve):
            then = linker(dve, link)
            for j in range(4):
                dve.wait_ge(*turned.take())
                part = flat(K.acc[:, 2 * j:2 * j + 2, :])
                then(dve.tensor_tensor(out=part, in0=part, in1=bank[j][:, :], op=ALU.add))
            ln.dve(dve, link, normed)
            dve.wait_ge(*normed.posted())
            for j in range(DT):
                dve.tensor_scalar(K.x[:, j, META:T2], K.acc[:, j, :], col("ln2_g", j), col("ln2_b", j), ALU.mult, ALU.add)\
                   .then_inc(*x_new.post())
            dve.wait_ge(K.small_loaded, loads)
    end_stage(K)


class RmsOfX:

    def __init__(self, K, ctx):
        self.K = K
        self.sq, self.rstd = (ctx.enter_context(K.nc.sbuf_tensor(n, s, F32)) for n, s in (("x_squares", [P, 2, T2]), ("x_rms", [P, T2])))
        self.squared, self.summed, self.var, self.root, self.inverse, self.hn_ready = \
            (Signal(K.new_semaphore("x_" + n)) for n in ("squared", "summed", "var", "root", "inverse", "hn"))
        self.sq_used = self.summed.reader()

    def square(self, act, j):
        used = self.sq_used.take()
        if j >= 2:
            act.wait_ge(used[0], used[1] - 2)
        act.activation(self.sq[:, j % 2, :], self.K.x[:, j, :], ACT.Square).then_inc(*self.squared.post())

    def gather(self, pe, j):
        pe.wait_ge(*self.squared.take())
        self.K.nc.tensor.matmul(self.K.bank[6][:, 0:T2], self.K.con["ones"][:, :], self.sq[:, j % 2, :], start=j == 0, stop=j == DT - 1)\
            .then_inc(*self.summed.post())

    def beside(self, pe):
        def side(n):
            if n >= 2 and n % 2:
                self.gather(pe, n // 2 - 1)
        return side

    def scalar(self, act):
        act.wait_ge(*self.var.take())
        act.activation(self.rstd[:, :], self.rstd[:, :], ACT.Sqrt).then_inc(*self.root.post())

    def vector(self, dve, gain, layer, hn):
        dve.wait_ge(*self.summed.take(DT))
        dve.tensor_scalar(self.rstd[:, :], self.K.bank[6][:, 0:T2], 1.0 / D, 1e-6, ALU.mult, ALU.add).then_inc(*self.var.post())
        dve.wait_ge(*self.root.take())
        dve.reciprocal(self.rstd[:, :], self.rstd[:, :]).then_inc(*self.inverse.post())
        dve.wait_ge(*self.inverse.posted())
        for j in range(DT):
            dve.scalar_tensor_tensor(out=hn[:, j, :], in0=self.K.x[:, j, :], scalar=self.K.col(gain, layer * DT + j), in1=self.rstd[:, :],
                                     op0=ALU.mult, op1=ALU.mult).then_inc(*self.hn_ready.post())


def swiglu(K, gain, layer, last=False):
    nc, block, bank = K.nc, K.block, K.bank
    T = T2
    name = f"{gain[:4]}_{layer}"
    with ExitStack() as st:
        def sb(n, shape):
            return st.enter_context(nc.sbuf_tensor(name + n, shape, F32))

        hn, h = sb("_hn", [P, DT, T]), sb("_h", [P, FFT, T])
        s = sb("_silu", [P, 2, T])
        rms = K.rms
        gu_ready, s_ready, h_free, h_ready, y_ready, y_free = \
            (new_signal(K, name + n) for n in ("_gu_ready", "_silu_ready", "_gu_free", "_h_ready", "_y_ready", "_y_free"))
        s_used, x_new = h_free.reader(), y_free.reader()

        @block.tensor
        def _(pe):
            for j in range(FFT):
                if j >= 2:
                    pe.wait_ge(*h_free.take())
                for half in range(2):
                    for k in range(DT):
                        if j == 0 and half == 0:
                            pe.wait_ge(*rms.hn_ready.take())
                        matmul(K, bank[2 * (j % 2) + half][:, 0:T], K.weights.take(pe), hn[:, k, :], k == 0, k == DT - 1,
                               gu_ready if half and k == DT - 1 else None)
            pe.wait_ge(*h_free.take(2))
            stream_linear(K, pe, DT, lambda k: h[:, k, :], FFT, T, y_ready, y_free,
                          side=None if last else rms.beside(pe))
            if not last:
                rms.gather(pe, DT - 1)

        @block.scalar
        def _(act):
            rms.scalar(act)
            for j in range(FFT):
                act.wait_ge(*gu_ready.take())
                if j >= 2:
                    act.wait_ge(*s_used.take())
                act.activation(s[:, j % 2, :], bank[2 * (j % 2)][:, 0:T], ACT.Silu).then_inc(*s_ready.post())
            for j in range(0 if last else DT):
                act.wait_ge(*x_new.take())
                rms.square(act, j)

        @block.vector
        def _(dve):
            rms.vector(dve, gain, layer, hn)
            for j in range(FFT):
                dve.wait_ge(*s_ready.take())
                dve.tensor_tensor(out=h[:, j, :], in0=s[:, j % 2, :], in1=bank[2 * (j % 2) + 1][:, 0:T], op=ALU.mult).then_inc(*h_free.post())
            for j in range(DT):
                dve.wait_ge(*y_ready.take())
                dve.scalar_tensor_tensor(out=K.x[:, j, :], in0=bank[j % 4][:, 0:T], scalar=0.5, in1=K.x[:, j, :], op0=ALU.mult, op1=ALU.add)\
                    .then_inc(*y_free.post())
    end_stage(K)


class Attention:

    def __init__(self, K, st, name, q, k, v, mask, out, sink=None):
        self.K, self.q, self.k, self.v, self.mask, self.out, self.sink = K, q, k, v, mask, out, sink
        sb = lambda n, s: st.enter_context(K.nc.sbuf_tensor(name + n, s, F32))
        self.s, self.p = sb("_scores", [P, 2, T2]), sb("_probs", [P, 2, T2])
        self.mx, self.total, self.extra = sb("_neg_max", [P, 2]), sb("_total", [P, 2]), sb("_sink", [P, 2])
        self.pt = sb("_probs_t", [P, 2, 3, P])
        self.s_ready, self.max_ready, self.e_ready, self.p_ready, self.t_ready, self.pt_ready, self.o_ready, self.o_free, self.chain, self.ac = \
            (new_signal(K, name + n) for n in ("_scores_ready", "_max", "_exps", "_probs_ready", "_turned", "_turned_sb", "_out_ready",
                                          "_out_free", "_chain", "_act_chain"))

    def turns(self):
        return [(h, qt, q0, qn) for h in range(8) for qt, (q0, qn) in enumerate(Q3)]

    def tensor(self, pe):
        K, nc, bank = self.K, self.K.nc, self.K.bank
        all_turns = self.turns()

        def scores(n):
            h, _, q0, qn = all_turns[n]
            nc.tensor.matmul(bank[n % 2][0:qn, 0:T2], self.q(h)[:, q0:q0 + qn], self.k(h), start=True, stop=True).then_inc(*self.s_ready.post())

        def values(n):
            h, _, q0, qn = all_turns[n]
            pe.wait_ge(*self.pt_ready.take())
            if n >= 2:
                pe.wait_ge(*self.o_free.take())
            r = 64 * (h % 2)
            for kt, (k0, kn) in enumerate(Q3):
                ins = nc.tensor.matmul(bank[4 + n % 2][r:r + 64, 0:qn], self.v(h, kt)[0:kn, :], self.pt[0:kn, n % 2, kt, 0:qn],
                                       start=kt == 0, stop=kt == 2)
            ins.then_inc(*self.o_ready.post())

        scores(0)
        scores(1)
        for n, (h, qt, q0, qn) in enumerate(all_turns):
            pe.wait_ge(*self.p_ready.take())
            for kt, (k0, kn) in enumerate(Q3):
                ins = nc.tensor.transpose(bank[2 + n % 2][0:kn, kt * P:kt * P + qn], self.p[0:qn, n % 2, k0:k0 + kn], K.con["eye"][0:qn, 0:qn])
            ins.then_inc(*self.t_ready.post())
            if n + 2 < len(all_turns):
                scores(n + 2)
            if n >= 1:
                values(n - 1)
        values(len(all_turns) - 1)
        pe.wait_ge(*self.o_free.take(2))

    def scalar(self, act):
        K, bank = self.K, self.K.bank
        all_turns = self.turns()

        def turned(n):
            _, _, _, qn = all_turns[n]
            b = n % 2
            act.wait_ge(*self.t_ready.take())
            if qn == P:
                act.activation(self.pt[:, b, 0:2, :].rearrange("p a q -> p (a q)"), bank[2 + b][:, 0:2 * P], ACT.Copy)
            else:
                for kt in range(2):
                    act.activation(self.pt[:, b, kt, 0:qn], bank[2 + b][:, kt * P:kt * P + qn], ACT.Copy)
            act.activation(self.pt[0:T2 - 256, b, 2, 0:qn], bank[2 + b][0:T2 - 256, 2 * P:2 * P + qn], ACT.Copy).then_inc(*self.pt_ready.post())

        for n, (h, qt, q0, qn) in enumerate(all_turns):
            b = n % 2
            act.wait_ge(*self.max_ready.take())
            if self.sink is not None:
                act.activation(self.extra[0:qn, b:b + 1], self.sink[0:qn, h:h + 1], ACT.Exp, bias=self.mx[0:qn, b:b + 1])
            act.activation(self.p[0:qn, b, :], self.s[0:qn, b, :], ACT.Exp, bias=self.mx[0:qn, b:b + 1],
                           accum_out=self.total[0:qn, b:b + 1]).then_inc(*self.e_ready.post())
            if n >= 1:
                turned(n - 1)
        turned(len(all_turns) - 1)

    def vector(self, dve):
        K, bank = self.K, self.K.bank
        then = linker(dve, self.chain)
        all_turns = self.turns()

        def masked(n):
            h, qt, q0, qn = all_turns[n]
            b = n % 2
            mx = self.mx[0:qn, b:b + 1]
            dve.wait_ge(*self.s_ready.take())
            then(dve.scalar_tensor_tensor(out=self.s[0:qn, b, :], in0=bank[b][0:qn, 0:T2], scalar=0.125, in1=self.mask(qt)[0:qn, :],
                                          op0=ALU.mult, op1=ALU.add))
            then(dve.tensor_reduce(out=mx, in_=self.s[0:qn, b, :], axis=AX.X, op=ALU.max))
            if self.sink is not None:
                then(dve.tensor_tensor(out=mx, in0=mx, in1=self.sink[0:qn, h:h + 1], op=ALU.max))
            dve.tensor_scalar(mx, mx, -1.0, None, ALU.mult).then_inc(*self.max_ready.post())

        def read_out(n):
            h, _, q0, qn = all_turns[n]
            r = 64 * (h % 2)
            dve.wait_ge(*self.o_ready.take())
            dve.tensor_copy(self.out[r:r + 64, h // 2, q0:q0 + qn], bank[4 + n % 2][r:r + 64, 0:qn]).then_inc(*self.o_free.post())

        masked(0)
        for n, (h, qt, q0, qn) in enumerate(all_turns):
            b = n % 2
            if n + 1 < len(all_turns):
                masked(n + 1)
            dve.wait_ge(*self.e_ready.take())
            total = self.total[0:qn, b:b + 1]
            if self.sink is not None:
                then(dve.tensor_tensor(out=total, in0=total, in1=self.extra[0:qn, b:b + 1], op=ALU.add))
            then(dve.reciprocal(total, total))
            dve.tensor_scalar(self.p[0:qn, b, :], self.p[0:qn, b, :], total, None, ALU.mult).then_inc(*self.p_ready.post())
            if n >= 2:
                read_out(n - 2)
        read_out(len(all_turns) - 2)
        read_out(len(all_turns) - 1)


def even_mixer(K):
    nc, block, bank, col = K.nc, K.block, K.bank, K.col
    T = T2
    with ExitStack() as outer:
        def sb(st, name, shape):
            return st.enter_context(nc.sbuf_tensor("even_" + name, shape, F32))

        y = sb(outer, "y", [P, 12, T])
        bq = sb(outer, "bq_bk", [P, 8, T])
        bg = sb(outer, "bg", [P, 8, T])
        bv = sb(outer, "bv", [P, 3, D])
        ret_con = constant_buffers(K, outer, "ret")
        with ExitStack() as st:
            con = load_constants(K, st, "even")
            fill_constants(K, ret_con)
            early = ExitStack()
            score, gains = sb(st, "score", [P, 3, T]), sb(st, "gains", [P, 2])
            aqk, av = sb(st, "aq_ak", [P, 8, T]), sb(st, "av", [P, 3, W])
            heads = HeadNorm(K, st, "ev", 8, y[:, 4:12], con["pair_gather"], con["pair_spread"], 64, 6, (4, 5))
            wiw = sb(early, "w_iw", [P, DT, 8])
            load(K, [(wiw[:, :, :], K.dram["ev_w_iw"]), (gains[:, :], K.dram["ev_gains"])])
            loads = 16 * K.small_loads
            hn, iq = sb(early, "hn", [P, DT, T]), sb(early, "iq_ik", [P, 5, T])
            iw = sb(early, "iw", [P, 3, 8])
            work, r, top = sb(early, "work", [P, T]), sb(early, "relu", [P, 2, T]), sb(early, "top", [P, 8])
            early.close()
            z_ready, z_free, v_ready, v_free, iw_ready = (new_signal(K, "ev_" + n) for n in ("z_ready", "z_free", "v_ready", "v_free", "iw"))
            z_sb, v_sb = z_free.reader(), v_free.reader()
            ix_ready, ix_free, link, masks, qk_ready = (new_signal(K, "ev_" + n) for n in ("index_ready", "index_free", "dve_chain", "masks", "qk_ready"))
            attn = Attention(K, st, "dsa", lambda h: aqk[64 * (h % 2):64 * (h % 2) + 64, h // 2, :],
                             lambda h: aqk[64 * (h % 2):64 * (h % 2) + 64, 4 + h // 2, :],
                             lambda h, kt: av[:, kt, 64 * h:64 * h + 64], lambda qt: score[:, qt, :], y)

            @block.tensor
            def _(pe):
                def index_scores(n):
                    qt, h = divmod(n, 8)
                    if n >= 2:
                        pe.wait_ge(*ix_free.take())
                    rr = slice(64 * (h % 2), 64 * (h % 2) + 64)
                    q0, qn = Q3[qt]
                    nc.tensor.matmul(bank[4 + n % 2][0:qn, 0:T], iq[rr, h // 2, q0:q0 + qn], iq[rr, 4, :], start=True, stop=True)\
                      .then_inc(*ix_ready.post())

                def side(n):
                    if 2 <= n < 18 and n % 2:
                        heads.gather(pe, n // 2 - 1)
                    if 22 <= n < 30:
                        heads.spread(pe, n - 22)
                    if n == 31:
                        pe.wait_ge(K.small_loaded, loads)
                        for qt, (q0, qn) in enumerate(Q3):
                            for k in range(DT):
                                ins = nc.tensor.matmul(bank[7][0:qn, 8 * qt:8 * qt + 8], hn[:, k, q0:q0 + qn], wiw[:, k, :],
                                                       start=k == 0, stop=k == DT - 1)
                        ins.then_inc(*iw_ready.post())
                    if 32 <= n < 56:
                        index_scores(n - 32)

                pe.wait_ge(K.small_loaded, loads)
                stream_linear(K, pe, 29, lambda k: hn[:, k, :], DT, T, z_ready, z_free, side=side, x_ready=K.rms.hn_ready)
                pe.wait_ge(*ix_free.take(2))
                for _ in range(3):
                    stream_tokens(K, pe, lambda k: hn[:, k, :], Q3, 4, v_ready, v_free, (4, 5, 6))
                pe.wait_ge(*qk_ready.take())
                attn.tensor(pe)

            @block.scalar
            def _(act):
                K.rms.scalar(act)
                for j in range(29):
                    dst = aqk[:, j, :] if j < 8 else iq[:, j - 8, :] if j < 13 else bq[:, j - 13, :] if j < 21 else bg[:, j - 21, :]
                    act.wait_ge(*z_ready.take())
                    if j < 8:
                        act.activation(y[:, 4 + j, :], bank[j % 4][:, 0:T], ACT.Square).then_inc(*heads.squared.post())
                    act.activation(dst, bank[j % 4][:, 0:T], ACT.Silu if j >= 21 else ACT.Copy).then_inc(*z_free.post())
                    if j == 9:
                        heads.scalar(act)
                for half in range(3):
                    for b, (t0, tn) in enumerate(Q3):
                        act.wait_ge(*v_ready.take())
                        dst = av[0:tn, b, :] if half == 0 else bv[0:tn, b, (half - 1) * 512:half * 512]
                        act.activation(dst, bank[4 + b][0:tn, :], ACT.Copy).then_inc(*v_free.post())
                attn.scalar(act)

            @block.vector
            def _(dve):
                then = linker(dve, link)
                K.rms.vector(dve, "mix_norm_2", 0, hn)
                dve.wait_ge(K.small_loaded, loads)
                heads.vector(dve)
                dve.wait_ge(*z_sb.take(8))
                for j in range(8):
                    dve.scalar_tensor_tensor(out=aqk[:, j, :], in0=aqk[:, j, :], scalar=gains[:, j // 4:j // 4 + 1], in1=heads.spread_to(dve, j),
                                             op0=ALU.mult, op1=ALU.mult).then_inc(*heads.free.post())
                dve.wait_ge(*iw_ready.take())
                for qt, (q0, qn) in enumerate(Q3):
                    then(dve.tensor_scalar(iw[0:qn, qt, :], bank[7][0:qn, 8 * qt:8 * qt + 8], 8 ** -0.5 * 64 ** -0.5, None, ALU.mult))
                n = 0
                for qt, (q0, qn) in enumerate(Q3):
                    s = score[0:qn, qt, :]
                    for h in range(8):
                        dve.wait_ge(*ix_ready.take())
                        dst = s if h == 0 else r[0:qn, h % 2, :]
                        dve.tensor_scalar(dst, bank[4 + n % 2][0:qn, 0:T], 0.0, iw[0:qn, qt, h:h + 1], ALU.max, ALU.mult).then_inc(*ix_free.post())
                        dve.wait_ge(*ix_free.posted())
                        if h:
                            then(dve.tensor_tensor(out=s, in0=s, in1=r[0:qn, h % 2, :], op=ALU.add))
                        n += 1
                for qt, (q0, qn) in enumerate(Q3):
                    s = score[0:qn, qt, :]
                    m = con["dsa_mask"][0:qn, qt * T:(qt + 1) * T]
                    then(dve.tensor_tensor(out=s, in0=s, in1=m, op=ALU.add))
                    src = s
                    for _ in range(TOPK2 // 8):
                        then(dve.max(top[0:qn, :], src))
                        then(dve.match_replace(work[0:qn, :], in_to_replace=top[0:qn, :], in_values=src, imm_value=-3e38))
                        src = work[0:qn, :]
                    then(dve.tensor_tensor(out=work[0:qn, :], in0=work[0:qn, :], in1=s, op=ALU.is_equal))
                    then(dve.scalar_tensor_tensor(out=s, in0=work[0:qn, :], scalar=NEG, in1=m, op0=ALU.mult, op1=ALU.add))
                dve.drain().then_inc(*qk_ready.post())
                attn.vector(dve)
        end_stage(K)
        retention(K, ret_con, bq, bg, bv, y)
        out_projection(K, "ev", y, 12)


def retention(K, con, bqk, bg, bv, y):
    nc, block, bank = K.nc, K.block, K.bank
    T = T2
    with ExitStack() as st:
        def sb(name, shape):
            return st.enter_context(nc.sbuf_tensor("ret_" + name, shape, F32))

        rotation_loads = 16 * K.small_loads
        con = dict(con, **load_constants(K, st, "ret_heads"))
        loads = 16 * K.small_loads
        t1, t2 = sb("cos_part", [P, 2, T]), sb("sin_part", [P, 2, T])
        s = sb("scores", [P, 2, 3, T])
        r_ready, r_free, rotated, s_ready, s_sb, o_ready, o_free, link, normed = \
            (new_signal(K, "re_" + n) for n in ("turned", "turned_read", "rotated", "scores_ready", "scores_sb", "out_ready", "out_free", "chain", "normed"))
        sq = sb("squares", [P, 8, T])
        heads = HeadNorm(K, st, "re", 8, sq, con["head_gather"], con["head_spread"], P, 0, (1, 2))
        o_done, o_sb = o_ready.reader(), o_free.reader()

        @block.tensor
        def _(pe):
            pe.wait_ge(K.small_loaded, rotation_loads)
            for j in range(8):
                if j >= 2:
                    pe.wait_ge(*r_free.take())
                nc.tensor.matmul(bank[j % 2][:, 0:T], con["rot"][:, :], bqk[:, j, :], start=True, stop=True).then_inc(*r_ready.post())
            pe.wait_ge(*r_free.take(2))
            pe.wait_ge(*rotated.take())
            pe.wait_ge(K.small_loaded, loads)

            def scores(h):
                rr = slice(64 * (h % 2), 64 * (h % 2) + 64)
                for jt, (j0, jn) in enumerate(Q3):
                    ins = nc.tensor.matmul(bank[jt + 3 * (h % 2)][0:jn, 0:T], bqk[rr, 4 + h // 2, j0:j0 + jn], bqk[rr, h // 2, :], start=True, stop=True)
                ins.then_inc(*s_ready.post())

            scores(0)
            for h in range(8):
                if h < 7:
                    scores(h + 1)
                pe.wait_ge(*s_sb.take())
                if h >= 2:
                    pe.wait_ge(*o_free.take())
                for jt, (j0, jn) in enumerate(Q3):
                    ins = nc.tensor.matmul(bank[6 + h % 2][:, 0:T], bv[0:jn, jt, h * P:(h + 1) * P], s[0:jn, h % 2, jt, :], start=jt == 0, stop=jt == 2)
                ins.then_inc(*o_ready.post())
            pe.wait_ge(*o_free.take(2))
            for j in range(8):
                heads.gather(pe, j)
            for j in range(8):
                heads.spread(pe, j)

        @block.scalar
        def _(act):
            for h in range(8):
                act.wait_ge(*o_done.take())
                act.activation(sq[:, h, :], bank[6 + h % 2][:, 0:T], ACT.Square).then_inc(*heads.squared.post())
                act.activation(y[:, 4 + h, :], bank[6 + h % 2][:, 0:T], ACT.Copy).then_inc(*o_free.post())
            heads.scalar(act)

        @block.vector
        def _(dve):
            then = linker(dve, link)
            dve.wait_ge(K.small_loaded, rotation_loads)
            for j in range(8):
                b = j % 2
                dve.wait_ge(*r_ready.take())
                dve.tensor_tensor(out=t2[:, b, :], in0=bank[b][:, 0:T], in1=con["sin"][:, :], op=ALU.mult).then_inc(*r_free.post())
                then(dve.tensor_tensor(out=t1[:, b, :], in0=bqk[:, j, :], in1=con["cos"][:, :], op=ALU.mult))
                then(dve.tensor_tensor(out=t1[:, b, :], in0=t1[:, b, :], in1=t2[:, b, :], op=ALU.add))
                scale = con["ret_q" if j < 4 else "ret_k"][:, (j % 4) * T:(j % 4 + 1) * T]
                then(dve.tensor_tensor(out=bqk[:, j, :], in0=t1[:, b, :], in1=scale, op=ALU.mult))
            dve.drain().then_inc(*rotated.post())
            dve.wait_ge(K.small_loaded, loads)
            s_used = o_ready.reader()
            for h in range(8):
                dve.wait_ge(*s_ready.take())
                if h >= 2:
                    dve.wait_ge(*s_used.take())
                for jt, (j0, jn) in enumerate(Q3):
                    ins = dve.tensor_tensor(out=s[0:jn, h % 2, jt, :], in0=bank[jt + 3 * (h % 2)][0:jn, 0:T],
                                            in1=con["ret_mask"][0:jn, jt * T:(jt + 1) * T], op=ALU.mult)
                ins.then_inc(*s_sb.post())
            dve.wait_ge(*o_sb.take(8))
            then(dve.tensor_tensor(out=y[:, 4:12, :], in0=y[:, 4:12, :], in1=bg[:, :, :], op=ALU.mult))
            heads.vector(dve)
            for j in range(8):
                o = y[:, 4 + j, :]
                dve.tensor_tensor(out=o, in0=o, in1=heads.spread_to(dve, j), op=ALU.mult).then_inc(*heads.free.post())
    end_stage(K)


def out_projection(K, name, y, n_in):
    block, bank = K.block, K.bank
    ready, free = new_signal(K, name + "_proj_ready"), new_signal(K, name + "_proj_free")
    x_new = free.reader()

    @block.tensor
    def _(pe):
        stream_linear(K, pe, DT, lambda k: y[:, k, :], n_in, T2, ready, free, side=K.rms.beside(pe))
        K.rms.gather(pe, DT - 1)

    @block.scalar
    def _(act):
        for j in range(DT):
            act.wait_ge(*x_new.take())
            K.rms.square(act, j)

    @block.vector
    def _(dve):
        for j in range(DT):
            dve.wait_ge(*ready.take())
            dve.tensor_tensor(out=K.x[:, j, :], in0=K.x[:, j, :], in1=bank[j % 4][:, 0:T2], op=ALU.add).then_inc(*free.post())
    end_stage(K)


def odd_mixer(K):
    nc, block, bank, col = K.nc, K.block, K.bank, K.col
    T = T2
    with ExitStack() as st:
        def sb(name, shape):
            return st.enter_context(nc.sbuf_tensor("odd_" + name, shape, F32))

        con = load_constants(K, st, "odd")
        gains, sinks, dmix = sb("gains", [P, 2]), sb("sinks", [P, 8]), sb("d_mix", [P, 4, P])
        load(K, [(gains[:, :], K.dram["od_gains"]), (sinks[:, :], K.dram["od_sinks"]), (dmix[:, :, :], K.dram["od_mix"])])
        loads = 16 * K.small_loads
        y, hn = sb("y", [P, 8, T]), sb("hn", [P, DT, T])
        cqk, cv = sb("cq_ck", [P, 6, T]), sb("cv", [P, 3, P])
        PAD = 16
        dx, s0, s1 = sb("dx", [P, 4, PAD + T]), sb("window_a", [P, PAD + T]), sb("window_b", [P, PAD + T])
        pooled = sb("pooled", [P, 4, T])
        sq = sb("qk_squares", [P, 6, T])
        heads = HeadNorm(K, st, "od", 6, sq, con["pair_gather"], con["pair_spread"], 64, 7, (0, 1))
        z_ready, z_free, v_ready, v_free, link = (new_signal(K, "od_" + n) for n in ("z_ready", "z_free", "v_ready", "v_free", "chain"))
        z_sb, v_sb = z_free.reader(), v_free.reader()
        qk_ready = new_signal(K, "od_qk_ready")
        pool_ready, mix_ready, mix_free = (new_signal(K, "od_" + n) for n in ("pooled", "mixed", "mixed_read"))
        attn = Attention(K, st, "swa", lambda h: cqk[64 * (h % 2):64 * (h % 2) + 64, h // 2, :],
                         lambda h: cqk[64 * (h % 2):64 * (h % 2) + 64, 4 + h // 4, :],
                         lambda h, kt: cv[:, kt, 64 * (h // 4):64 * (h // 4) + 64],
                         lambda qt: con["swa_mask"][:, qt * T:(qt + 1) * T], y, sink=sinks)

        @block.tensor
        def _(pe):
            def side(n):
                if n == 1:
                    pe.wait_ge(K.small_loaded, loads)
                if 2 <= n < 14 and n % 2:
                    heads.gather(pe, n // 2 - 1)

            stream_linear(K, pe, 10, lambda k: hn[:, k, :], DT, T, z_ready, z_free, side=side, x_ready=K.rms.hn_ready)
            stream_tokens(K, pe, lambda k: hn[:, k, :], Q3, 1, v_ready, v_free, (4, 5, 6))
            for j in range(6):
                heads.spread(pe, j)
            pe.wait_ge(*pool_ready.take())
            for j in range(4):
                nc.tensor.matmul(bank[2 + j][:, 0:T], dmix[:, j, :], pooled[:, j, :], start=True, stop=True).then_inc(*mix_ready.post())
            pe.wait_ge(*mix_free.take())
            pe.wait_ge(*qk_ready.take())
            attn.tensor(pe)

        @block.scalar
        def _(act):
            K.rms.scalar(act)
            for j in range(10):
                act.wait_ge(*z_ready.take())
                if j < 6:
                    act.activation(sq[:, j, :], bank[j % 4][:, 0:T], ACT.Square).then_inc(*heads.squared.post())
                act.activation(cqk[:, j, :] if j < 6 else dx[:, j - 6, PAD:PAD + T], bank[j % 4][:, 0:T], ACT.Copy).then_inc(*z_free.post())
                if j == 8:
                    heads.scalar(act)
            for b, (t0, tn) in enumerate(Q3):
                act.wait_ge(*v_ready.take())
                act.activation(cv[0:tn, b, :], bank[4 + b][0:tn, 0:P], ACT.Copy).then_inc(*v_free.post())
            attn.scalar(act)

        @block.vector
        def _(dve):
            then = linker(dve, link)
            K.rms.vector(dve, "mix_norm_2", 1, hn)
            for t in (s0, s1):
                then(dve.memset(t[:, 0:PAD], 0.0))
            then(dve.memset(dx[:, :, 0:PAD], 0.0))
            dve.wait_ge(K.small_loaded, loads)
            heads.vector(dve)
            dve.wait_ge(*z_sb.take(10))
            for j in range(4):
                src = dx[:, j, :]
                for step in range(j + 1):
                    dst = (s0, s1)[step % 2]
                    sh = 2 ** step
                    then(dve.tensor_tensor(out=dst[:, PAD:PAD + T], in0=src[:, PAD:PAD + T], in1=src[:, PAD - sh:PAD + T - sh], op=ALU.add))
                    src = dst[:, :]
                then(dve.tensor_tensor(out=pooled[:, j, :], in0=src[:, PAD:PAD + T], in1=con["pool_inv"][:, j * T:(j + 1) * T], op=ALU.mult))
                then(dve.tensor_tensor(out=pooled[:, j, :], in0=pooled[:, j, :], in1=dx[:, j, PAD:PAD + T], op=ALU.subtract))
            dve.drain().then_inc(*pool_ready.post())
            for j in range(6):
                dve.scalar_tensor_tensor(out=cqk[:, j, :], in0=cqk[:, j, :], scalar=gains[:, j // 4:j // 4 + 1], in1=heads.spread_to(dve, j),
                                         op0=ALU.mult, op1=ALU.mult).then_inc(*heads.free.post())
            for j in range(4):
                dve.wait_ge(*mix_ready.take())
                ins = dve.tensor_scalar(y[:, 4 + j, :], bank[2 + j][:, 0:T], col("od_d_scale_2", j), None, ALU.mult)
            ins.then_inc(*mix_free.post())
            dve.drain().then_inc(*qk_ready.post())
            attn.vector(dve)
        end_stage(K)
        out_projection(K, "od", y, 8)


STAGES = [rwkv_branch, hgrn_branch, mlstm_branch, lru_branch, merge, router_and_ple, experts, second_norm,
          lambda K: swiglu(K, "ffn1_norm_2", 0), even_mixer, lambda K: swiglu(K, "ffn2_norm_2", 0),
          lambda K: swiglu(K, "ffn1_norm_2", 1), odd_mixer, lambda K: swiglu(K, "ffn2_norm_2", 1, last=True)]

SMALL = {"rwkv_w2a2": (P, W), "rwkv_g2": (P, W), "mlstm_w_gates": (P, DT, 8), "mlstm_gate_bias": (4, 2), "lru_w": (P, 8, P),
         "router_w": (P, DT, NE), "router_b": (P, NE), "p": (P, 2, T1), "expert_b_down": (NE, D), "expert_b_gu": (NE, 2 * D), "meta": (P, DT, META),
         "ev_w_iw": (P, DT, 8), "ev_gains": (P, 2), "od_gains": (P, 2), "od_sinks": (P, 8), "od_mix": (P, 4, P)}


def build(nc, upto=len(STAGES)):
    K = Kernel()
    K.nc = nc

    def dram(name, shape, kind="ExternalInput"):
        return nc.dram_tensor(name, list(shape), F32, kind=kind).ap()

    stream = dram("weight_stream", (N_CHUNKS, P, CHUNK_TILES * P))
    x_in = dram("x_t", (P, DT, T1))
    cols_in = dram("columns", (P, N_COLS))
    K.dram = {n: dram("in_" + n, s) for n, s in SMALL.items()}
    K.const_dram = {n: dram("const_" + n, v.shape) for n, v in constants().items()}
    out = dram("out_t", (P, DT, T1), "ExternalOutput")
    with ExitStack() as ctx:
        def sb(name, shape):
            return ctx.enter_context(nc.sbuf_tensor(name, shape, F32))

        sem = lambda name: ctx.enter_context(nc.semaphore(name))
        K.new_semaphore, K.spare, K.counts = sem, [], []
        K.bank = [ctx.enter_context(nc.psum_tensor(f"bank{i}", [P, 512], F32)) for i in range(8)]
        ring = sb("weight_ring", [P, SLOTS, CHUNK_TILES * P])
        K.x = sb("x", [P, DT, T2])
        K.cols = sb("columns_sb", [P, N_COLS])
        K.col = lambda name, j: K.cols[:, COL_AT[name] + j:COL_AT[name] + j + 1]
        loaded = [sem(f"weights_loaded{i}") for i in range(SLOTS)]
        used = [sem(f"weights_used{i}") for i in range(SLOTS)]
        K.weights = Weights(ring, loaded, used)
        K.small_loaded, K.small_loads = sem("small_loaded"), 0
        K.x_loaded, K.cols_loaded, K.stage_done, stored = sem("x_loaded"), sem("cols_loaded"), sem("stage_done"), sem("stored")
        K.stages = 0
        K.rms = RmsOfX(K, ctx)
        K.block = ctx.enter_context(nc.Block())

        @K.block.sync
        def _(sp):
            sp.dma_start(K.x[:, :, 0:T1], x_in).then_inc(K.x_loaded, 16)
            sp.dma_start(K.cols[:, :], cols_in).then_inc(K.cols_loaded, 16)
            for slot in range(SLOTS):
                sp.dma_start(ring[:, slot, :], stream[slot, :, :]).then_inc(loaded[slot], 16)
            with sp.Fori(1, K_ROUNDS[0]) as i:
                for slot in range(SLOTS):
                    sp.wait_ge(used[slot], i)
                    sp.dma_start(ring[:, slot, :], stream[bass.ds(i * SLOTS + slot, 1), :, :].rearrange("a p n -> (a p) n"))\
                        .then_inc(loaded[slot], 16)

        K.con = {c: sb("c_" + c, [P, K.const_dram[c].shape[1]]) for c in CONST_SETS["all"]}
        load(K, [(K.con[c][:, :], K.const_dram[c]) for c in CONST_SETS["all"]])
        with ExitStack() as first:
            K.y_branch = first.enter_context(nc.sbuf_tensor("y_branches", [P, 4, WT, T1], F32))
            for s in STAGES[:min(upto, 5)]:
                s(K)
        with ExitStack() as moe:
            K.gates = moe.enter_context(nc.sbuf_tensor("gates", [NE, T1], F32))
            K.chosen, K.gates_rows, K.place = (moe.enter_context(nc.sbuf_tensor(n, [P, 2, NE + 1], F32)) for n in ("chosen", "gate_rows", "place"))
            K.x_rows = moe.enter_context(nc.sbuf_tensor("x_rows", [P, 2, D], F32))
            K.moe = moe.enter_context(nc.sbuf_tensor("moe_rows", [P, 2, D], F32))
            K.load_of = moe.enter_context(nc.sbuf_tensor("tokens_of_expert", [P, NE], mybir.dt.int32))
            K.acc = moe.enter_context(nc.sbuf_tensor("moe_sum", [P, DT, T1], F32))
            for s in STAGES[5:min(upto, 8)]:
                s(K)
        for s in STAGES[8:upto]:
            s(K)
        n = K.stages

        @K.block.scalar
        def _(act):
            act.dma_start(out, K.x[:, :, META:T2]).then_inc(stored, 16)
            act.wait_ge(stored, 16)
    return K


K_ROUNDS = [N_CHUNKS // SLOTS]


def layout(inputs):
    a = {k: np.asarray(v) for k, v in inputs.items()}
    kt = lambda w: w.reshape(-1, P, w.shape[-1]).transpose(1, 0, 2)
    ev = a["ev_w_in_2"][0]
    od = a["od_w_in_2"][0]
    src = {"ev_ik": np.concatenate([ev[:, 2048:2112]] * 2, 1),
           "od_ck": np.concatenate([od[:, 512:576]] * 2 + [od[:, 576:640]] * 2, 1)}
    stream = np.empty((N_CHUNKS, P, CHUNK_TILES, P), np.float32)
    at = 0
    for name, idx, ks, cols, order in tile_groups():
        w = src[name] if name in src else a[name] if idx is None else a[name][idx]
        seq = [(k, c) for c in cols for k in ks] if order == "nk" else [(k, c) for k in ks for c in cols]
        for t, (k, c) in enumerate(seq, at):
            stream[t // CHUNK_TILES, :, t % CHUNK_TILES, :] = w[k * P:(k + 1) * P, c:c + P]
        at += len(seq)
    arrays = {"weight_stream": stream.reshape(N_CHUNKS, P, CHUNK_TILES * P)}
    arrays["x_t"] = a["x"][0].T.reshape(DT, P, T1).transpose(1, 0, 2)
    arrays["columns"] = np.concatenate([a[n].reshape(-1, P).T for n, _ in COLUMNS], 1)
    small = {
        "rwkv_w2a2": np.concatenate([a["rwkv_w2"][0], a["rwkv_a2"][0]], 0), "rwkv_g2": a["rwkv_g2"][0],
        "mlstm_w_gates": kt(a["w_in_first"][:, 1792 + 2048 + 2048:1792 + 2048 + 2056]),
        "mlstm_gate_bias": np.stack([a["mlstm_i_bias"][0], a["mlstm_f_bias"][0]], 1),
        "router_w": kt(a["router_w"][0]), "router_b": np.broadcast_to(a["router_b"][0], (P, NE)),
        "p": a["p"][0, 0].T.reshape(2, P, T1).transpose(1, 0, 2), "expert_b_down": a["expert_b_down"][0],
        "expert_b_gu": a["expert_b_gu"][0],
        "meta": a["meta_tokens_2"].T.reshape(DT, P, META).transpose(1, 0, 2),
        "ev_w_iw": kt(ev[:, 2112:2120]),
        "ev_gains": np.stack([np.concatenate([a[n][0]] * 2) for n in ("ev_a_q_norm_2", "ev_a_k_norm_2")], 1),
        "od_gains": np.stack([np.concatenate([a[n][0]] * 2) for n in ("od_c_q_norm_2", "od_c_k_norm_2")], 1),
        "od_sinks": np.broadcast_to(a["od_c_sinks_2"][0], (P, 8)), "od_mix": a["od_d_mix_2"][0].transpose(1, 0, 2),
    }
    lru = np.zeros((P, 8, P), np.float32)
    for f, name in enumerate(("lru_wx", "lru_wa")):
        for b in range(8):
            r = 64 * (b % 2)
            lru[r:r + 64, 4 * f + b // 2, r:r + 64] = a[name][0, b]
    small["lru_w"] = lru
    arrays.update({"in_" + n: v for n, v in small.items()})
    arrays.update({"const_" + n: v for n, v in constants().items()})
    return {k: np.ascontiguousarray(v) for k, v in arrays.items()}


def kernel(**inputs):
    import concourse.bacc as bacc
    from concourse.bass_utils import run_bass_kernel_spmd

    nc = bacc.Bacc("TRN2", target_bir_lowering=False, num_devices=1)
    arrays = layout(inputs)
    build(nc)
    r = run_bass_kernel_spmd(nc, [arrays], core_ids=[0])
    y = r.results[0]["out_t"]
    return np.ascontiguousarray(y.transpose(1, 0, 2).reshape(D, T1).T.reshape(1, T1, D))
```
